# Optimizing a Trainium2 kernel written in Bass

```python
import math
import jax, jax.numpy as jnp
from jax import lax
import numpy as np
import jax
import jax.numpy as jnp

D_MODEL = 1024
BATCH = 1
SEQ = 256
DEPTH = 2

HEAD_DIM = 64
N_MOBA_HEADS = D_MODEL // (2 * HEAD_DIM)
N_DSA_HEADS = D_MODEL // (2 * HEAD_DIM)
MOBA_WIDTH = N_MOBA_HEADS * HEAD_DIM
DSA_WIDTH = N_DSA_HEADS * HEAD_DIM
MIX_WIDTH = MOBA_WIDTH + DSA_WIDTH
ROPE_THETA = 500000.0
ROPE_DIM = HEAD_DIM // 4
MOBA_BLOCK = 256
MOBA_TOPK = 3
MOBA_Q_CHUNK = 32
N_IDX_HEADS = 8
IDX_DIM = 64
DSA_TOPK = 256
DSA_Q_CHUNK = 64
D_FF = 2816
CONV_WIDTH = 3
NORM_EPS = 1e-6
N_MOD = 6
PROJ_WIDTH = 3 * MOBA_WIDTH + 3 * DSA_WIDTH + N_IDX_HEADS * IDX_DIM + IDX_DIM + N_IDX_HEADS


def rms_norm(x, g):
    xf = x.astype(jnp.float32)
    y = xf * lax.rsqrt(jnp.mean(xf * xf, axis=-1, keepdims=True) + NORM_EPS)
    return (y * g.astype(jnp.float32)).astype(x.dtype)

def rope_tables(seq):
    pos = jnp.arange(seq, dtype=jnp.float32)
    inv_freq = ROPE_THETA ** (-jnp.arange(0, ROPE_DIM, 2, dtype=jnp.float32) / ROPE_DIM)
    ang = pos[:, None] * inv_freq[None, :]
    return jnp.cos(ang), jnp.sin(ang)

def partial_rope(x, cos, sin):
    xf = x.astype(jnp.float32)
    half = ROPE_DIM // 2
    x1, x2, xp = xf[..., :half], xf[..., half:ROPE_DIM], xf[..., ROPE_DIM:]
    c = cos[None, :, None, :]
    s = sin[None, :, None, :]
    out = jnp.concatenate([x1 * c - x2 * s, x2 * c + x1 * s, xp], axis=-1)
    return out.astype(x.dtype)

def moba_attention(q, k, v):
    B, S, H, Dh = q.shape
    nb = -(-S // MOBA_BLOCK)
    pad = nb * MOBA_BLOCK - S
    kp = jnp.pad(k, ((0, 0), (0, pad), (0, 0), (0, 0)))
    vp = jnp.pad(v, ((0, 0), (0, pad), (0, 0), (0, 0)))
    kb = kp.reshape(B, nb, MOBA_BLOCK, H, Dh)
    vb = vp.reshape(B, nb, MOBA_BLOCK, H, Dh)
    k_mean = jnp.mean(kb.astype(jnp.float32), axis=2)
    kb_g = kb.transpose(0, 3, 1, 2, 4).reshape(B, H, nb, MOBA_BLOCK * Dh)
    vb_g = vb.transpose(0, 3, 1, 2, 4).reshape(B, H, nb, MOBA_BLOCK * Dh)
    n_sel = min(MOBA_TOPK, nb)
    C = MOBA_Q_CHUNK
    n_chunks = S // C
    scale = HEAD_DIM ** -0.5
    qc = q.reshape(B, n_chunks, C, H, Dh).swapaxes(0, 1)
    blk_ids = jnp.arange(nb)

    def chunk(args):
        ci, qb = args
        t0 = ci * C
        cur = t0 // MOBA_BLOCK
        tq = t0 + jnp.arange(C)
        qf = qb.astype(jnp.float32)
        gate = jnp.einsum('bchd,bnhd->bhcn', qf, k_mean)
        gate = jnp.where(blk_ids < cur, gate, -jnp.inf)
        _, sel = lax.top_k(gate, n_sel)
        sel_ok = jnp.repeat(sel < cur, MOBA_BLOCK, axis=-1)
        gidx = sel.reshape(B, H, C * n_sel)[..., None]
        kg = jnp.take_along_axis(kb_g, gidx, axis=2).reshape(B, H, C, n_sel * MOBA_BLOCK, Dh)
        vg = jnp.take_along_axis(vb_g, gidx, axis=2).reshape(B, H, C, n_sel * MOBA_BLOCK, Dh)
        k_own = lax.dynamic_slice_in_dim(kp, cur * MOBA_BLOCK, MOBA_BLOCK, axis=1)
        v_own = lax.dynamic_slice_in_dim(vp, cur * MOBA_BLOCK, MOBA_BLOCK, axis=1)
        own_pos = cur * MOBA_BLOCK + jnp.arange(MOBA_BLOCK)
        causal = own_pos[None, :] <= tq[:, None]
        s_sel = jnp.einsum('bchd,bhckd->bhck', qb, kg).astype(jnp.float32) * scale
        s_own = jnp.einsum('bchd,bkhd->bhck', qb, k_own).astype(jnp.float32) * scale
        s_sel = jnp.where(sel_ok, s_sel, -jnp.inf)
        s_own = jnp.where(causal[None, None], s_own, -jnp.inf)
        p = jax.nn.softmax(jnp.concatenate([s_sel, s_own], axis=-1), axis=-1).astype(v.dtype)
        p_sel, p_own = p[..., : n_sel * MOBA_BLOCK], p[..., n_sel * MOBA_BLOCK:]
        return (jnp.einsum('bhck,bhckd->bchd', p_sel, vg)
                + jnp.einsum('bhck,bkhd->bchd', p_own, v_own))

    out = lax.map(chunk, (jnp.arange(n_chunks), qc))
    return out.swapaxes(0, 1).reshape(B, S, H * Dh)

def dsa_attention(q, k, v, q_idx, k_idx, w_idx):
    B, S, H, Dh = q.shape
    n_keep = min(DSA_TOPK, S // 4)
    C = DSA_Q_CHUNK
    n_chunks = S // C
    scale = HEAD_DIM ** -0.5
    idx_scale = IDX_DIM ** -0.5
    w_scale = N_IDX_HEADS ** -0.5
    kf = k.reshape(B, S, H * Dh)
    vf = v.reshape(B, S, H * Dh)
    kif = k_idx.astype(jnp.float32)
    key_pos = jnp.arange(S)
    qc = q.reshape(B, n_chunks, C, H, Dh).swapaxes(0, 1)
    qic = q_idx.reshape(B, n_chunks, C, N_IDX_HEADS, IDX_DIM).swapaxes(0, 1)
    wc = w_idx.reshape(B, n_chunks, C, N_IDX_HEADS).swapaxes(0, 1)

    def chunk(args):
        ci, qb, qib, wb = args
        tq = ci * C + jnp.arange(C)
        logits = jnp.einsum('bchd,bsd->bchs', qib.astype(jnp.float32), kif) * idx_scale
        score = jnp.einsum('bch,bchs->bcs', wb.astype(jnp.float32) * w_scale, jax.nn.relu(logits))
        admissible = key_pos[None, :] <= tq[:, None]
        score = jnp.where(admissible[None], score, -jnp.inf)
        _, sel = lax.top_k(score, n_keep)
        sel_ok = sel <= tq[None, :, None]
        gidx = sel.reshape(B, C * n_keep)[..., None]
        kg = jnp.take_along_axis(kf, gidx, axis=1).reshape(B, C, n_keep, H, Dh)
        vg = jnp.take_along_axis(vf, gidx, axis=1).reshape(B, C, n_keep, H, Dh)
        s = jnp.einsum('bchd,bckhd->bhck', qb, kg).astype(jnp.float32) * scale
        s = jnp.where(sel_ok[:, None], s, -jnp.inf)
        p = jax.nn.softmax(s, axis=-1).astype(v.dtype)
        return jnp.einsum('bhck,bckhd->bchd', p, vg)

    out = lax.map(chunk, (jnp.arange(n_chunks), qc, qic, wc))
    return out.swapaxes(0, 1).reshape(B, S, H * Dh)

def token_mixer(h, w_in, g_moba_out, g_dsa_out, w_out, cos, sin):
    B, S, _ = h.shape
    proj = h @ w_in
    sizes = [MOBA_WIDTH] * 3 + [DSA_WIDTH] * 3 + [N_IDX_HEADS * IDX_DIM, IDX_DIM, N_IDX_HEADS]
    offs = []
    acc = 0
    for sz in sizes[:-1]:
        acc += sz
        offs.append(acc)
    mq, mk, mv, dq, dk, dv, qi, ki, wi = jnp.split(proj, offs, axis=-1)
    mq = partial_rope(mq.reshape(B, S, N_MOBA_HEADS, HEAD_DIM), cos, sin)
    mk = partial_rope(mk.reshape(B, S, N_MOBA_HEADS, HEAD_DIM), cos, sin)
    mv = mv.reshape(B, S, N_MOBA_HEADS, HEAD_DIM)
    dq = partial_rope(dq.reshape(B, S, N_DSA_HEADS, HEAD_DIM), cos, sin)
    dk = partial_rope(dk.reshape(B, S, N_DSA_HEADS, HEAD_DIM), cos, sin)
    dv = dv.reshape(B, S, N_DSA_HEADS, HEAD_DIM)
    qi = partial_rope(qi.reshape(B, S, N_IDX_HEADS, IDX_DIM), cos, sin)
    ki = partial_rope(ki[:, :, None, :], cos, sin)[:, :, 0, :]
    o_moba = moba_attention(mq, mk, mv)
    o_dsa = dsa_attention(dq, dk, dv, qi, ki, wi)
    o = jnp.concatenate([rms_norm(o_moba, g_moba_out), rms_norm(o_dsa, g_dsa_out)], axis=-1)
    return o @ w_out

def causal_depthwise_conv(u, w, b):
    out = lax.conv_general_dilated(
        u, w[:, None, :].astype(u.dtype), window_strides=(1,),
        padding=[(CONV_WIDTH - 1, 0)], dimension_numbers=('NWC', 'WIO', 'NWC'),
        feature_group_count=u.shape[-1])
    return out + b.astype(u.dtype)

def conv_glu_ffn(h, w_up_act, w_up_lin, w_conv, b_conv, w_down):
    a = causal_depthwise_conv(h @ w_up_act, w_conv, b_conv)
    return (jax.nn.gelu(a) * (h @ w_up_lin)) @ w_down

def first_inputs(seed: int = 0) -> dict:
    key = jax.random.key(seed)
    ks = jax.random.split(key, 20)
    f32 = jnp.float32
    nrm = lambda k, shape, s: jax.random.normal(k, shape, f32) * s
    return {
        "x": nrm(ks[0], (BATCH, SEQ, D_MODEL), 1.0),
        "c": nrm(ks[1], (BATCH, D_MODEL), 1.0),
        "w_ada": nrm(ks[2], (DEPTH, D_MODEL, N_MOD * D_MODEL), 0.5 * D_MODEL ** -0.5),
        "b_ada": nrm(ks[3], (DEPTH, N_MOD * D_MODEL), 0.02),
        "g_pre_mix": 1.0 + nrm(ks[4], (DEPTH, D_MODEL), 0.02),
        "w_in": nrm(ks[5], (DEPTH, D_MODEL, PROJ_WIDTH), D_MODEL ** -0.5),
        "g_moba_out": 1.0 + nrm(ks[6], (DEPTH, MOBA_WIDTH), 0.1),
        "g_dsa_out": 1.0 + nrm(ks[7], (DEPTH, DSA_WIDTH), 0.1),
        "w_out": nrm(ks[8], (DEPTH, MIX_WIDTH, D_MODEL), MIX_WIDTH ** -0.5),
        "g_post_mix": 1.0 + nrm(ks[9], (DEPTH, D_MODEL), 0.02),
        "g_pre_ffn": 1.0 + nrm(ks[10], (DEPTH, D_MODEL), 0.02),
        "w_up_act": nrm(ks[11], (DEPTH, D_MODEL, D_FF), D_MODEL ** -0.5),
        "w_up_lin": nrm(ks[12], (DEPTH, D_MODEL, D_FF), D_MODEL ** -0.5),
        "w_conv": nrm(ks[13], (DEPTH, CONV_WIDTH, D_FF), CONV_WIDTH ** -0.5),
        "b_conv": nrm(ks[14], (DEPTH, D_FF), 0.02),
        "w_down": nrm(ks[15], (DEPTH, D_FF, D_MODEL), D_FF ** -0.5),
        "g_post_ffn": 1.0 + nrm(ks[16], (DEPTH, D_MODEL), 0.02),
    }

def first_block(x, c, w_ada, b_ada, g_pre_mix, w_in, g_moba_out, g_dsa_out, w_out, g_post_mix,
              g_pre_ffn, w_up_act, w_up_lin, w_conv, b_conv, w_down, g_post_ffn):
    cos, sin = rope_tables(x.shape[1])
    c_act = jax.nn.silu(c)
    for l in range(DEPTH):
        mod = c_act @ w_ada[l] + b_ada[l]
        sh_m, sc_m, gt_m, sh_f, sc_f, gt_f = jnp.split(mod[:, None, :], N_MOD, axis=-1)
        h = rms_norm(x, g_pre_mix[l]) * (1.0 + sc_m) + sh_m
        y = token_mixer(h, w_in[l], g_moba_out[l], g_dsa_out[l], w_out[l], cos, sin)
        x = x + gt_m * rms_norm(y, g_post_mix[l])
        h = rms_norm(x, g_pre_ffn[l]) * (1.0 + sc_f) + sh_f
        y = conv_glu_ffn(h, w_up_act[l], w_up_lin[l], w_conv[l], b_conv[l], w_down[l])
        x = x + gt_f * rms_norm(y, g_post_ffn[l])
    return x


D_MIX = D_MODEL
S5_WIDTH = D_MIX // 2
S5_GROUP_CH = 16
S5_GROUPS = S5_WIDTH // S5_GROUP_CH
S5_STATE = 64
S5_CHUNK = 128
GLA_WIDTH = D_MIX - S5_WIDTH
GLA_HEADS = 4
GLA_DK = GLA_WIDTH // 2
GLA_HEAD_K = GLA_DK // GLA_HEADS
GLA_HEAD_V = GLA_WIDTH // GLA_HEADS
GLA_GATE_RANK = 16
GLA_GATE_TAU = 16.0
GLA_CHUNK = 64
IN_SPLITS = (S5_WIDTH, S5_WIDTH + GLA_DK, S5_WIDTH + 2 * GLA_DK, S5_WIDTH + 2 * GLA_DK + GLA_WIDTH, S5_WIDTH + 2 * GLA_DK + 2 * GLA_WIDTH)
IN_COLS = S5_WIDTH + 2 * GLA_DK + 2 * GLA_WIDTH + GLA_GATE_RANK
D_FF_2 = 7 * D_MODEL // 2
N_EXPERTS = 8
TOP_K = 2
N_DENSE = (DEPTH + 1) // 2
N_MOE = DEPTH // 2
DN_ALPHA = (2.0 * DEPTH) ** 0.25
DN_BETA = (8.0 * DEPTH) ** -0.25
MOD_STD = 0.1
LN_EPS = 1e-5
RMS_EPS = 1e-6


def _layer_norm(x, gain, bias):
    xf = x.astype(jnp.float32)
    mu = jnp.mean(xf, axis=-1, keepdims=True)
    var = jnp.mean(jnp.square(xf - mu), axis=-1, keepdims=True)
    return ((xf - mu) * lax.rsqrt(var + LN_EPS)).astype(x.dtype) * gain + bias

def _rms_norm(x, gain):
    xf = x.astype(jnp.float32)
    return xf * lax.rsqrt(jnp.mean(xf * xf, axis=-1, keepdims=True) + RMS_EPS) * gain.astype(jnp.float32)

def _linear_recurrence_op(e1, e2):
    a1, b1 = e1
    a2, b2 = e2
    return a1 * a2, a2 * b1 + b2

def _s5_group(u, lam_re, lam_im, log_dt, b_re, b_im, c_re, c_im, d_skip, w_glu, b_glu):
    bsz, seq, _ = u.shape
    n_chunks = seq // S5_CHUNK
    f32 = jnp.float32
    uf = u.astype(f32)
    lam = lax.complex(lam_re.astype(f32), lam_im.astype(f32))
    dt = jnp.exp(log_dt.astype(f32))[:, None]
    lam_bar = jnp.exp(lam * dt)
    b_mat = lax.complex(b_re.astype(f32), b_im.astype(f32))
    b_bar = ((lam_bar - 1.0) / lam)[:, :, None] * b_mat
    c_mat = lax.complex(c_re.astype(f32), c_im.astype(f32))
    u_chunks = uf.reshape(bsz, n_chunks, S5_CHUNK, S5_GROUPS, S5_GROUP_CH).transpose(1, 0, 2, 3, 4)
    a_elems = jnp.broadcast_to(lam_bar, (bsz, S5_CHUNK, S5_GROUPS, S5_STATE))

    def chunk_step(h, u_c):
        bu = jnp.einsum('gph,blgh->blgp', b_bar, u_c.astype(jnp.complex64))
        a_cum, s = lax.associative_scan(_linear_recurrence_op, (a_elems, bu), axis=1)
        states = s + a_cum * h[:, None]
        y = jnp.einsum('ghp,blgp->blgh', c_mat, states).real
        return states[:, -1], y

    h0 = jnp.zeros((bsz, S5_GROUPS, S5_STATE), jnp.complex64)
    _, y = lax.scan(chunk_step, h0, u_chunks)
    y = y.transpose(1, 0, 2, 3, 4).reshape(bsz, seq, S5_WIDTH) + d_skip.astype(f32) * uf
    y = jax.nn.gelu(y).astype(u.dtype)
    return y * jax.nn.sigmoid(y @ w_glu + b_glu)

def _gla_group(q, k, v, g_out, a_low, w_alpha_up, b_alpha, head_gain):
    bsz, seq, _ = q.shape
    nc = seq // GLA_CHUNK
    f32 = jnp.float32

    def heads(t, dh):
        return t.astype(f32).reshape(bsz, nc, GLA_CHUNK, GLA_HEADS, dh).transpose(1, 0, 3, 2, 4)

    log_alpha = jax.nn.log_sigmoid((a_low @ w_alpha_up + b_alpha).astype(f32)) / GLA_GATE_TAU
    qc = heads(q, GLA_HEAD_K) * (GLA_HEAD_K ** -0.5)
    kc = heads(k, GLA_HEAD_K)
    vc = heads(v, GLA_HEAD_V)
    bc = jnp.cumsum(heads(log_alpha, GLA_HEAD_K), axis=3)
    causal = jnp.tril(jnp.ones((GLA_CHUNK, GLA_CHUNK), dtype=bool))

    def chunk_step(state, inp):
        q_c, k_c, v_c, b_c = inp
        o_inter = jnp.einsum('bhik,bhkv->bhiv', q_c * jnp.exp(b_c), state)
        diff = b_c[:, :, :, None, :] - b_c[:, :, None, :, :]
        decay = jnp.exp(jnp.where(causal[:, :, None], diff, -jnp.inf))
        scores = jnp.einsum('bhik,bhjk,bhijk->bhij', q_c, k_c, decay)
        o_intra = jnp.einsum('bhij,bhjv->bhiv', scores, v_c)
        b_last = b_c[:, :, -1:, :]
        k_dec = k_c * jnp.exp(b_last - b_c)
        new_state = jnp.exp(b_last[:, :, 0, :])[..., None] * state + jnp.einsum('bhjk,bhjv->bhkv', k_dec, v_c)
        return new_state, o_inter + o_intra

    s0 = jnp.zeros((bsz, GLA_HEADS, GLA_HEAD_K, GLA_HEAD_V), f32)
    _, o = lax.scan(chunk_step, s0, (qc, kc, vc, bc))
    o = o.transpose(1, 0, 3, 2, 4).reshape(bsz, seq, GLA_HEADS, GLA_HEAD_V)
    o = _rms_norm(o, head_gain.reshape(GLA_HEADS, GLA_HEAD_V)).reshape(bsz, seq, GLA_WIDTH)
    return (o * jax.nn.silu(g_out.astype(f32))).astype(q.dtype)

def _swiglu(x, w_gate, w_up, w_down):
    return (jax.nn.silu(x @ w_gate) * (x @ w_up)) @ w_down

def _moe_swiglu(x, w_router, b_router, w_gate, w_up, w_down):
    logits = (x @ w_router).astype(jnp.float32) + b_router.astype(jnp.float32)
    top_vals, top_idx = lax.top_k(logits, TOP_K)
    top_w = jax.nn.softmax(top_vals, axis=-1)
    combine = jnp.sum(jax.nn.one_hot(top_idx, N_EXPERTS, dtype=jnp.float32) * top_w[..., None], axis=-2)
    out = jnp.zeros_like(x)
    for e in range(N_EXPERTS):
        out = out + combine[..., e:e + 1].astype(x.dtype) * _swiglu(x, w_gate[e], w_up[e], w_down[e])
    return out

def second_inputs(seed: int = 0) -> dict:
    key = jax.random.key(seed)
    ks = jax.random.split(key, 32)
    f32 = jnp.float32

    def nrm(k, shape, std):
        return std * jax.random.normal(k, shape, f32)

    G, P, H = S5_GROUPS, S5_STATE, S5_GROUP_CH
    return {
        'x': jax.random.normal(ks[0], (BATCH, SEQ, D_MODEL), f32),
        'c': jax.random.normal(ks[1], (BATCH, D_MODEL), f32),
        'mod_w': nrm(ks[2], (DEPTH, D_MODEL, N_MOD * D_MODEL), MOD_STD * D_MODEL ** -0.5),
        'mod_b': nrm(ks[3], (DEPTH, N_MOD * D_MODEL), 0.01),
        'w_in': nrm(ks[4], (DEPTH, D_MODEL, IN_COLS), D_MODEL ** -0.5),
        'w_out': nrm(ks[5], (DEPTH, D_MIX, D_MODEL), DN_BETA * D_MIX ** -0.5),
        's5_lam_re': -0.5 * jnp.exp(nrm(ks[6], (DEPTH, G, P), 0.05)),
        's5_lam_im': math.pi * jnp.arange(P, dtype=f32)[None, None, :] + nrm(ks[7], (DEPTH, G, P), 0.01),
        's5_log_dt': jax.random.uniform(ks[8], (DEPTH, G), f32, math.log(1e-3), math.log(1e-1)),
        's5_b_re': nrm(ks[9], (DEPTH, G, P, H), (2.0 * H) ** -0.5),
        's5_b_im': nrm(ks[10], (DEPTH, G, P, H), (2.0 * H) ** -0.5),
        's5_c_re': nrm(ks[11], (DEPTH, G, H, P), (2.0 * P) ** -0.5),
        's5_c_im': nrm(ks[12], (DEPTH, G, H, P), (2.0 * P) ** -0.5),
        's5_d': nrm(ks[13], (DEPTH, S5_WIDTH), 1.0),
        's5_w_glu': nrm(ks[14], (DEPTH, S5_WIDTH, S5_WIDTH), S5_WIDTH ** -0.5),
        's5_b_glu': nrm(ks[15], (DEPTH, S5_WIDTH), 0.01),
        'gla_w_alpha_up': nrm(ks[16], (DEPTH, GLA_GATE_RANK, GLA_DK), GLA_GATE_RANK ** -0.5),
        'gla_b_alpha': nrm(ks[17], (DEPTH, GLA_DK), 0.01),
        'gla_head_gain': 1.0 + nrm(ks[18], (DEPTH, GLA_WIDTH), 0.02),
        'ln_mix_g': 1.0 + nrm(ks[19], (DEPTH, D_MODEL), 0.02),
        'ln_mix_b': nrm(ks[20], (DEPTH, D_MODEL), 0.01),
        'ffn_w_gate': nrm(ks[21], (N_DENSE, D_MODEL, D_FF_2), D_MODEL ** -0.5),
        'ffn_w_up': nrm(ks[22], (N_DENSE, D_MODEL, D_FF_2), D_MODEL ** -0.5),
        'ffn_w_down': nrm(ks[23], (N_DENSE, D_FF_2, D_MODEL), DN_BETA * D_FF_2 ** -0.5),
        'moe_w_router': nrm(ks[24], (N_MOE, D_MODEL, N_EXPERTS), D_MODEL ** -0.5),
        'moe_b_router': nrm(ks[25], (N_MOE, N_EXPERTS), 0.01),
        'moe_w_gate': nrm(ks[26], (N_MOE, N_EXPERTS, D_MODEL, D_FF_2), D_MODEL ** -0.5),
        'moe_w_up': nrm(ks[27], (N_MOE, N_EXPERTS, D_MODEL, D_FF_2), D_MODEL ** -0.5),
        'moe_w_down': nrm(ks[28], (N_MOE, N_EXPERTS, D_FF_2, D_MODEL), DN_BETA * D_FF_2 ** -0.5),
        'ln_ffn_g': 1.0 + nrm(ks[29], (DEPTH, D_MODEL), 0.02),
        'ln_ffn_b': nrm(ks[30], (DEPTH, D_MODEL), 0.01),
    }

def second_block(x, c, mod_w, mod_b, w_in, w_out, s5_lam_re, s5_lam_im, s5_log_dt, s5_b_re, s5_b_im, s5_c_re, s5_c_im, s5_d, s5_w_glu, s5_b_glu, gla_w_alpha_up, gla_b_alpha, gla_head_gain, ln_mix_g, ln_mix_b, ffn_w_gate, ffn_w_up, ffn_w_down, moe_w_router, moe_b_router, moe_w_gate, moe_w_up, moe_w_down, ln_ffn_g, ln_ffn_b):
    c_act = jax.nn.silu(c)
    for layer in range(DEPTH):
        mod = c_act @ mod_w[layer] + mod_b[layer]
        sh_m, sc_m, gt_m, sh_f, sc_f, gt_f = jnp.split(mod[:, None, :], N_MOD, axis=-1)
        h = x * (1 + sc_m) + sh_m
        u, q, k, v, g_out, a_low = jnp.split(h @ w_in[layer], IN_SPLITS, axis=-1)
        y_s5 = _s5_group(u, s5_lam_re[layer], s5_lam_im[layer], s5_log_dt[layer], s5_b_re[layer], s5_b_im[layer], s5_c_re[layer], s5_c_im[layer], s5_d[layer], s5_w_glu[layer], s5_b_glu[layer])
        y_gla = _gla_group(q, k, v, g_out, a_low, gla_w_alpha_up[layer], gla_b_alpha[layer], gla_head_gain[layer])
        y = jnp.concatenate([y_s5, y_gla], axis=-1) @ w_out[layer]
        x = _layer_norm(DN_ALPHA * x + (1 + gt_m) * y, ln_mix_g[layer], ln_mix_b[layer])
        h = x * (1 + sc_f) + sh_f
        i = layer // 2
        if layer % 2 == 0:
            f = _swiglu(h, ffn_w_gate[i], ffn_w_up[i], ffn_w_down[i])
        else:
            f = _moe_swiglu(h, moe_w_router[i], moe_b_router[i], moe_w_gate[i], moe_w_up[i], moe_w_down[i])
        x = _layer_norm(DN_ALPHA * x + (1 + gt_f) * f, ln_ffn_g[layer], ln_ffn_b[layer])
    return x


def setup_inputs(seed=0):
    out = dict(first_inputs(seed))
    for name, value in second_inputs(seed + 1).items():
        if name != "x":
            out[name + "_2"] = value
    return out


def reference(
    x, c, w_ada, b_ada, g_pre_mix, w_in, g_moba_out, g_dsa_out, w_out, g_post_mix, g_pre_ffn,
    w_up_act, w_up_lin, w_conv, b_conv, w_down, g_post_ffn, c_2, mod_w_2, mod_b_2, w_in_2,
    w_out_2, s5_lam_re_2, s5_lam_im_2, s5_log_dt_2, s5_b_re_2, s5_b_im_2, s5_c_re_2, s5_c_im_2,
    s5_d_2, s5_w_glu_2, s5_b_glu_2, gla_w_alpha_up_2, gla_b_alpha_2, gla_head_gain_2,
    ln_mix_g_2, ln_mix_b_2, ffn_w_gate_2, ffn_w_up_2, ffn_w_down_2, moe_w_router_2,
    moe_b_router_2, moe_w_gate_2, moe_w_up_2, moe_w_down_2, ln_ffn_g_2, ln_ffn_b_2,
):
    x = first_block(
        x, c, w_ada, b_ada, g_pre_mix, w_in, g_moba_out, g_dsa_out, w_out, g_post_mix,
        g_pre_ffn, w_up_act, w_up_lin, w_conv, b_conv, w_down, g_post_ffn,
    )
    return second_block(
        x, c_2, mod_w_2, mod_b_2, w_in_2, w_out_2, s5_lam_re_2, s5_lam_im_2, s5_log_dt_2,
        s5_b_re_2, s5_b_im_2, s5_c_re_2, s5_c_im_2, s5_d_2, s5_w_glu_2, s5_b_glu_2,
        gla_w_alpha_up_2, gla_b_alpha_2, gla_head_gain_2, ln_mix_g_2, ln_mix_b_2, ffn_w_gate_2,
        ffn_w_up_2, ffn_w_down_2, moe_w_router_2, moe_b_router_2, moe_w_gate_2, moe_w_up_2,
        moe_w_down_2, ln_ffn_g_2, ln_ffn_b_2,
    )


_drawn_inputs = setup_inputs


def setup_inputs(seed=0):
    import zlib

    import numpy as np

    out = dict(_drawn_inputs(seed))
    spreads = {}
    factors = {'g_post_mix': 3.225,
     'g_pre_ffn': 2.961,
     'b_conv': 3.409,
     'g_post_ffn': 4.053,
     'mod_b_2': 3.206,
     's5_lam_re_2': 64.0,
     's5_lam_im_2': 33.832,
     's5_log_dt_2': 35.912,
     's5_b_re_2': 35.408,
     's5_b_im_2': 54.616,
     's5_c_re_2': 43.696,
     's5_c_im_2': 38.544,
     's5_b_glu_2': 64.0,
     'gla_b_alpha_2': 8.0,
     'gla_head_gain_2': 5.808,
     'ln_mix_b_2': 2.721,
     'moe_b_router_2': 5.621,
     'ln_ffn_b_2': 2.839}
    for name, (base, spread) in spreads.items():
        noise = np.random.default_rng([zlib.crc32(name.encode()), seed]).standard_normal(out[name].shape)
        drawn = base * np.exp(spread * noise) if base else spread * noise
        out[name] = jnp.asarray(drawn.astype(out[name].dtype))
    for name, factor in factors.items():
        out[name] = (out[name] * factor).astype(out[name].dtype)
    return out
```

```python
import math

import numpy as np
import concourse.bass as bass
from concourse import mybir

F32 = mybir.dt.float32
U8 = mybir.dt.uint8
ALU = mybir.AluOpType
ACT = mybir.ActivationFunctionType
AX = mybir.AxisListType

P = 128
D = 1024
S = 256
NT = S // P
KD = D // P
LAYERS = 4
NMOD = 6
HD = 64
NH = 8
ROPE = HD // 4
TOPK = S // 4
PROJ1 = 3 * NH * HD * 2 + 8 * 64 + 64 + 8
PROJ2 = 512 + 256 * 2 + 512 * 2 + 16
FF = (2816, 2816, 3584, 3584)
NE = 8
CW = 256
SLOTS = 7
REGION = 20224
SLOT = KD * CW
NEG = -1e30
LOWEST = -3e38
QI, KI, WI = 3072, 3584, 3648
ALPHA = float(np.float32((2.0 * 2) ** 0.25))
PROJ_ORDER = [12, 13, 14, 0, 1, 2, 3, 6, 7, 8, 9, 4, 5, 10, 11]
LEVELS = [64, 32, 16, 8, 4, 2, 1, 0]
GROUPS = FF[3] // CW
CAP = P
EXTRA = 2 * S // (CAP + 1)
TURNS = NE + EXTRA
assert S <= 2 * CAP
assert 3 * GROUPS % SLOTS == 0
UNITS1 = [(g, t, n) for g in (0, 1) for t in (0, 1) for n in range(4 if t else 2)]
PROW = {"b_ada": 0, "g_pre_mix": 48, "g_moba_out": 56, "g_dsa_out": 60, "g_pre_ffn": 64,
        "w_conv": 128, "b_conv": 194}
PROW2 = {"mod_b_2": 0, "s5_lam_re_2": 48, "s5_lam_im_2": 64, "s5_d_2": 80, "s5_b_glu_2": 84,
         "gla_b_alpha_2": 88, "gla_head_gain_2": 90, "s5_log_dt_2": 96}


def unit_heads(t, n):
    return [4 * (n // 2) + n % 2, 4 * (n // 2) + n % 2 + 2] if t else [n, n + 2, n + 4, n + 6]


def constants():
    p = np.arange(P)
    pos = np.arange(S, dtype=np.float32)
    inv = np.float32(500000.0) ** (-np.arange(0, ROPE, 2, dtype=np.float32) / np.float32(ROPE))
    ang = (pos[:, None] * inv[None, :]).astype(np.float32)
    key = np.arange(S)
    query = p[:, None] + P * np.arange(NT)[None, :]
    causal = np.where(key[None, None, :] <= query[:, :, None], 0.0, NEG).astype(np.float32)
    levels = np.zeros((P, len(LEVELS), P), np.float32)
    for n, half in enumerate(LEVELS):
        j, i = p[:, None], p[None, :]
        if half:
            levels[:, n] = (j // (2 * half) == i // (2 * half)) & (j % (2 * half) < half) & (i % (2 * half) >= half)
        else:
            levels[:, n] = j == i
    fold = lambda a: np.ascontiguousarray(a.reshape(NT, P, -1).transpose(1, 0, 2)).reshape(P, -1)
    return {
        "ident": np.eye(P, dtype=np.float32),
        "causal": causal.reshape(P, NT * S),
        "rope_cos": fold(np.cos(ang).astype(np.float32)),
        "rope_sin": fold(np.sin(ang).astype(np.float32)),
        "levels": levels.reshape(P, -1),
        "parity": (p[:, None] // 64 == (p[None, :] // 16) % 2).astype(np.float32),
        "earlier": (p[:, None] < p[None, :]).astype(np.float32),
        "iota": np.broadcast_to(p[None, :].astype(np.float32), (P, CAP)).copy(),
        "before": np.broadcast_to((np.arange(NE)[None, :] < np.arange(NE)[:, None]).astype(np.float32).reshape(1, -1), (P, NE * NE)).copy(),
    }


class Signals:

    def __init__(self, sems, known):
        self.sems, self.known = sems, known
        self.count, self.at, self.owner = {}, {}, {}

    def of(self, engine):
        return Done(self, engine)

    def until(self, *event):
        return self.sems[event[0]], self.known[event]

    def within(self, r, back, *event):
        name = event[0]
        each = self.known["each", name]
        return self.sems[name], r * each + max(self.known[event] - back * each, 0)


class Done:

    def __init__(self, signals, engine):
        self.signals, self.engine, self.last = signals, engine, None

    def begin(self):
        self.before = dict(self.signals.count)

    def end(self, *names):
        for n in names:
            self.signals.at["each", n] = self.signals.count[n] - self.before.get(n, 0)

    def __call__(self, *event):
        s, name = self.signals, event[0]
        assert s.owner.setdefault(name, self.engine) == self.engine and event not in s.at, event
        s.count[name] = s.count.get(name, 0) + 1
        s.at[event] = s.count[name]
        self.last = (s.sems[name], s.count[name])
        return s.sems[name], 1

    def prev(self):
        return self.last

    def dma(self, *event):
        s, name = self.signals, event[0]
        assert event not in s.at, event
        s.count[name] = s.count.get(name, 0) + 16
        s.at[event] = s.count[name]
        return s.sems[name], 16


def ffn_groups(l):
    return FF[l] // CW


def ada_in_ffn(l, g):
    if l + 1 >= LAYERS:
        return []
    n, chunks = ffn_groups(l), NMOD * D // CW
    return list(range(chunks * g // n, chunks * (g + 1) // n))


def chunk_plan():
    plan = [(("ada", 0, q), ("mod_sum", 0, q)) for q in range(8)]
    for l in range(LAYERS):
        if l < 2:
            for i, n in enumerate(PROJ_ORDER):
                plan.append((("in", l, n), ("pe_tile", "in", l, n)))
                if l == 0:
                    for q in ([8 + i] if i < 14 else [22, 23]):
                        plan.append((("ada", 0, q), ("mod_sum", 0, q)))
        else:
            for n in (8, 0, 1, 2, 3, 4, 5, 6, 7):
                plan.append((("in", l, n), ("pe_tile", "in", l, n)))
            plan.append((("glu", l), ("pe_tile", "glu", l, 1)))
        for n in range(4):
            plan.append((("out", l, n), ("pe_used", "out", l, n)))
        for e in range(1):
            groups = ffn_groups(l)
            if l == 3:
                break
            for g in range(groups):
                for m in (0, 1):
                    plan.append((("up", l, e, g, m), ("pe_tile", "up", l, e, 2 * g + 1)))
                for q in ada_in_ffn(l, g):
                    plan.append((("ada", l + 1, q), ("mod_sum", l + 1, q)))
                if g:
                    plan.append((("down", l, e, g - 1), ("pe_used", "down", l, e, g - 1)))
            plan.append((("down", l, e, groups - 1), ("pe_used", "down", l, e, groups - 1)))
    for e in ("first", "loop"):
        for g in range(GROUPS):
            for m in (0, 1):
                plan.append((("up", 3, e, g, m), ("moe_tile", "up", g, e)))
            if g:
                plan.append((("down", 3, e, g - 1), ("moe_used", "down", g - 1, e)))
        plan.append((("down", 3, e, GROUPS - 1), ("moe_used", "down", GROUPS - 1, e)))
    return plan


def program(nc, A, out, sems, known):
    sig = Signals(sems, known)
    until, within = sig.until, sig.within
    sb = lambda name, cols, dt=F32: nc.alloc_sbuf_tensor(name, [P, cols], dt)[:, :]

    plan = chunk_plan()
    where = {key: i for i, (key, _) in enumerate(plan)}

    x = sb("x", NT * D).rearrange("p (t d) -> p t d", t=NT)
    xn = sb("xn", NT * D).rearrange("p (t d) -> p t d", t=NT)
    hT = sb("hT", KD * S).rearrange("p (k s) -> p k s", k=KD)
    ring = sb("ring", SLOTS * SLOT)
    mod_gate = sb("mod_gate", 3 * D).rearrange("p (m d) -> p m d", m=3)
    mod_col = sb("mod_col", 2 * 48).rearrange("p (b c) -> p b c", b=2)
    scale_col = sb("scale_col", 2 * KD).rearrange("p (b c) -> p b c", b=2)
    mod_acc = sb("mod_acc", 4 * CW).rearrange("p (b c) -> p b c", b=4)
    rows = sb("rows", 2 * D).rearrange("p (m d) -> p m d", m=2)
    hf = sb("hf", 4 * S).rearrange("p (b s) -> p b s", b=4)
    ffn_tmp = sb("ffn_tmp", 4 * S).rearrange("p (b s) -> p b s", b=4)
    ident = sb("ident_sb", P)
    causal = sb("causal_sb", NT * S).rearrange("p (t s) -> p t s", t=NT)
    cos = sb("cos_sb", NT * 8).rearrange("p (t f) -> p t f", t=NT)
    sin = sb("sin_sb", NT * 8).rearrange("p (t f) -> p t f", t=NT)
    levels = sb("levels_sb", len(LEVELS) * P, U8).rearrange("p (n i) -> p n i", n=len(LEVELS))
    parity = sb("parity_sb", P)
    before = sb("before_sb", NE * NE).rearrange("p (a b) -> p a b", a=NE)
    ones = sb("ones", P)
    prow = sb("prow", 6 * P).rearrange("p (n c) -> p n c", n=6)
    pcol = sb("pcol", 6 * P).rearrange("p (n c) -> p n c", n=6)
    crow = sb("crow", P)
    dt_row = sb("dt_row", 4).rearrange("p (l g) -> p l g", l=2)
    c_act = sb("c_act", 2 * KD).rearrange("p (b k) -> p b k", b=2)
    s5p = sb("s5p", 2 * 5 * 16).rearrange("p (l v j) -> p l v j", l=2, v=5)
    s5t = sb("s5t", 12 * 16).rearrange("p (v j) -> p v j", v=12)
    stat = sb("stat", 64)
    minus_half = sb("minus_half", 4)
    w_alpha = sb("w_alpha", S)
    router = sb("router", KD * NE).rearrange("p (k e) -> p k e", k=KD)
    router_b = sb("router_b", NE)
    moe = sb("moe", 12 * NE * NT).rearrange("p (v t e) -> p v t e", v=12, t=NT)
    moe_pair = sb("moe_pair", 2 * NE * NE).rearrange("p (v a b) -> p v a b", v=2, a=NE)
    region = sb("region", REGION)

    class Carve:
        def __init__(self, at=0):
            self.at = at

        def __call__(self, pattern, **sizes):
            n = math.prod(sizes.values())
            v = region[:, self.at:self.at + n]
            self.at += n
            assert self.at <= REGION, self.at
            names = " ".join(sizes)
            return v.rearrange(f"p ({names}) -> p {names}", **dict(list(sizes.items())[:-1])) if len(sizes) > 1 else v

    c1 = Carve()
    proj = c1("", t=NT, n=PROJ1)
    qk = c1("", b=4, c=4, s=S)
    kiT = c1("", s=S)
    kidup = c1("", t=NT, n=P)
    idx_r = c1("", b=2, s=512)
    idx_acc = c1("", t=NT, s=S)
    idx_work = c1("", t=NT, s=S)
    dsa_mask = c1("", t=NT, s=S)
    att_s = c1("", b=2, s=512)
    att_p = c1("", b=2, s=512)
    att_pT = c1("", b=2, s=512)
    rope_t = c1("", v=4, t=NT, h=16, f=8)
    top8 = c1("", t=NT, n=8)
    w_idx = c1("", t=NT, n=8)
    att_nm = c1("", u=12, h=4)
    att_rs = c1("", g=2, t=NT, h=NH)
    att_ri = c1("", g=2, t=NT, h=NH)

    c2 = Carve()
    eC = c2("", j=16, s=S)
    eS = c2("", j=16, s=S)
    uT = c2("", c=4, s=S)
    gqT = c2("", c=2, s=S)
    gkT = c2("", c=2, s=S)
    aT = c2("", s=S)
    Bst = c2("", r=2, c=4, n=P)
    Cst = c2("", r=2, c=4, n=P)
    gb = c2("", c=2, s=S)
    work_at = c2.at
    w5 = c2("", r=2, j=2, s=S)
    t5 = c2("", r=2, j=2, s=S)
    g5 = c2("", b=2, r=2, j=2, s=S)
    h5 = c2("", b=2, r=2, j=2, s=S)
    p5 = c2("", r=2, j=2, s=S)
    cw = Carve(work_at)
    e_tmp = cw("", r=2, j=16, s=64)
    Bnat = cw("", r=2, j=16, c=32)
    Cnat = cw("", r=2, c=4, n=P)
    Cmask = cw("", r=2, c=4, n=P)
    assert cw.at <= c2.at
    cg = Carve(work_at)
    gz = cg("", v=3, c=2, s=S)
    gD = cg("", b=2, n=512)
    gQ = cg("", b=2, n=512)
    gK = cg("", b=2, n=512)
    scT = cg("", b=2, j=2, c=2, i=P)
    scO = cg("", b=2, c=2, i=P)
    o_gla = cg("", t=NT, n=512)
    assert cg.at <= REGION
    vg = xn
    cm = Carve()
    earlier = cm("", n=P)
    iota = cm("", n=CAP)
    xg = cm("", k=KD, n=CAP)
    pick = cm("", t=NT, n=CAP)
    pick_w = cm("", t=NT, n=CAP)
    spread = cm("", n=S)
    moe_h = cm("", b=2, i=2, n=CAP)
    moe_s = cm("", b=2, i=2, n=CAP)
    moe_y = cm("", n=D)
    place = cm("", t=NT, n=TURNS + 1)
    weight = cm("", t=NT, n=TURNS + 1)
    turns = nc.alloc_sbuf_tensor("turns", [P, TURNS], mybir.dt.int32)[:, :]
    junk = ffn_tmp.rearrange("p b s -> p (b s)")

    psum = [nc.alloc_psum_tensor(f"bank{i}", [P, 512], F32)[:, :] for i in range(8)]
    bank_of = {}
    sig_pe, sig_act, sig_dve, sig_pool, sig_sp = (sig.of(e) for e in ("pe", "act", "dve", "pool", "sp"))

    def slot(key):
        i = where[key] % SLOTS
        return ring[:, i * SLOT:(i + 1) * SLOT]

    def loaded(key, r=None):
        i = where[key]
        n = 16 * (i // SLOTS + 1)
        return sems[f"slot_loaded{i % SLOTS}"], n if r is None else r * (16 * 3 * GROUPS // SLOTS) + n

    def col(l, name, n=1, at=0):
        r = (PROW if l < 2 else PROW2)[name] + at
        b = 2 * l + r // P if l < 2 else 4 + l - 2
        return pcol[:, b, r % P:r % P + n]

    kinds = {"mod_w": "w_ada", "in": "w_in", "out": "w_out"}

    def source(key, turn=None):
        kind, l = key[0], key[1]
        li = l % 2
        if kind in ("ada", "in"):
            name = {("ada", 0): "w_ada", ("ada", 1): "mod_w_2", ("in", 0): "w_in", ("in", 1): "w_in_2"}[kind, l // 2]
            w = A[name][li]
            n = min(CW, w.shape[1] - key[2] * CW)
            return w[:, key[2] * CW:key[2] * CW + n].rearrange("(k p) n -> p k n", p=P), KD, n
        if kind == "glu":
            return A["s5_w_glu_2"][li].rearrange("(k p) n -> p k n", p=P), 4, 512
        if kind == "out":
            w = A["w_out" if l < 2 else "w_out_2"][li]
            return w[key[2] * 256:(key[2] + 1) * 256, :].rearrange("(k p) n -> p k n", p=P), 2, D
        e, g = key[2], key[3]
        if kind == "up":
            if l < 2:
                w = A[("w_up_act", "w_up_lin")[key[4]]][li]
            elif l == 2:
                w = A[("ffn_w_gate_2", "ffn_w_up_2")[key[4]]][0]
            else:
                w = A[("moe_w_gate_2", "moe_w_up_2")[key[4]]][0]
                w = w[0] if turn is None else w[bass.ds(turn, 1)].rearrange("e k n -> (e k) n")
            return w[:, g * CW:(g + 1) * CW].rearrange("(k p) n -> p k n", p=P), KD, CW
        w = A["w_down"][li] if l < 2 else A["ffn_w_down_2"][0] if l == 2 else A["moe_w_down_2"][0]
        if l == 3:
            w = w[0] if turn is None else w[bass.ds(turn, 1)].rearrange("e k n -> (e k) n")
        return w[g * CW:(g + 1) * CW, :].rearrange("(k p) n -> p k n", p=P), 2, D

    def chunk(key):
        _, k, n = source(key)
        return slot(key)[:, 0:k * n].rearrange("p (k n) -> p k n", k=k)

    def x_ready(l, stage):
        if stage == "ffn":
            return ("x_new", l, "mix")
        return ("x_new", l - 1, "ffn") if l else ("x_loaded",)

    with nc.Block() as block:

        @block.tensor
        def _(pe):
            done = sig_pe
            user = [None] * 8
            turn = [0]

            def bank(key, freed, among=range(8)):
                b = among[turn[0] % len(among)]
                turn[0] += 1
                if user[b]:
                    pe.wait_ge(*until(*user[b]))
                user[b] = freed
                bank_of[key] = b
                return psum[b]

            def transposes(key, freed, pieces, among=range(8)):
                o = bank(key, freed, among)
                for c, piece in pieces:
                    m = nc.tensor.transpose(o[0:piece.shape[1], c:c + P], piece, ident)
                m.then_inc(*done("pe_tile", *key))

            def mod_tile(l, q, among=range(8)):
                pe.wait_ge(*until("mod_sum", l, q))
                o = bank(("mod", l, q), ("mod_out", l, q), among)
                if q // 4 in (2, 5):
                    m = nc.tensor.matmul(o[:, 0:CW], ones, mod_acc[:, q % 4, :], start=True, stop=True)
                else:
                    for i in range(2):
                        m = nc.tensor.matmul(o[:, i:i + 1], mod_acc[:, q % 4, i * P:(i + 1) * P], ones[:, 0:1],
                                             start=True, stop=True)
                m.then_inc(*done("pe_tile", "mod", l, q))

            def norm_tiles(l, stage):
                src = xn if l < 2 else x
                for b in range(4):
                    if b == 0:
                        pe.wait_ge(*(until("xn", l, stage) if l < 2 else until(*x_ready(l, stage))))
                    key = ("norm", l, stage, b)
                    transposes(key, ("hT", l, stage, b) if b % 2 == 0 else ("hTd", l, stage, b),
                               [(i * S + t * P, src[:, t, (2 * b + i) * P:(2 * b + i + 1) * P])
                                for i in range(2) for t in range(NT)])

            def hT_ready(l, stage):
                pe.wait_ge(*until("hT", l, stage, 2))
                pe.wait_ge(*until("hTd", l, stage, 3))

            def in_tokens(l, n):
                key = ("in", l, n)
                pe.wait_ge(*loaded(key))
                w = chunk(key)
                nn = w.shape[2]
                o = bank(key, ("in_out", l, n)).rearrange("p (t n) -> p t n", t=NT)
                for t in range(NT):
                    for k in range(KD):
                        m = nc.tensor.matmul(o[:, t, 0:nn], hT[:, k, t * P:(t + 1) * P], w[:, k, :],
                                             start=k == 0, stop=k == KD - 1)
                m.then_inc(*done("pe_tile", *key))

            def in_features(l, n):
                key = ("in", l, n)
                pe.wait_ge(*loaded(key))
                w = chunk(key)
                nn = w.shape[2]
                o = bank(key, ("in_out", l, n)).rearrange("p (t n) -> p t n", t=NT)
                for i in range(-(-nn // P)):
                    r = min(P, nn - i * P)
                    for k in range(KD):
                        m = nc.tensor.matmul(o[0:r, i, :], w[:, k, i * P:i * P + r], hT[:, k, :],
                                             start=k == 0, stop=k == KD - 1)
                m.then_inc(*done("pe_tile", *key))

            def qk_tiles(l, b, c0, evac, among=range(8)):
                for i in range(2):
                    transposes(("qk", l, b, evac, i), ("qk_out", l, evac, i),
                               [(j * S + t * P, proj[:, t, c0 + (2 * i + j) * P:c0 + (2 * i + j + 1) * P])
                                for j in range(2) for t in range(NT)], among)

            def indexer(l):
                pe.wait_ge(*until("rope", l, 2))
                qk_tiles(l, 0, QI, "qi")
                pe.wait_ge(*until("kidup", l))
                transposes(("kiT", l), ("kiT_out", l), [(t * P, kidup[:, t, :]) for t in range(NT)])

            def indexer_logits(l):
                pe.wait_ge(*until("kiT_out", l))
                for t in range(NT):
                    for n in range(4 if t else 2):
                        o = bank(("idx", l, t, n), ("idx_relu", l, t, n))
                        kn = (t + 1) * P
                        for i, h in enumerate(unit_heads(t, n)):
                            r = 64 * (h % 2)
                            m = nc.tensor.matmul(o[:, i * kn:(i + 1) * kn], qk[r:r + 64, 0, h // 2, t * P:(t + 1) * P],
                                                 kiT[r:r + 64, 0:kn], start=True, stop=True)
                        m.then_inc(*done("pe_tile", "idx", l, t, n))

            def attention(l):
                o = {}
                for u in range(len(UNITS1) + 2):
                    if u < len(UNITS1):
                        g, t, n = UNITS1[u]
                        kn = (t + 1) * P
                        if (t, n) == (0, 0):
                            if g:
                                pe.wait_ge(*until("rope", l, 1))
                                qk_tiles(l, 0, 1536, "dq", range(6))
                                qk_tiles(l, 3, 2048, "dk", range(6))
                            pe.wait_ge(*until("qk_out", l, ("mk", "dk")[g], 1))
                        s = bank(("sc", l, u), ("att_mask", l, u), range(6))
                        for i, h in enumerate(unit_heads(t, n)):
                            r = 64 * (h % 2)
                            m = nc.tensor.matmul(s[:, i * kn:(i + 1) * kn],
                                                 qk[r:r + 64, (1, 0)[g], h // 2, t * P:(t + 1) * P],
                                                 qk[r:r + 64, (2, 3)[g], h // 2, 0:kn], start=True, stop=True)
                        m.then_inc(*done("pe_tile", "sc", l, u))
                    if 1 <= u <= len(UNITS1):
                        g, t, n = UNITS1[u - 1]
                        pe.wait_ge(*until("att_exp", l, u - 1))
                        transposes(("pT", l, u - 1), ("att_pT", l, u - 1),
                                   [(i * P, att_p[:, (u - 1) % 2, i * P:(i + 1) * P]) for i in range(4)], range(6))
                    if u >= 2:
                        g, t, n = UNITS1[u - 2]
                        heads = unit_heads(t, n)
                        if n == 0:
                            b = 6 + (2 * g + t) % 2
                            if user[b]:
                                pe.wait_ge(*until(*user[b]))
                            user[b] = ("att_o", l, g, t)
                            bank_of[("o", l, g, t)] = b
                            o[g, t] = psum[b]
                        pe.wait_ge(*until("att_pT", l, u - 2))
                        for i, h in enumerate(heads):
                            for kb in range(t + 1):
                                at = (i * (t + 1) + kb) * P
                                vc = 1536 * g + 1024 + h * HD
                                m = nc.tensor.matmul(o[g, t][:, h * HD:(h + 1) * HD], att_pT[:, (u - 2) % 2, at:at + P],
                                                     proj[:, kb, vc:vc + HD], start=kb == 0, stop=kb == t)
                        m.then_inc(*done("pe_tile", "pv", l, u - 2))

            def o_transposes(l):
                for b in range(4):
                    pe.wait_ge(*until("att_on", l, b // 2, 1))
                    transposes(("oT", l, b), ("oT_out", l, b),
                               [(i * S + t * P, xn[:, t, (2 * b + i) * P:(2 * b + i + 1) * P])
                                for i in range(2) for t in range(NT)])

            def out_projection(l):
                tiles = [bank(("y", l, "mix", i), ("post", l, "mix", i), range(4, 8)) for i in range(4)]
                for n in range(4):
                    key = ("out", l, n)
                    pe.wait_ge(*loaded(key))
                    w = chunk(key)
                    for k in range(2):
                        kk = 2 * n + k
                        for i in range(4):
                            t, c = i // 2, i % 2
                            m = nc.tensor.matmul(tiles[i], hT[:, kk, t * P:(t + 1) * P], w[:, k, c * 512:(c + 1) * 512],
                                                 start=kk == 0, stop=kk == KD - 1, skip_group_check=True)
                    m.then_inc(*done("pe_used", *key))

            def ffn(l):
                tiles = [None] * 4
                up_banks = range(4)

                def up(e, f):
                    g, i = f // 2, f % 2
                    o = bank(("up", l, e, f), ("up_out", l, e, f), up_banks)
                    for m in (0, 1):
                        key = ("up", l, e, g, m)
                        pe.wait_ge(*loaded(key))
                        w = chunk(key)
                        for k in range(KD):
                            last = nc.tensor.matmul(o[:, m * S:(m + 1) * S], w[:, k, i * P:(i + 1) * P], hT[:, k, :],
                                                    start=k == 0, stop=k == KD - 1)
                    last.then_inc(*done("pe_tile", "up", l, e, f))

                def down(e, f):
                    g, i = f // 2, f % 2
                    key = ("down", l, e, g)
                    pe.wait_ge(*loaded(key))
                    pe.wait_ge(*until("up_out", l, e, f))
                    w = chunk(key)
                    first, final = e == 0 and f == 0, e == experts - 1 and f == FF[l] // P - 1
                    for j in range(4):
                        t, c = j // 2, j % 2
                        last = nc.tensor.matmul(tiles[j], hf[:, f % 4, t * P:(t + 1) * P], w[:, i, c * 512:(c + 1) * 512],
                                                start=first, stop=final, skip_group_check=True)
                    if i == 1:
                        last.then_inc(*done("pe_used", *key))

                experts = 1
                hT_ready(l, "ffn")
                turn[0] = 0
                for j in range(4):
                    b = 4 + j
                    if user[b]:
                        pe.wait_ge(*until(*user[b]))
                    user[b] = ("post", l, "ffn", j)
                    bank_of["y", l, "ffn", j] = b
                    tiles[j] = psum[b]
                fs = [(e, f) for e in range(experts) for f in range(FF[l] // P)]
                lag = 2
                for n in range(len(fs) + lag):
                    if n < len(fs):
                        up(*fs[n])
                        if fs[n][1] % 2 == 1 and fs[n][1] > 1:
                            for q in ada_in_ffn(l, fs[n][1] // 2 - 1):
                                mod_tile(l + 1, q, up_banks)
                    if n >= lag:
                        down(*fs[n - lag])
                for q in ada_in_ffn(l, ffn_groups(l) - 1):
                    mod_tile(l + 1, q, up_banks)

            def mixer_two(l):
                norm_tiles(l, "mix")
                hT_ready(l, "mix")
                for n in (8, 0, 1, 2, 3):
                    in_features(l, n)
                pe.wait_ge(*until("b_masked", l))
                for r in range(2):
                    transposes(("BT", l, r), ("bst", l, r), [(q * P, Bnat[:, r, 4 * q:4 * q + 4, :].rearrange("p j c -> p (j c)")) for q in range(4)])
                for r in range(2):
                    transposes(("CT", l, r), ("c_masked", l, r), [(q * P, Cnat[:, r, q, :]) for q in range(4)])
                o = bank(("lg", l), ("gla_z", l))
                pe.wait_ge(*until("w_alpha", l))
                pe.wait_ge(*until("in_out", l, 8))
                for i in range(2):
                    m = nc.tensor.matmul(o[:, i * S:(i + 1) * S], w_alpha[0:16, i * P:(i + 1) * P], aT[0:16, :],
                                         start=True, stop=True)
                m.then_inc(*done("pe_tile", "lg", l))

                def s5_in(u):
                    qq, i = u // 4, u % 4
                    for r in range(2):
                        o = bank(("bu", l, u, r), ("s5_w", l, u), range(6))
                        for jj in range(2):
                            q = 2 * qq + jj
                            m = nc.tensor.matmul(o[:, jj * S:(jj + 1) * S], Bst[32 * i:32 * i + 32, r, q, :],
                                                 uT[32 * i:32 * i + 32, q, :], start=True, stop=True)
                        m.then_inc(*done("pe_tile", "bu", l, u, r))

                ys = {}

                def s5_out(u):
                    qq, i = u // 4, u % 4
                    if i == 0:
                        b = 6 + qq
                        if user[b]:
                            pe.wait_ge(*until(*user[b]))
                        user[b] = ("s5_y", l, qq)
                        bank_of["s5y", l, qq] = b
                        ys[qq] = psum[b]
                    pe.wait_ge(*until("s5_h", l, u))
                    if u == 0:
                        pe.wait_ge(*until("cst", l))
                    for jj in range(2):
                        for r in range(2):
                            m = nc.tensor.matmul(ys[qq][32 * i:32 * i + 32, jj * S:(jj + 1) * S],
                                                 Cst[:, r, 2 * qq + jj, 32 * i:32 * i + 32], h5[:, u % 2, r, jj, :],
                                                 start=r == 0, stop=r == 1)
                    m.then_inc(*done("pe_tile", "s5o", l, u))

                pe.wait_ge(*until("bst", l, 1))
                pe.wait_ge(*until("in_out", l, 1))
                s5_in(0)
                s5_in(1)
                for u in range(2, 10):
                    if u in (2, 3, 4, 5):
                        n = u + 2
                        key = ("in", l, n)
                        pe.wait_ge(*loaded(key))
                        w = chunk(key)
                        o = bank(key, ("in_out", l, n), range(6)).rearrange("p (t n) -> p t n", t=NT)
                        for t in range(NT):
                            for k in range(KD):
                                m = nc.tensor.matmul(o[:, t, :], hT[:, k, t * P:(t + 1) * P], w[:, k, :],
                                                     start=k == 0, stop=k == KD - 1)
                        m.then_inc(*done("pe_tile", *key))
                    if u < 8:
                        s5_in(u)
                    s5_out(u - 2)
                key = ("glu", l)
                pe.wait_ge(*loaded(key))
                pe.wait_ge(*until("s5_gelu", l, 1))
                w = chunk(key)
                for b in range(2):
                    o = bank(("glu", l, b), ("s5_sig", l, b))
                    for i in range(2):
                        for k in range(4):
                            m = nc.tensor.matmul(o[:, i * S:(i + 1) * S], w[:, k, (2 * b + i) * P:(2 * b + i + 1) * P],
                                                 uT[:, k, :], start=k == 0, stop=k == 3)
                    m.then_inc(*done("pe_tile", "glu", l, b))
                pe.wait_ge(*until("gla_k", l, 128))
                for par in range(2):
                    r = 64 * par
                    o = bank(("off", l, par), ("off_out", l, par))
                    for c in range(2):
                        m = nc.tensor.matmul(o[:, c * P:(c + 1) * P], gK[r:r + 64, 0, c * S:c * S + P],
                                             gQ[r:r + 64, 0, c * S + P:c * S + S], start=True, stop=True)
                    m.then_inc(*done("pe_tile", "off", l, par))
                for n, half in enumerate(LEVELS):
                    if half:
                        pe.wait_ge(*until("gla_k", l, half))
                    for par in range(2):
                        r = 64 * par
                        o = bank(("lv", l, n, par), ("lv_out", l, n, par))
                        for t in range(NT):
                            for c in range(2):
                                at = c * S + t * P
                                kk = gK[r:r + 64, (n + 1) % 2, at:at + P] if half else gkT[r:r + 64, c, t * P:(t + 1) * P]
                                qq = gQ[r:r + 64, (n + 1) % 2, at:at + P] if half else gqT[r:r + 64, c, t * P:(t + 1) * P]
                                m = nc.tensor.matmul(o[:, (2 * t + c) * P:(2 * t + c + 1) * P], kk, qq, start=True, stop=True)
                        m.then_inc(*done("pe_tile", "lv", l, n, par))
                pe.wait_ge(*until("off_out", l, 1))
                pe.wait_ge(*until("lv_out", l, len(LEVELS) - 1, 1))
                pe.wait_ge(*until("in_out", l, 5))
                for t in range(NT):
                    o = bank(("go", l, t), ("gla_o", l, t))
                    for h in range(4):
                        for j in range(t + 1):
                            lhs = scT[:, h % 2, j, h // 2, :] if j == t else scO[:, h % 2, h // 2, :]
                            m = nc.tensor.matmul(o[:, h * P:(h + 1) * P], lhs, vg[:, j, h * P:(h + 1) * P],
                                                 start=j == 0, stop=j == t)
                    m.then_inc(*done("pe_tile", "go", l, t))
                pe.wait_ge(*until("gla_o", l, 1))
                for b in range(2):
                    transposes(("goT", l, b), ("goT_out", l, b),
                               [(i * S + t * P, o_gla[:, t, (2 * b + i) * P:(2 * b + i + 1) * P])
                                for i in range(2) for t in range(NT)])
                pe.wait_ge(*until("goT_out", l, 1))
                pe.wait_ge(*until("s5_done", l))

            def mixture():
                up_b, pick_b, y_b, z_b = psum[0:2], psum[2:4], psum[4:6], psum[6:8]

                def pick_tiles(e, r):
                    for b in range(2):
                        if b == 0:
                            pe.wait_ge(*(within(r, 0, "moe_vec", "pick", e) if r is not None else until("moe_vec", "pick", e)))
                        for i in range(4):
                            k = 4 * b + i
                            for t in range(NT):
                                m = nc.tensor.matmul(pick_b[b][:, i * CAP:(i + 1) * CAP], x[:, t, k * P:(k + 1) * P], pick[:, t, :],
                                                     start=t == 0, stop=t == NT - 1)
                        m.then_inc(*done("moe_tile", "pick", b, e))

                def spread_y(e, w_y, w_add):
                    pe.wait_ge(*w_y)
                    for i in range(4):
                        t, c = i // 2, i % 2
                        if i >= 2:
                            pe.wait_ge(*w_add(i - 2))
                        nc.tensor.matmul(z_b[i % 2], spread[:, t * P:(t + 1) * P], moe_y[:, c * 512:(c + 1) * 512],
                                         start=True, stop=True).then_inc(*done("moe_tile" if e != "tail" else "moe_tail", "z", i, e))

                def body(e, r):
                    now = (lambda *ev: until(*ev, e)) if r is None else (lambda *ev: within(r, 0, *ev, e))

                    def up(g):
                        if g >= 2:
                            pe.wait_ge(*now("moe_vec", "h", g - 2))
                        elif r is not None:
                            pe.wait_ge(*within(r, 1, "moe_vec", "h", GROUPS - 2 + g, e))
                        if g == 0:
                            pe.wait_ge(*(until("moe_act", "xg", "start") if r is None else within(r, 1, "moe_act", "xg", e)))
                        o = up_b[g % 2]
                        for m in (0, 1):
                            key = ("up", 3, e, g, m)
                            pe.wait_ge(*loaded(key, r))
                            w = chunk(key)
                            for i in range(2):
                                at = (2 * m + i) * CAP
                                for k in range(KD):
                                    last = nc.tensor.matmul(o[:, at:at + CAP], w[:, k, i * P:(i + 1) * P], xg[:, k, :],
                                                            start=k == 0, stop=k == KD - 1)
                        last.then_inc(*done("moe_tile", "up", g, e))

                    def down(g):
                        key = ("down", 3, e, g)
                        pe.wait_ge(*loaded(key, r))
                        pe.wait_ge(*now("moe_vec", "h", g))
                        w = chunk(key)
                        for i in range(2):
                            for c in range(2):
                                last = nc.tensor.matmul(y_b[c], moe_h[:, g % 2, i, :], w[:, i, c * 512:(c + 1) * 512],
                                                        start=g + i == 0, stop=g == GROUPS - 1 and i == 1, skip_group_check=True)
                        last.then_inc(*done("moe_used", "down", g, e))

                    up(0)
                    up(1)
                    if r is not None:
                        spread_y(e, within(r, 1, "moe_act", "y", e), lambda i: now("moe_vec", "z", i))
                    if r is None:
                        pe.wait_ge(*until("moe_vec", "pick", "start"))
                    for t in range(NT):
                        m = nc.tensor.transpose(pick_b[0][:, t * P:(t + 1) * P], pick_w[:, t, :], ident)
                    m.then_inc(*done("moe_tile", "spread", e))
                    for g in range(GROUPS):
                        if 2 <= g + 1 < GROUPS:
                            up(g + 1)
                        if g == GROUPS - 2:
                            pe.wait_ge(*now("moe_act", "spread"))
                            pick_tiles(e, r)
                        down(g)

                pe.wait_ge(*until("chosen"))
                pe.wait_ge(*until("const_moe", 1))
                o = bank(("places",), ("placed",))
                sel = moe[:, 8]
                nc.tensor.matmul(o[:, 0:NE], earlier, sel[:, 0, :], start=True, stop=True)
                for part, lhs in ((1, earlier), (2, ones)):
                    nc.tensor.matmul(o[:, part * NE:(part + 1) * NE], ones, sel[:, 0, :], start=True, stop=False)
                    m = nc.tensor.matmul(o[:, part * NE:(part + 1) * NE], lhs, sel[:, 1, :], start=False, stop=True)
                m.then_inc(*done("pe_tile", "places"))
                pe.wait_ge(*until("placed"))
                pick_tiles("start", None)
                body("first", None)
                pe.wait_ge(*until("turns"))
                n = pe.value_load(turns[0:1, 0:1], min_val=NE - 1, max_val=TURNS - 1)
                done.begin()
                with pe.Fori(0, n) as r:
                    body("loop", r)
                done.end("moe_tile", "moe_used")
                spread_y("tail", within(n, 1, "moe_act", "y", "loop"), lambda i: until("moe_last", "z", i))

            pe.wait_ge(*until("const", "ident"))
            pe.wait_ge(*until("param_rows"))
            pe.wait_ge(*until("dt_rows", 3))
            pe.wait_ge(*until("memset_ones"))
            for b in range(2):
                transposes(("param", b), ("pcol", b), [(i * P, prow[:, 4 * b + i, :]) for i in range(4 if b == 0 else 2)])
            transposes(("cT",), ("c_raw",), [(0, crow)])
            for q in range(8):
                mod_tile(0, q)
            for l in range(LAYERS):
                if l < 2:
                    norm_tiles(l, "mix")
                    hT_ready(l, "mix")
                    for i, n in enumerate(PROJ_ORDER):
                        in_tokens(l, n)
                        if l == 0:
                            for q in ([8 + i] if i < 14 else [22, 23]):
                                mod_tile(0, q)
                        if i == 4:
                            indexer(l)
                        if i == 6:
                            indexer_logits(l)
                    pe.wait_ge(*until("rope", l, 0))
                    qk_tiles(l, 1, 0, "mq")
                    qk_tiles(l, 2, 512, "mk")
                    attention(l)
                    o_transposes(l)
                    pe.wait_ge(*until("oT_out", l, 3))
                else:
                    mixer_two(l)
                out_projection(l)
                norm_tiles(l, "ffn")
                if l == 3:
                    hT_ready(l, "ffn")
                    pe.wait_ge(*until("router_loaded"))
                    pe.wait_ge(*until("router_b_loaded"))
                    o = bank(("router",), ("logits",))
                    for t in range(NT):
                        for k in range(KD):
                            nc.tensor.matmul(o[:, t * NE:(t + 1) * NE], hT[:, k, t * P:(t + 1) * P], router[:, k, :],
                                             start=k == 0, stop=False)
                        m = nc.tensor.matmul(o[:, t * NE:(t + 1) * NE], ones[0:1, :], router_b[0:1, :],
                                             start=False, stop=True)
                    m.then_inc(*done("pe_tile", "router"))
                    mixture()
                else:
                    ffn(l)

        @block.sync
        def _(sp):
            body = where["up", 3, "loop", 0, 0]
            for i, (key, _) in enumerate(plan[:body]):
                if i >= SLOTS:
                    sp.wait_ge(*until(*plan[i - SLOTS][1]))
                src, _, _ = source(key)
                sp.dma_start(chunk(key), src).then_inc(sems[f"slot_loaded{i % SLOTS}"], 16)
            sp.wait_ge(*until("turns"))
            n = sp.value_load(turns[0:1, 0:1], min_val=NE - 1, max_val=TURNS - 1)
            with sp.Fori(0, n) as r:
                turn = sp.value_load(turns[0:1, bass.ds(r + 1, 1)], min_val=0, max_val=NE - 1)
                for c in range(3 * GROUPS):
                    key = plan[body + c][0]
                    src, _, _ = source(key, turn)
                    sp.wait_ge(*(within(r, 0, *plan[body + c - SLOTS][1]) if c >= SLOTS
                                 else within(r, 1, *plan[body + c - SLOTS + 3 * GROUPS][1])))
                    sp.dma_start(chunk(key), src).then_inc(sems[f"slot_loaded{(body + c) % SLOTS}"], 16)
            for i in range(4):
                t, c = i // 2, i % 2
                if c == 0:
                    sp.wait_ge(*until("x_new_t", LAYERS - 1, "ffn", t) if t == 0 else until("x_new", LAYERS - 1, "ffn"))
                    sp.dma_start(out[0, t * P:(t + 1) * P, :], x[:, t, :]).then_inc(*sig_sp.dma("stored", t))
            sp.wait_ge(*until("stored", 1))

        @block.gpsimd
        def _(pool):
            done = sig_pool
            nc.gpsimd.memset(minus_half, -0.5).then_inc(*done("pool_chain", "half"))
            nc.gpsimd.memset(ones, 1.0).then_inc(*done("memset_ones"))
            pool.wait_ge(*done.prev())

            def tables(l):
                sl = l - 2
                eC4, eS4 = eC, eS
                nc.gpsimd.tensor_copy(eC4[:, :, 0:1], s5p[:, sl, 1, :].unsqueeze(2)).then_inc(*done("pool_chain", l, "c0"))
                nc.gpsimd.tensor_copy(eS4[:, :, 0:1], s5p[:, sl, 2, :].unsqueeze(2)).then_inc(*done("pool_chain", l, "s0"))
                k = 1
                while k < S:
                    for h0 in range(0, k, 64):
                        w = min(64, k)
                        ca, sa = eC4[:, :, h0:h0 + w], eS4[:, :, h0:h0 + w]
                        cb = eC4[:, :, k - 1:k].broadcast_to([P, 16, w])
                        sb_ = eS4[:, :, k - 1:k].broadcast_to([P, 16, w])
                        oc, os_ = eC4[:, :, k + h0:k + h0 + w], eS4[:, :, k + h0:k + h0 + w]
                        ta, tb = e_tmp[:, 0, :, 0:w], e_tmp[:, 1, :, 0:w]
                        pool.wait_ge(*done.prev())
                        nc.gpsimd.tensor_tensor(oc, ca, cb, ALU.mult).then_inc(*done("pool_chain", l, k, h0, 0))
                        nc.gpsimd.tensor_tensor(ta, sa, sb_, ALU.mult).then_inc(*done("pool_chain", l, k, h0, 1))
                        nc.gpsimd.tensor_tensor(os_, sa, cb, ALU.mult).then_inc(*done("pool_chain", l, k, h0, 2))
                        nc.gpsimd.tensor_tensor(tb, ca, sb_, ALU.mult).then_inc(*done("pool_chain", l, k, h0, 3))
                        pool.wait_ge(*done.prev())
                        nc.gpsimd.tensor_tensor(oc, oc, ta, ALU.subtract).then_inc(*done("pool_chain", l, k, h0, 4))
                        nc.gpsimd.tensor_tensor(os_, os_, tb, ALU.add).then_inc(*done("pool_chain", l, k, h0, 5))
                    k *= 2
                pool.wait_ge(*done.prev())
                nc.gpsimd.memset(stat[:, 63:64], 0.0).then_inc(*done("tables", l))

            def rotate(l, u):
                qq, i = u // 4, u % 4
                c, s = eC[:, 8 * qq + i:8 * qq + i + 5:4, :], eS[:, 8 * qq + i:8 * qq + i + 5:4, :]
                g, h = g5[:, u % 2], h5[:, u % 2]
                pool.wait_ge(*until("s5_g", l, u))
                if u >= 2:
                    pool.wait_ge(*until("pe_tile", "s5o", l, u - 2))
                nc.gpsimd.tensor_tensor(h[:, 0], c, g[:, 0], ALU.mult).then_inc(*done("pool_chain", l, "r", u, 0))
                nc.gpsimd.tensor_tensor(p5[:, 0], s, g[:, 1], ALU.mult).then_inc(*done("pool_chain", l, "r", u, 1))
                nc.gpsimd.tensor_tensor(h[:, 1], s, g[:, 0], ALU.mult).then_inc(*done("pool_chain", l, "r", u, 2))
                nc.gpsimd.tensor_tensor(p5[:, 1], c, g[:, 1], ALU.mult).then_inc(*done("pool_chain", l, "r", u, 3))
                pool.wait_ge(*done.prev())
                nc.gpsimd.tensor_tensor(h[:, 0], h[:, 0], p5[:, 0], ALU.subtract).then_inc(*done("pool_chain", l, "r", u, 4))
                nc.gpsimd.tensor_tensor(h[:, 1], h[:, 1], p5[:, 1], ALU.add).then_inc(*done("s5_h", l, u))
                pool.wait_ge(*done.prev())

            def power(dst, *key):
                pool.wait_ge(*until("variance", *key))
                nc.gpsimd.tensor_tensor(dst, dst, minus_half[:, 0:dst.shape[1]], ALU.pow).then_inc(*done("rstd", *key))

            for l in range(LAYERS):
                if l < 2:
                    power(stat[:, 32:34], l, "norm", "mix")
                    power(stat[:, 36:40], l, "o")
                    power(stat[:, 42:44], l, "post", "mix")
                    power(stat[:, 32:34], l, "norm", "ffn")
                else:
                    for u in range(8):
                        rotate(l, u)
                    pool.wait_ge(*until("s5_y", l, 1))
                    nc.gpsimd.memset(scT, 0.0).then_inc(*done("gla_zero", l, 0))
                    nc.gpsimd.memset(gQ, 0.0).then_inc(*done("gla_zero", l, 1))
                    nc.gpsimd.memset(gK, 0.0).then_inc(*done("gla_zero", l, 2))
                    for t in range(NT):
                        power(stat[:, 36:40], l, "gla", t)
                    for t in range(NT):
                        power(stat[:, 58:59], l, "post", "mix", t)
                if l in (1, 2):
                    pool.wait_ge(*until("post", l, "mix", 3))
                    if l == 1:
                        pool.wait_ge(*until("s5_params"))
                    tables(l + 1)
                if l < 2:
                    power(stat[:, 42:44], l, "post", "ffn")
                else:
                    for t in range(NT):
                        power(stat[:, 58:59], l, "post", "ffn", t)

        @block.scalar
        def _(act):
            done = sig_act

            def tile(*key):
                act.wait_ge(*until("pe_tile", *key))
                return psum[bank_of[key]]

            def run(out_, in_, func, *event, **kw):
                return nc.scalar.activation(out_, in_, func, **kw).then_inc(*done(*event))

            def load(dst, src, *event):
                return act.dma_start(dst, src).then_inc(*done.dma(*event))

            def squares(l, stage):
                for t in range(NT):
                    if t == 0:
                        act.wait_ge(*until(*x_ready(l, stage)))
                    else:
                        act.wait_ge(*done.prev())
                    run(junk, x[:, t, :], ACT.Square, "ssq", l, stage, t, accum_out=stat[:, 2 * (stage == "ffn") + t:2 * (stage == "ffn") + t + 1])

            def norm_out(l, stage):
                act.wait_ge(*until("scales", l, stage))
                b0 = 24 * (stage == "ffn")
                for b in (0, 2):
                    p_ = tile("norm", l, stage, b)
                    for i in range(2):
                        k = 2 * b + i
                        name = ("hT", l, stage, b) if i else ("hT_half", l, stage, b)
                        run(hT[:, k, :], p_[:, i * S:(i + 1) * S], ACT.Identity, *name,
                            scale=scale_col[:, int(stage == "ffn"), k:k + 1], bias=mod_col[:, l % 2, b0 + k:b0 + k + 1])

            def in_out(l, n):
                p_ = tile("in", l, n).rearrange("p (t n) -> p t n", t=NT)
                nn = min(CW, PROJ1 - n * CW)
                run(proj[:, :, n * CW:n * CW + nn], p_[:, :, 0:nn], ACT.Copy, "in_out", l, n)

            def post_squares(l, stage):
                for i in range(4):
                    if i:
                        act.wait_ge(*done.prev())
                    act.wait_ge(*until("pe_used", "out", l, 3) if stage == "mix" else until("pe_used", "down", l, 0, ffn_groups(l) - 1))
                    run(junk[:, 0:512], psum[bank_of["y", l, stage, i]], ACT.Square, "y_ssq", l, stage, i,
                        accum_out=stat[:, 8 + i:9 + i])

            def mixer_one(l):
                squares(l, "mix")
                norm_out(l, "mix")
                for i, n in enumerate(PROJ_ORDER):
                    in_out(l, n)
                    if i == 4:
                        for j in range(2):
                            p_ = tile("qk", l, 0, "qi", j)
                            run(qk[:, 0, 2 * j:2 * j + 2, :].rearrange("p c s -> p (c s)"), p_, ACT.Copy, "qk_out", l, "qi", j)
                        p_ = tile("kiT", l)
                        run(kiT, p_[:, 0:S], ACT.Copy, "kiT_out", l)
                    if i == 6:
                        for t in range(NT):
                            for n2 in range(4 if t else 2):
                                p_ = tile("idx", l, t, n2)
                                m = n2 if t else n2
                                order = n2 + (2 if t else 0)
                                if order >= 2:
                                    act.wait_ge(*until("idx_sum", l, order - 2))
                                run(idx_r[:, order % 2, :], p_, ACT.Relu, "idx_relu", l, t, n2, scale=0.125)
                for b, name in ((1, "mq"), (2, "mk")):
                    for j in range(2):
                        p_ = tile("qk", l, b, name, j)
                        run(qk[:, b, 2 * j:2 * j + 2, :].rearrange("p c s -> p (c s)"), p_, ACT.Copy, "qk_out", l, name, j,
                            scale=0.125 if b == 1 else 1.0)
                for u, (g, t, n) in enumerate(UNITS1):
                    if g == 1 and (t, n) == (0, 0):
                        for b, name in ((0, "dq"), (3, "dk")):
                            for j in range(2):
                                p_ = tile("qk", l, b, name, j)
                                run(qk[:, b, 2 * j:2 * j + 2, :].rearrange("p c s -> p (c s)"), p_, ACT.Copy, "qk_out", l, name, j,
                                    scale=0.125 if b == 0 else 1.0)
                    act.wait_ge(*until("att_max", l, u))
                    if u >= 2:
                        act.wait_ge(*until("pe_tile", "pT", l, u - 2))
                    kn = (t + 1) * P
                    heads = unit_heads(t, n)
                    for i, h in enumerate(heads):
                        event = ("att_exp", l, u) if i == len(heads) - 1 else ("act_chain", l, "exp", u, i)
                        run(att_p[:, u % 2, i * kn:(i + 1) * kn], att_s[:, u % 2, i * kn:(i + 1) * kn], ACT.Exp, *event,
                            bias=att_nm[:, u, i:i + 1], accum_out=att_rs[:, g, t, h:h + 1])
                for g in range(2):
                    for t in range(NT):
                        act.wait_ge(*until("att_o", l, g, t))
                        act.wait_ge(*done.prev())
                        run(junk[:, 0:512], xn[:, t, g * 512:(g + 1) * 512], ACT.Square, "o_ssq", l, g, t,
                            accum_out=stat[:, 16 + 2 * g + t:17 + 2 * g + t])
                for b in range(4):
                    p_ = tile("oT", l, b)
                    for i in range(2):
                        k = 2 * b + i
                        name = ("oT_out", l, b) if i else ("act_chain", l, "oT", b)
                        run(hT[:, k, :], p_[:, i * S:(i + 1) * S], ACT.Copy, *name, scale=col(l, "g_moba_out", 1, k))

            def mixer_two(l):
                norm_out(l, "mix")
                feats = {8: aT[0:16, :], 0: uT[:, 0:2, :], 1: uT[:, 2:4, :], 2: gqT, 3: gkT}
                for n in (8, 0, 1, 2, 3):
                    p_ = tile("in", l, n)
                    dst = feats[n] if n == 8 else feats[n].rearrange("p c s -> p (c s)")
                    run(dst, p_[0:16, 0:S] if n == 8 else p_, ACT.Copy, "in_out", l, n, scale=0.125 if n == 2 else 1.0)
                for r in range(2):
                    p_ = tile("BT", l, r)
                    run(Bst[:, r].rearrange("p c n -> p (c n)"), p_, ACT.Copy, "bst", l, r)
                for n in (4, 5, 6, 7):
                    p_ = tile("in", l, n).rearrange("p (t n) -> p t n", t=NT)
                    run(vg[:, :, (n - 4) * CW:(n - 3) * CW], p_, ACT.Copy if n < 6 else ACT.Silu, "in_out", l, n)
                for qq in range(2):
                    act.wait_ge(*until("s5_y", l, qq))
                    v = uT[:, 2 * qq:2 * qq + 2, :].rearrange("p c s -> p (c s)")
                    run(v, v, ACT.Gelu_apprx_tanh, "s5_gelu", l, qq)
                for b in range(2):
                    p_ = tile("glu", l, b)
                    for i in range(2):
                        c = 2 * b + i
                        name = ("s5_sig", l, b) if i else ("act_chain", l, "sig", b)
                        run(hT[:, c, :], p_[:, i * S:(i + 1) * S], ACT.Sigmoid, *name, bias=col(l, "s5_b_glu_2", 1, c))
                act.wait_ge(*until("gla_abs", l))
                run(gz[:, 1], gz[:, 1], ACT.Exp, "act_chain", l, "lse")
                act.wait_ge(*done.prev())
                run(gz[:, 1], gz[:, 1], ACT.Ln, "gla_ln", l, bias=1.0)
                for m, half in enumerate([P] + LEVELS[:-1]):
                    act.wait_ge(*until("gla_d", l, half))
                    run(gD[:, m % 2, :], gD[:, m % 2, :], ACT.Exp, "gla_e", l, half)
                    if m == 0:
                        for par in range(2):
                            p_ = tile("off", l, par)
                            run(scO[:, par].rearrange("p c i -> p (c i)"), p_[:, 0:S], ACT.Copy, "off_out", l, par)
                for t in range(NT):
                    p_ = tile("go", l, t)
                    for h in range(4):
                        act.wait_ge(*done.prev())
                        run(junk[:, 0:P], p_[:, h * P:(h + 1) * P], ACT.Square, "go_ssq", l, t, h,
                            accum_out=stat[:, 20 + 4 * t + h:21 + 4 * t + h])
                for b in range(2):
                    p_ = tile("goT", l, b)
                    for i in range(2):
                        k = 2 * b + i
                        name = ("goT_out", l, b) if i else ("act_chain", l, "goT", b)
                        run(hT[:, 4 + k, :], p_[:, i * S:(i + 1) * S], ACT.Copy, *name, scale=col(l, "gla_head_gain_2", 1, k))

            def load_rows(l, stage):
                if (l, stage) != (0, "mix"):
                    act.wait_ge(*until("x_new", *((l, "mix") if stage == "ffn" else (l - 1, "ffn"))))
                if l < 2:
                    load(rows[:, 0, :], A["g_post_" + stage][l].partition_broadcast(P), f"rows_{stage}{l}", 0)
                else:
                    for i, g in enumerate("gb"):
                        load(rows[:, i, :], A[f"ln_{stage}_{g}_2"][l - 2].partition_broadcast(P), f"rows_{stage}{l}", i)

            def load_gate_bias(l):
                b = A["b_ada"][l] if l < 2 else A["mod_b_2"][l - 2]
                if l:
                    act.wait_ge(*until("x_new", l - 1, "mix"))
                load(mod_gate[:, 0, :], b[2 * D:3 * D].partition_broadcast(P), f"gate_bias_mix{l}")
                load(mod_gate[:, 1 + l % 2, :], b[5 * D:6 * D].partition_broadcast(P), f"gate_bias_ffn{l}")

            def mixture():
                def picked(e, r):
                    for b in range(2):
                        act.wait_ge(*(until("moe_tile", "pick", b, e) if r is None else within(r, 0, "moe_tile", "pick", b, e)))
                        for i in range(4):
                            k = 4 * b + i
                            run(xg[:, k, :], psum[2 + b][:, i * CAP:(i + 1) * CAP], ACT.Identity,
                                *(("moe_act", "xg", e) if k == KD - 1 else ("moe_act", "xg", k, e)),
                                scale=scale_col[:, 1, k:k + 1], bias=mod_col[:, 1, 24 + k:25 + k])

                def body(e, r):
                    now = (lambda *ev: until(*ev, e)) if r is None else (lambda *ev: within(r, 0, *ev, e))
                    for g in range(GROUPS):
                        act.wait_ge(*now("moe_tile", "up", g))
                        if g >= 2:
                            act.wait_ge(*now("moe_vec", "h", g - 2))
                        elif r is not None:
                            act.wait_ge(*within(r, 1, "moe_vec", "h", GROUPS - 2 + g, e))
                        run(moe_s[:, g % 2].rearrange("p i n -> p (i n)"), psum[g % 2][:, 0:2 * CAP], ACT.Silu, "moe_act", "silu", g, e)
                        if g == 1:
                            act.wait_ge(*now("moe_tile", "spread"))
                            run(spread, psum[2][:, 0:S], ACT.Copy, "moe_act", "spread", e)
                    picked(e, r)
                    act.wait_ge(*now("moe_used", "down", GROUPS - 1))
                    for c in range(2):
                        run(moe_y[:, c * 512:(c + 1) * 512], psum[4 + c], ACT.Copy, *(("moe_act", "y", e) if c else ("moe_act", "y0", e)))

                picked("start", None)
                body("first", None)
                act.wait_ge(*until("turns"))
                n = act.value_load(turns[0:1, 0:1], min_val=NE - 1, max_val=TURNS - 1)
                done.begin()
                with act.Fori(0, n) as r:
                    body("loop", r)
                done.end("moe_act")

            for name, t_ in (("ident", ident), ("parity", parity), ("causal", causal.rearrange("p t s -> p (t s)")),
                             ("rope_cos", cos.rearrange("p t f -> p (t f)")), ("rope_sin", sin.rearrange("p t f -> p (t f)")),
                             ("levels", xn[:, 0, :]), ("before", before.rearrange("p a b -> p (a b)"))):
                act.dma_start(t_, A["const_" + name]).then_inc(*done.dma("const_dma", name))
            act.dma_start(x, A["x"][0].rearrange("(t p) d -> p t d", p=P)).then_inc(*done.dma("x_loaded"))
            n_rows = 0
            act.wait_ge(*until("prow_zero"))
            act.dma_start(crow[0:KD, :], A["c"][0].rearrange("(k p) -> k p", p=P)).then_inc(*done.dma("c_rows", 0))
            act.dma_start(crow[32:32 + KD, :], A["c_2"][0].rearrange("(k p) -> k p", p=P)).then_inc(*done.dma("c_rows", 1))
            for l in range(LAYERS):
                for name, r in (PROW if l < 2 else PROW2).items():
                    a = A[name][l % 2]
                    if name == "s5_log_dt_2":
                        load(dt_row[r:r + 16, l - 2, :], a.rearrange("(j g) -> j g", g=2), f"dt_loaded{l}")
                        continue
                    elif name == "w_conv":
                        src = a.rearrange("w (c p) -> (w c) p", p=P)
                    elif len(a.shape) == 2:
                        src = a.rearrange("(j g) p -> j (g p)", g=2)
                    else:
                        src = a.rearrange("(r p) -> r p", p=P)
                    n = src.shape[0]
                    at = 0
                    while at < n:
                        row = r + at
                        b = 2 * l + row // P if l < 2 else 4 + l - 2
                        take = min(n - at, P - row % P)
                        dst = prow[row % P:row % P + take, b, :]
                        act.dma_start(dst, src[at:at + take]).then_inc(*done.dma("param_dma", l, name, at))
                        n_rows += 1
                        last_param = ("param_dma", l, name, at)
                        at += take
            load_gate_bias(0)
            act.wait_ge(*until("const_dma", "before"))
            run(stat[:, 62:63], ident[:, 0:1], ACT.Copy, "const", "ident")
            act.wait_ge(*until(*last_param))
            act.wait_ge(*until("c_rows", 1))
            run(stat[:, 61:62], ident[:, 0:1], ACT.Copy, "param_rows")
            for b in range(2):
                p_ = tile("param", b)
                n = 512 if b == 0 else 256
                run(pcol[:, 4 * b:4 * b + n // P, :].rearrange("p n c -> p (n c)"), p_[:, 0:n], ACT.Copy, "pcol", b)
            p_ = tile("cT")
            run(c_act.rearrange("p b k -> p (b k)")[:, 0:KD], p_[:, 0:KD], ACT.Silu, "act_chain", "silu_c")
            run(c_act.rearrange("p b k -> p (b k)")[:, KD:2 * KD], p_[:, 32:32 + KD], ACT.Silu, "c_raw")
            for l in (2, 3):
                act.wait_ge(*done.prev())
                run(s5t[:, l - 2, :], col(l, "s5_log_dt_2", 16), ACT.Exp, "s5_dt", l)
            for l in (2, 3):
                act.wait_ge(*until("s5_angle", l))
                run(s5p[:, l - 2, 0, :], s5t[:, 2, :], ACT.Exp, "s5_exp", l)
                run(s5p[:, l - 2, 2, :], s5t[:, 4, :], ACT.Sin, "act_chain", l, "s5sin")
                run(s5t[:, 5, :], s5t[:, 4, :], ACT.Sin, "s5_sin", l, scale=0.5)
            for l in range(LAYERS):
                load_rows(l, "mix")
                if l < 2:
                    mixer_one(l)
                    post_squares(l, "mix")
                else:
                    mixer_two(l)
                load_rows(l, "ffn")
                if l < 3:
                    load_gate_bias(l + 1)
                if l < 2:
                    squares(l, "ffn")
                if 1 <= l < 3:
                    act.wait_ge(*until("post", l, "mix", 3))
                    n = l + 1
                    for r, name in enumerate(("re", "im")):
                        b5 = A[f"s5_b_{name}_2"][n - 2].rearrange("g p h -> (g p) h").rearrange("(j q) h -> q j h", q=P)
                        c5 = A[f"s5_c_{name}_2"][n - 2].rearrange("g h p -> (g h) p").rearrange("(c q) p -> q c p", q=P)
                        for i in range(2):
                            load(Bnat[:, r, :, 16 * i:16 * i + 16], b5, f"s5_load{n}", r, i, 0)
                            load(Cnat[:, r, :, HD * i:HD * i + HD], c5, f"s5_load{n}", r, i, 1)
                    load(w_alpha[0:16, :], A["gla_w_alpha_up_2"][n - 2], "w_alpha", n)
                if l == 0:
                    load(router, A["moe_w_router_2"][0].rearrange("(k p) e -> p k e", p=P), "router_loaded")
                    load(router_b[0:1, :], A["moe_b_router_2"][0:1, :], "router_b_loaded")
                norm_out(l, "ffn")
                if l == 3:
                    load(earlier, A["const_earlier"], "const_moe", 0)
                    load(iota, A["const_iota"], "const_moe", 1)
                    act.wait_ge(*until("moe_shift"))
                    run(moe[:, 7], moe[:, 6], ACT.Exp, "moe_exp")
                    mixture()
                    continue
                for e in range(1):
                    for f in range(FF[l] // P):
                        n = e * (FF[l] // P) + f
                        if n >= 2:
                            act.wait_ge(*until("up_out", l, *divmod(n - 2, FF[l] // P)))
                        if l < 2:
                            act.wait_ge(*until("conv", l, f))
                            run(ffn_tmp[:, 2 + n % 2, :], ffn_tmp[:, n % 2, :], ACT.Gelu_apprx_tanh, "up_act", l, e, f)
                        else:
                            p_ = tile("up", l, e, f)
                            run(ffn_tmp[:, 2 + n % 2, :], p_[:, 0:S], ACT.Silu, "up_act", l, e, f)
                if l < 2:
                    post_squares(l, "ffn")

        @block.vector
        def _(dve):
            done = sig_dve
            v = nc.vector

            def tile(*key):
                dve.wait_ge(*until("pe_tile", *key))
                return psum[bank_of[key]]

            def after():
                dve.wait_ge(*done.prev())

            chain = [0]

            def link():
                chain[0] += 1
                return done("dve_chain", chain[0])

            def mod_sum(l, q):
                key = ("ada", l, q)
                dve.wait_ge(*loaded(key))
                if q >= 4:
                    dve.wait_ge(*until("pe_tile", "mod", l, q - 4))
                w, acc, ca = chunk(key), mod_acc[:, q % 4, :], c_act[:, l // 2, :]
                v.tensor_scalar(acc, w[:, 0, :], ca[:, 0:1], None, ALU.mult).then_inc(*link())
                for k in range(1, KD):
                    after()
                    v.scalar_tensor_tensor(acc, w[:, k, :], ca[:, k:k + 1], acc, ALU.mult, ALU.add)\
                        .then_inc(*(done("mod_sum", l, q) if k == KD - 1 else link()))

            def mod_out(l, q):
                p_ = tile("mod", l, q)
                m, c = q // 4, q % 4
                if m in (2, 5):
                    dve.wait_ge(*until(f"gate_bias_{'mix' if m == 2 else 'ffn'}{l}"))
                    dst = mod_gate[:, 0 if m == 2 else 1 + l % 2, c * CW:(c + 1) * CW]
                    v.tensor_tensor(dst, p_[:, 0:CW], dst, ALU.add).then_inc(*done("mod_out", l, q))
                else:
                    at = 8 * m + 2 * c
                    v.tensor_tensor(mod_col[:, l % 2, at:at + 2], p_[:, 0:2], col(l, "b_ada" if l < 2 else "mod_b_2", 2, at),
                                    ALU.add).then_inc(*done("mod_out", l, q))

            def rstd(dst, src, scale, eps, *key):
                v.tensor_scalar(dst, src, scale, eps, ALU.mult, ALU.add).then_inc(*done("variance", *key))
                dve.wait_ge(*until("rstd", *key))

            def scales(l, stage):
                b0 = 24 * (stage == "ffn")
                s = mod_col[:, l % 2, b0 + 8:b0 + 16]
                dst = scale_col[:, int(stage == "ffn"), :]
                after()
                if l < 2:
                    v.scalar_tensor_tensor(dst, s, 1.0, col(l, "g_pre_" + stage, 8), ALU.add, ALU.mult).then_inc(*done("scales", l, stage))
                else:
                    v.tensor_scalar(dst, s, 1.0, None, ALU.add).then_inc(*done("scales", l, stage))

            def norm(l, stage):
                if l < 2:
                    st = 2 * (stage == "ffn")
                    dve.wait_ge(*until("ssq", l, stage, 1))
                    rstd(stat[:, 32:34], stat[:, st:st + 2], 1.0 / D, 1e-6, l, "norm", stage)
                    for t in range(NT):
                        v.tensor_scalar(xn[:, t, :], x[:, t, :], stat[:, 32 + t:33 + t], None, ALU.mult)\
                            .then_inc(*(done("xn", l, stage) if t else link()))
                after()
                b0 = 24 * (stage == "ffn")
                for b in (1, 3):
                    p_ = tile("norm", l, stage, b)
                    for i in range(2):
                        k = 2 * b + i
                        v.tensor_scalar(hT[:, k, :], p_[:, i * S:(i + 1) * S], scale_col[:, int(stage == "ffn"), k:k + 1],
                                        mod_col[:, l % 2, b0 + k:b0 + k + 1], ALU.mult, ALU.add)\
                            .then_inc(*(done("hTd", l, stage, b) if i else link()))

            def rope(l, c0, heads, *event):
                a = proj[:, :, c0:c0 + heads * HD].rearrange("p t (h d) -> p t h d", d=HD)
                x1, x2 = a[:, :, :, 0:8], a[:, :, :, 8:16]
                for t in range(NT):
                    y1, y2 = x1[:, t], x2[:, t]
                    c = cos[:, t].unsqueeze(1).broadcast_to([P, heads, 8])
                    s = sin[:, t].unsqueeze(1).broadcast_to([P, heads, 8])
                    ta, tb, tc, td = (rope_t[:, i, t, 0:heads, :] for i in range(4))
                    v.tensor_tensor(ta, y1, c, ALU.mult).then_inc(*link())
                    v.tensor_tensor(tb, y2, s, ALU.mult).then_inc(*link())
                    v.tensor_tensor(tc, y2, c, ALU.mult).then_inc(*link())
                    v.tensor_tensor(td, y1, s, ALU.mult).then_inc(*link())
                    after()
                    v.tensor_tensor(y1, ta, tb, ALU.subtract).then_inc(*link())
                    v.tensor_tensor(y2, tc, td, ALU.add).then_inc(*(done(*event) if t else link()))

            def indexer_sum(l):
                order = 0
                for t in range(NT):
                    kn = (t + 1) * P
                    acc = idx_acc[:, t, 0:kn]
                    first = True
                    for n in range(4 if t else 2):
                        dve.wait_ge(*until("idx_relu", l, t, n))
                        heads = unit_heads(t, n)
                        for i, h in enumerate(heads):
                            r = idx_r[:, order % 2, i * kn:(i + 1) * kn]
                            last = i == len(heads) - 1
                            ev = done("idx_sum", l, order) if last else link()
                            if first:
                                v.tensor_scalar(acc, r, w_idx[:, t, h:h + 1], None, ALU.mult).then_inc(*ev)
                            else:
                                v.scalar_tensor_tensor(acc, r, w_idx[:, t, h:h + 1], acc, ALU.mult, ALU.add).then_inc(*ev)
                            after()
                            first = False
                        order += 1
                    v.tensor_tensor(idx_work[:, t, 0:kn], acc, causal[:, t, 0:kn], ALU.add).then_inc(*link())

            def top_keys(l):
                for r in range(TOPK // 8):
                    for t in range(NT):
                        kn = (t + 1) * P
                        after()
                        v.max(top8[:, t, :], idx_work[:, t, 0:kn]).then_inc(*link())
                        after()
                        v.match_replace(idx_work[:, t, 0:kn], top8[:, t, :], idx_work[:, t, 0:kn], LOWEST).then_inc(*link())
                for t in range(NT):
                    kn = (t + 1) * P
                    after()
                    v.tensor_scalar(dsa_mask[:, t, 0:kn], idx_work[:, t, 0:kn], -2e38, NEG, ALU.is_gt, ALU.mult).then_inc(*link())
                    after()
                    v.tensor_tensor(dsa_mask[:, t, 0:kn], dsa_mask[:, t, 0:kn], causal[:, t, 0:kn], ALU.min).then_inc(*link())

            def attention(l):
                n_units = len(UNITS1)
                for u in range(n_units + 2):
                    if u < n_units:
                        g, t, n = UNITS1[u]
                        kn, nh = (t + 1) * P, 2 if t else 4
                        p_ = tile("sc", l, u)
                        if u >= 2:
                            dve.wait_ge(*until("att_exp", l, u - 2))
                        s = att_s[:, u % 2, :].rearrange("p (h k) -> p h k", h=nh)
                        mask = (dsa_mask if g else causal)[:, t, 0:kn].unsqueeze(1).broadcast_to([P, nh, kn])
                        v.tensor_tensor(s, p_.rearrange("p (h k) -> p h k", h=nh), mask, ALU.add).then_inc(*done("att_mask", l, u))
                        after()
                        v.tensor_reduce(att_nm[:, u, 0:nh], s, AX.X, ALU.max, negate=True).then_inc(*done("att_max", l, u))
                    if 1 <= u <= n_units:
                        p_ = tile("pT", l, u - 1)
                        if u >= 3:
                            dve.wait_ge(*until("pe_tile", "pv", l, u - 3))
                        v.tensor_copy(att_pT[:, (u - 1) % 2, :], p_).then_inc(*done("att_pT", l, u - 1))
                    if u >= 2:
                        g, t, n = UNITS1[u - 2]
                        if n == (3 if t else 1):
                            dve.wait_ge(*until("pe_tile", "pv", l, u - 2))
                            v.reciprocal(att_ri[:, g, t, :], att_rs[:, g, t, :]).then_inc(*link())
                            after()
                            o = psum[bank_of["o", l, g, t]].rearrange("p (h d) -> p h d", d=HD)
                            v.tensor_tensor(xn[:, t, g * 512:(g + 1) * 512].rearrange("p (h d) -> p h d", d=HD), o,
                                            att_ri[:, g, t, :].unsqueeze(2).broadcast_to([P, NH, HD]), ALU.mult)\
                                .then_inc(*done("att_o", l, g, t))
                dve.wait_ge(*until("o_ssq", l, 1, 1))
                rstd(stat[:, 36:40], stat[:, 16:20], 1.0 / 512, 1e-6, l, "o")
                for g in range(2):
                    for t in range(NT):
                        o = xn[:, t, g * 512:(g + 1) * 512]
                        v.tensor_scalar(o, o, stat[:, 36 + 2 * g + t:37 + 2 * g + t], None, ALU.mult).then_inc(*done("att_on", l, g, t))

            def post(l, stage):
                gate = mod_gate[:, 0 if stage == "mix" else 1 + l % 2, :]
                dve.wait_ge(*until(f"rows_{stage}{l}", 0 if l < 2 else 1))
                y_done = ("pe_used", "out", l, 3) if stage == "mix" else ("pe_used", "down", l, 0, ffn_groups(l) - 1)
                if l < 2:
                    after()
                    v.tensor_tensor(gate, gate, rows[:, 0, :], ALU.mult).then_inc(*link())
                    dve.wait_ge(*until("y_ssq", l, stage, 3))
                    v.tensor_reduce(stat[:, 40:42], stat[:, 8:12].rearrange("p (t c) -> p t c", c=2), AX.X, ALU.add).then_inc(*link())
                    after()
                    rstd(stat[:, 42:44], stat[:, 40:42], 1.0 / D, 1e-6, l, "post", stage)
                    for i in range(4):
                        t, c = i // 2, i % 2
                        sl = slice(c * 512, (c + 1) * 512)
                        y = psum[bank_of["y", l, stage, i]]
                        v.scalar_tensor_tensor(xn[:, t, sl], y, stat[:, 42 + t:43 + t], gate[:, sl], ALU.mult, ALU.mult)\
                            .then_inc(*done("post", l, stage, i))
                    for t in range(NT):
                        after()
                        v.tensor_tensor(x[:, t, :], x[:, t, :], xn[:, t, :], ALU.add)\
                            .then_inc(*done(*(("x_new", l, stage) if t else ("x_new_t", l, stage, 0))))
                    return
                experts = (l, stage) == (3, "ffn")
                dve.wait_ge(*(done.prev() if experts else until(*y_done)))
                for i in range(4):
                    t, c = i // 2, i % 2
                    sl = slice(c * 512, (c + 1) * 512)
                    y = xn[:, t, sl] if experts else psum[bank_of["y", l, stage, i]]
                    v.scalar_tensor_tensor(xn[:, t, sl], gate[:, sl], 1.0, y, ALU.add, ALU.mult).then_inc(*done("post", l, stage, i))
                for t in range(NT):
                    after()
                    v.scalar_tensor_tensor(x[:, t, :], x[:, t, :], ALPHA, xn[:, t, :], ALU.mult, ALU.add).then_inc(*link())
                    after()
                    for c in range(2):
                        v.bn_stats(stat[:, 44 + 6 * c:50 + 6 * c], x[:, t, c * 512:(c + 1) * 512]).then_inc(*link())
                    after()
                    v.bn_aggr(stat[:, 56:58], stat[:, 44:56]).then_inc(*link())
                    after()
                    rstd(stat[:, 58:59], stat[:, 57:58], 1.0, 1e-5, l, "post", stage, t)
                    v.tensor_scalar(xn[:, t, :], x[:, t, :], stat[:, 56:57], stat[:, 58:59], ALU.subtract, ALU.mult).then_inc(*link())
                    after()
                    v.tensor_tensor(xn[:, t, :], xn[:, t, :], rows[:, 0, :], ALU.mult).then_inc(*link())
                    after()
                    v.tensor_tensor(x[:, t, :], xn[:, t, :], rows[:, 1, :], ALU.add)\
                        .then_inc(*done(*(("x_new", l, stage) if t else ("x_new_t", l, stage, 0))))

            def mixture():
                sel, cb = moe[:, 8], moe[:, 9]
                v.memset(place, -1.0).then_inc(*link())
                v.memset(weight, 0.0).then_inc(*link())
                v.memset(xn, 0.0).then_inc(*link())
                p_ = tile("places")
                after()
                pl = p_[:, 0:NT * NE].rearrange("p (t e) -> p t e", t=NT)
                v.scalar_tensor_tensor(place[:, :, 0:NE], pl, 1.0, sel, ALU.add, ALU.mult).then_inc(*link())
                over, rank, hot, mine = moe[:, 4, 0, :], moe[:, 5, 0, :], moe[:, 10], moe[:, 11]
                v.tensor_scalar(over, p_[:, 2 * NE:3 * NE], CAP + 0.5, None, ALU.is_gt).then_inc(*link())
                after()
                v.tensor_scalar(place[:, :, 0:NE], place[:, :, 0:NE], -1.0, None, ALU.add).then_inc(*link())
                v.tensor_tensor_scan(rank, ones[:, 0:1].broadcast_to([P, NE]), over, 0.0, ALU.mult, ALU.add).then_inc(*link())
                v.tensor_copy(weight[:, :, 0:NE], cb).then_inc(*link())
                after()
                v.memset(stat[:, 60:61], 0.0).then_inc(*done("placed"))
                dve.wait_ge(*until("const_moe", 1))
                v.tensor_copy(turns[:, 1:NE], iota[:, 1:NE]).then_inc(*link())
                for j in range(EXTRA):
                    is_jth = hot[:, 0, :]
                    after()
                    v.scalar_tensor_tensor(is_jth, rank, float(j + 1), over, ALU.is_equal, ALU.mult).then_inc(*link())
                    after()
                    v.tensor_tensor(hot[:, 1, :], is_jth, iota[:, 0:NE], ALU.mult).then_inc(*link())
                    after()
                    v.tensor_reduce(stat[:, 48:49], hot[:, 1, :], AX.X, ALU.add).then_inc(*link())
                    after()
                    v.tensor_copy(turns[:, NE + j:NE + j + 1], stat[:, 48:49]).then_inc(*link())
                    for what in (place, weight):
                        after()
                        v.tensor_tensor(mine, what[:, :, 0:NE], is_jth.unsqueeze(1).broadcast_to([P, NT, NE]), ALU.mult).then_inc(*link())
                        after()
                        v.tensor_reduce(what[:, :, NE + j], mine, AX.X, ALU.add).then_inc(*link())
                after()
                v.tensor_scalar(place[:, :, NE:TURNS], place[:, :, NE:TURNS], float(-CAP), None, ALU.add).then_inc(*link())
                after()
                v.tensor_scalar(turns[:, 0:1], rank[:, NE - 1:NE], NE - 1.0, None, ALU.add).then_inc(*done("turns"))

                def picks(e, at):
                    for t in range(NT):
                        v.tensor_scalar(pick[:, t, :], iota, place[:, t, at], None, ALU.is_equal).then_inc(*done("moe_vec", "p", t, e))
                        v.tensor_scalar(pick_w[:, t, :], iota, place[:, t, at], weight[:, t, at], ALU.is_equal, ALU.mult)\
                            .then_inc(*(done("moe_vec", "pick", e) if t else done("moe_vec", "w", t, e)))

                def add_z(name, e, i, *wait):
                    t, c = i // 2, i % 2
                    dve.wait_ge(*wait)
                    o = xn[:, t, c * 512:(c + 1) * 512]
                    v.tensor_tensor(o, psum[6 + i % 2], o, ALU.add).then_inc(*done(name, "z", i, *e))

                def body(e, r):
                    now = (lambda *ev: until(*ev, e)) if r is None else (lambda *ev: within(r, 0, *ev, e))
                    for g in range(GROUPS):
                        dve.wait_ge(*now("moe_act", "silu", g))
                        v.tensor_tensor(moe_h[:, g % 2].rearrange("p i n -> p (i n)"), psum[g % 2][:, 2 * CAP:4 * CAP],
                                        moe_s[:, g % 2].rearrange("p i n -> p (i n)"), ALU.mult).then_inc(*done("moe_vec", "h", g, e))
                        if g == 1 and r is not None:
                            for i in range(4):
                                add_z("moe_vec", (e,), i, *now("moe_tile", "z", i))
                        if g == 4:
                            dve.wait_ge(*now("moe_tile", "spread"))
                            picks(e, slice(1, 2) if r is None else bass.ds(r + 2, 1))

                picks("start", slice(0, 1))
                body("first", None)
                n = dve.value_load(turns[0:1, 0:1], min_val=NE - 1, max_val=TURNS - 1)
                done.begin()
                with dve.Fori(0, n) as r:
                    body("loop", r)
                done.end("moe_vec")
                for i in range(4):
                    add_z("moe_last", (), i, *until("moe_tail", "z", i, "tail"))

            def ffn(l):
                pending = []
                for e in range(1):
                    for f in range(FF[l] // P):
                        n = e * (FF[l] // P) + f
                        p_ = tile("up", l, e, f)
                        if l < 2:
                            a, u = ffn_tmp[:, n % 2, :], p_[:, 0:S]
                            w = [col(l, "w_conv", 1, 22 * i + f) for i in range(3)]
                            if n >= 2:
                                dve.wait_ge(*until("up_act", l, e, f - 2))
                            v.tensor_scalar(a, u, w[2], col(l, "b_conv", 1, f), ALU.mult, ALU.add).then_inc(*link())
                            after()
                            v.scalar_tensor_tensor(a[:, 1:S], u[:, 0:S - 1], w[1], a[:, 1:S], ALU.mult, ALU.add).then_inc(*link())
                            after()
                            v.scalar_tensor_tensor(a[:, 2:S], u[:, 0:S - 2], w[0], a[:, 2:S], ALU.mult, ALU.add).then_inc(*done("conv", l, f))
                        dve.wait_ge(*until("up_act", l, e, f))
                        g = ffn_tmp[:, 2 + n % 2, :]
                        v.tensor_tensor(hf[:, f % 4, :], g, p_[:, S:2 * S], ALU.mult).then_inc(*done("up_out", l, e, f))
                        if f % 2 == 1:
                            for q in ada_in_ffn(l, f // 2):
                                mod_sum(l + 1, q)
                                if pending:
                                    mod_out(l + 1, pending.pop(0))
                                pending.append(q)
                for q in pending:
                    mod_out(l + 1, q)

            def s5_params(l):
                dt, lre, lim = s5t[:, l - 2, :], col(l, "s5_lam_re_2", 16), col(l, "s5_lam_im_2", 16)
                X, Y, TH, SH, T, U, FR, FI, M = (s5t[:, i, :] for i in (2, 3, 4, 5, 6, 7, 8, 9, 10))
                R, CO, SI, fr, fi = (s5p[:, l - 2, i, :] for i in range(5))

                def ts(o, i, a, b, f, g=None):
                    after()
                    (v.tensor_scalar(o, i, a, b, f, g) if g is not None else v.tensor_scalar(o, i, a, b, f)).then_inc(*link())

                def tt(o, a, b, f):
                    after()
                    v.tensor_tensor(o, a, b, f).then_inc(*link())

                dve.wait_ge(*until("s5_dt", l))
                if l == 3:
                    dve.wait_ge(*until("s5_sin", 2))
                v.tensor_tensor(X, lre, dt, ALU.mult).then_inc(*link())
                tt(Y, lim, dt, ALU.mult)
                ts(T, Y, 1.0 / (2 * math.pi), 12582912.0, ALU.mult, ALU.add)
                ts(T, T, 12582912.0, None, ALU.subtract)
                c1_, c2_ = 6.28125, float(np.float32(2 * math.pi - 6.28125))
                c3_ = float(2 * math.pi - 6.28125 - c2_)
                after()
                v.scalar_tensor_tensor(TH, T, -c1_, Y, ALU.mult, ALU.add).then_inc(*link())
                after()
                v.scalar_tensor_tensor(TH, T, -c2_, TH, ALU.mult, ALU.add).then_inc(*link())
                after()
                v.scalar_tensor_tensor(TH, T, -c3_, TH, ALU.mult, ALU.add).then_inc(*link())
                pi = 3.1415925
                after()
                v.tensor_scalar(TH, TH, pi, -pi, ALU.min, ALU.max).then_inc(*done("s5_angle", l))
                ts(U, X, -0.5, 0.5, ALU.max, ALU.min)
                ts(T, U, 1.0 / 9, 1.0, ALU.mult, ALU.add)
                for n in range(8, 1, -1):
                    tt(T, T, U, ALU.mult)
                    ts(T, T, 1.0 / n, 1.0, ALU.mult, ALU.add)
                tt(T, T, U, ALU.mult)
                dve.wait_ge(*until("s5_sin", l))
                ts(M, X, U, None, ALU.is_equal) if False else tt(M, X, U, ALU.is_equal)
                ts(U, R, -1.0, None, ALU.add)
                tt(T, T, U, ALU.subtract)
                tt(T, T, M, ALU.mult)
                tt(T, T, U, ALU.add)
                tt(SH, SH, SH, ALU.mult)
                ts(SH, SH, -2.0, None, ALU.mult)
                ts(CO, SH, 1.0, None, ALU.add)
                tt(FR, T, CO, ALU.mult)
                tt(FR, FR, SH, ALU.add)
                tt(FI, R, SI, ALU.mult)
                tt(T, lre, lre, ALU.mult)
                tt(U, lim, lim, ALU.mult)
                tt(T, T, U, ALU.add)
                after()
                v.reciprocal(M, T).then_inc(*link())
                tt(fr, FR, lre, ALU.mult)
                tt(T, FI, lim, ALU.mult)
                tt(fr, fr, T, ALU.add)
                tt(fr, fr, M, ALU.mult)
                tt(fi, FI, lre, ALU.mult)
                tt(T, FR, lim, ALU.mult)
                tt(fi, fi, T, ALU.subtract)
                after()
                v.tensor_tensor(fi, fi, M, ALU.mult).then_inc(*(done("s5_params") if l == 3 else link()))

            def s5(l):
                dve.wait_ge(*until(f"s5_load{l}", 1, 1, 1))
                mask = parity.unsqueeze(1).broadcast_to([P, 4, P])
                for r in range(2):
                    b = Bnat[:, r].rearrange("p (c j) n -> p c (j n)", c=4)
                    v.tensor_tensor(b, b, mask, ALU.mult).then_inc(*(done("b_masked", l) if r else link()))
                for r in range(2):
                    p_ = tile("CT", l, r).rearrange("p (c n) -> p c n", c=4)
                    v.tensor_tensor(Cmask[:, r], p_, mask, ALU.mult).then_inc(*done("c_masked", l, r))
                fr, fi = (s5p[:, l - 2, i, :].unsqueeze(2).broadcast_to([P, 16, 32]) for i in (3, 4))
                cr, ci, o0, o1, tmp = (a.rearrange("p c (j n) -> p (c j) n", n=32) for a in
                                       (Cmask[:, 0], Cmask[:, 1], Cst[:, 0], Cst[:, 1], Cnat[:, 0]))
                after()
                v.tensor_tensor(o0, cr, fr, ALU.mult).then_inc(*link())
                v.tensor_tensor(tmp, ci, fi, ALU.mult).then_inc(*link())
                after()
                v.tensor_tensor(o0, o0, tmp, ALU.subtract).then_inc(*link())
                after()
                v.tensor_tensor(o1, cr, fi, ALU.mult).then_inc(*link())
                v.tensor_tensor(tmp, ci, fr, ALU.mult).then_inc(*link())
                after()
                v.scalar_tensor_tensor(o1, o1, -1.0, tmp, ALU.mult, ALU.subtract).then_inc(*done("cst", l))
                p_ = tile("lg", l)
                for c in range(2):
                    v.tensor_scalar(gb[:, c, :], p_[:, c * S:(c + 1) * S], col(l, "gla_b_alpha_2", 1, c), None, ALU.add)\
                        .then_inc(*(done("gla_z", l) if c else link()))
                dve.wait_ge(*until("tables", l))
                after()
                for u in range(8):
                    qq, i = u // 4, u % 4
                    c, s = eC[:, 8 * qq + i:8 * qq + i + 5:4, :], eS[:, 8 * qq + i:8 * qq + i + 5:4, :]
                    re = tile("bu", l, u, 0).rearrange("p (j s) -> p j s", j=2)
                    im = tile("bu", l, u, 1).rearrange("p (j s) -> p j s", j=2)
                    v.tensor_tensor(w5[:, 0], c, re, ALU.mult).then_inc(*link())
                    v.tensor_tensor(t5[:, 0], s, im, ALU.mult).then_inc(*link())
                    v.tensor_tensor(w5[:, 1], c, im, ALU.mult).then_inc(*link())
                    v.tensor_tensor(t5[:, 1], s, re, ALU.mult).then_inc(*done("s5_w", l, u))
                    after()
                    v.tensor_tensor(w5[:, 0], w5[:, 0], t5[:, 0], ALU.add).then_inc(*link())
                    v.tensor_tensor(w5[:, 1], w5[:, 1], t5[:, 1], ALU.subtract).then_inc(*link())
                    after()
                    if u >= 2:
                        dve.wait_ge(*until("s5_h", l, u - 2))
                    for r in range(2):
                        for jj in range(2):
                            j = 8 * qq + i + 4 * jj
                            v.tensor_tensor_scan(g5[:, u % 2, r, jj, :], s5p[:, l - 2, 0, j:j + 1].broadcast_to([P, S]),
                                                 w5[:, r, jj, :], 0.0, ALU.mult, ALU.add)\
                                .then_inc(*(done("s5_g", l, u) if r and jj else link()))
                    after()
                for qq in range(2):
                    dve.wait_ge(*until("pe_tile", "s5o", l, 4 * qq + 3))
                    y = psum[bank_of["s5y", l, qq]]
                    for i in range(2):
                        c = 2 * qq + i
                        v.scalar_tensor_tensor(uT[:, c, :], uT[:, c, :], col(l, "s5_d_2", 1, c), y[:, i * S:(i + 1) * S],
                                               ALU.mult, ALU.add).then_inc(*(done("s5_y", l, qq) if i else link()))

            def gla(l):
                v.scalar_tensor_tensor(gz[:, 1], gb, -1.0, gb, ALU.mult, ALU.min).then_inc(*done("gla_abs", l))
                dve.wait_ge(*until("gla_ln", l))
                v.scalar_tensor_tensor(gz[:, 0], gb, 0.0, gz[:, 1], ALU.min, ALU.subtract).then_inc(*link())
                after()
                v.tensor_scalar(gz[:, 0], gz[:, 0], 1.0 / 16, None, ALU.mult).then_inc(*link())
                after()
                for c in range(2):
                    v.tensor_tensor_scan(gb[:, c, :], ones[:, 0:1].broadcast_to([P, S]), gz[:, 0, c, :], 0.0, ALU.mult, ALU.add)\
                        .then_inc(*link())
                after()
                dve.wait_ge(*until("gla_zero", l, 2))
                dve.wait_ge(*until("in_out", l, 3))
                b2, q2, k2 = (a.rearrange("p c s -> p (c s)") for a in (gb, gqT, gkT))
                halves = [P] + LEVELS[:-1]
                view = lambda a, h: a.rearrange("p (n w) -> p n w", w=2 * h)

                def factors(m):
                    h = halves[m]
                    d, b = view(gD[:, m % 2, :], h), view(b2, h)
                    mid = b[:, :, h - 1:h].broadcast_to([P, 512 // (2 * h), h])
                    after()
                    v.tensor_tensor(d[:, :, 0:h], mid, b[:, :, 0:h], ALU.subtract).then_inc(*link())
                    v.tensor_tensor(d[:, :, h:2 * h], b[:, :, h:2 * h], mid, ALU.subtract).then_inc(*done("gla_d", l, h))

                def products(m):
                    h = halves[m]
                    dve.wait_ge(*until("gla_e", l, h))
                    if m >= 2:
                        dve.wait_ge(*until("pe_tile", "off", l, 1) if m == 2 else until("pe_tile", "lv", l, m - 3, 1))
                    d = view(gD[:, m % 2, :], h)
                    v.tensor_tensor(view(gQ[:, m % 2, :], h)[:, :, h:2 * h], view(q2, h)[:, :, h:2 * h], d[:, :, h:2 * h], ALU.mult).then_inc(*link())
                    v.tensor_tensor(view(gK[:, m % 2, :], h)[:, :, 0:h], view(k2, h)[:, :, 0:h], d[:, :, 0:h], ALU.mult).then_inc(*done("gla_k", l, h))

                def collect(n):
                    for par in range(2):
                        p_ = tile("lv", l, n, par)
                        after()
                        v.copy_predicated(scT[:, par].rearrange("p j c i -> p (j c) i"),
                                          levels[:, n, :].unsqueeze(1).broadcast_to([P, 4, P]),
                                          p_.rearrange("p (a i) -> p a i", a=4)).then_inc(*done("lv_out", l, n, par))

                factors(0)
                for m in range(len(halves)):
                    if m + 1 < len(halves):
                        factors(m + 1)
                    products(m)
                    if m >= 2:
                        collect(m - 2)
                for n in range(len(halves) - 2, len(LEVELS)):
                    collect(n)
                for t in range(NT):
                    dve.wait_ge(*until("go_ssq", l, t, 3))
                    rstd(stat[:, 36:40], stat[:, 20 + 4 * t:24 + 4 * t], 1.0 / P, 1e-6, l, "gla", t)
                    if t == 0:
                        dve.wait_ge(*until("in_out", l, 7))
                    p_ = psum[bank_of["go", l, t]]
                    for h in range(4):
                        v.scalar_tensor_tensor(o_gla[:, t, h * P:(h + 1) * P], p_[:, h * P:(h + 1) * P], stat[:, 36 + h:37 + h],
                                               vg[:, t, 512 + h * P:512 + (h + 1) * P], ALU.mult, ALU.mult)\
                            .then_inc(*(done("gla_o", l, t) if h == 3 else link()))
                    after()

            def route():
                lg, m1, sh, ex, cb = moe[:, 0], moe[:, 1], moe[:, 6], moe[:, 7], moe[:, 9]
                p_ = tile("router")
                v.tensor_copy(lg, p_[:, 0:NT * NE].rearrange("p (t e) -> p t e", t=NT)).then_inc(*done("logits"))
                after()
                v.tensor_reduce(m1[:, :, 0], lg, AX.X, ALU.max).then_inc(*link())
                after()
                v.tensor_tensor(sh, lg, m1[:, :, 0:1].broadcast_to([P, NT, NE]), ALU.subtract).then_inc(*done("moe_shift"))
                for t in range(NT):
                    row = lg[:, t, :].unsqueeze(1).broadcast_to([P, NE, NE])
                    own = lg[:, t, :].unsqueeze(2).broadcast_to([P, NE, NE])
                    more, same = moe_pair[:, 0], moe_pair[:, 1]
                    v.tensor_tensor(more, row, own, ALU.is_gt).then_inc(*link())
                    v.tensor_tensor(same, row, own, ALU.is_equal).then_inc(*link())
                    after()
                    v.tensor_tensor(same, same, before, ALU.mult).then_inc(*link())
                    after()
                    v.tensor_tensor(more, more, same, ALU.add).then_inc(*link())
                    after()
                    v.tensor_reduce(moe[:, 8, t, :], more, AX.X, ALU.add).then_inc(*link())
                    after()
                after()
                v.tensor_scalar(moe[:, 8], moe[:, 8], 1.5, None, ALU.is_lt).then_inc(*done("chosen"))
                dve.wait_ge(*until("moe_exp"))
                after()
                v.tensor_tensor(cb, ex, moe[:, 8], ALU.mult).then_inc(*link())
                after()
                v.tensor_reduce(moe[:, 2, :, 0], cb, AX.X, ALU.add).then_inc(*link())
                after()
                v.reciprocal(moe[:, 3, :, 0], moe[:, 2, :, 0]).then_inc(*link())
                after()
                v.tensor_tensor(cb, cb, moe[:, 3, :, 0:1].broadcast_to([P, NT, NE]), ALU.mult).then_inc(*done("comb"))

            v.memset(prow, 0.0).then_inc(*link())
            v.memset(crow, 0.0).then_inc(*done("prow_zero"))
            for l in (2, 3):
                dve.wait_ge(*until(f"dt_loaded{l}"))
                r = PROW2["s5_log_dt_2"]
                v.tensor_copy(prow[r:r + 16, 2 + l, :].rearrange("j (g p) -> j g p", g=2),
                              dt_row[r:r + 16, l - 2, :].unsqueeze(2).broadcast_to([16, 2, HD])).then_inc(*done("dt_rows", l))
            dve.wait_ge(*until("const", "ident"))
            v.tensor_copy(levels.rearrange("p n i -> p (n i)"), xn[:, 0, :]).then_inc(*link())
            dve.wait_ge(*until("c_raw"))
            dve.wait_ge(*until("pcol", 1))
            for q in range(8):
                mod_sum(0, q)
                if q:
                    mod_out(0, q - 1)
            mod_out(0, 7)
            s5_params(2)
            s5_params(3)
            for l in range(LAYERS):
                scales(l, "mix")
                norm(l, "mix")
                if l < 2:
                    pending = []
                    for i, n in enumerate(PROJ_ORDER):
                        if l == 0:
                            for q in ([8 + i] if i < 14 else [22, 23]):
                                mod_sum(0, q)
                                if pending:
                                    mod_out(0, pending.pop(0))
                                pending.append(q)
                        if i == 2:
                            dve.wait_ge(*until("in_out", l, 14))
                            v.tensor_scalar(w_idx, proj[:, :, WI:WI + 8], float(np.float32(8 ** -0.5)), None, ALU.mult).then_inc(*link())
                            rope(l, QI, 9, "rope", l, 2)
                            after()
                            for h in range(2):
                                v.tensor_copy(kidup[:, :, HD * h:HD * h + HD], proj[:, :, KI:KI + HD])\
                                    .then_inc(*(done("kidup", l) if h else link()))
                        if i == 6:
                            dve.wait_ge(*until("in_out", l, 3))
                            rope(l, 0, 16, "rope", l, 0)
                            indexer_sum(l)
                        if i == 10:
                            dve.wait_ge(*until("in_out", l, 9))
                            rope(l, 1536, 16, "rope", l, 1)
                    for q in pending:
                        mod_out(0, q)
                    top_keys(l)
                    after()
                    attention(l)
                else:
                    s5(l)
                    for b in range(2):
                        dve.wait_ge(*until("s5_sig", l, b))
                        h2 = hT[:, 2 * b:2 * b + 2, :]
                        v.tensor_tensor(h2, h2, uT[:, 2 * b:2 * b + 2, :], ALU.mult)\
                            .then_inc(*(done("s5_done", l) if b else done("s5_wait", l)))
                    gla(l)
                post(l, "mix")
                scales(l, "ffn")
                norm(l, "ffn")
                if l == 3:
                    route()
                    mixture()
                else:
                    ffn(l)
                post(l, "ffn")

    return sig


_INS = ["x", "c", "w_ada", "b_ada", "g_pre_mix", "w_in", "g_moba_out", "g_dsa_out", "w_out", "g_post_mix", "g_pre_ffn",
        "w_up_act", "w_up_lin", "w_conv", "b_conv", "w_down", "g_post_ffn", "c_2", "mod_w_2", "mod_b_2", "w_in_2",
        "w_out_2", "s5_lam_re_2", "s5_lam_im_2", "s5_log_dt_2", "s5_b_re_2", "s5_b_im_2", "s5_c_re_2", "s5_c_im_2",
        "s5_d_2", "s5_w_glu_2", "s5_b_glu_2", "gla_w_alpha_up_2", "gla_b_alpha_2", "gla_head_gain_2", "ln_mix_g_2",
        "ln_mix_b_2", "ffn_w_gate_2", "ffn_w_up_2", "ffn_w_down_2", "moe_w_router_2", "moe_b_router_2", "moe_w_gate_2",
        "moe_w_up_2", "moe_w_down_2", "ln_ffn_g_2", "ln_ffn_b_2"]


class _Any(dict):

    def __missing__(self, key):
        return 1


def kernel(**inputs):
    import numpy as _np
    import concourse.bacc as _bacc
    from concourse import mybir as _mybir
    from concourse.bass_utils import run_bass_kernel_spmd as _run

    arrays = {f"in_{n}": _np.ascontiguousarray(inputs[n]) for n in _INS}
    arrays |= {f"in_const_{n}": a for n, a in constants().items()}
    names, known = [], _Any()
    for last in (False, True):
        nc = _bacc.Bacc("TRN2", target_bir_lowering=False, num_devices=1)
        A = {n[3:]: nc.dram_tensor(n, a.shape, _mybir.dt.from_np(a.dtype), kind="ExternalInput").ap() for n, a in arrays.items()}
        out = nc.dram_tensor("out_0", (1, S, D), F32, kind="ExternalOutput").ap()

        class Sems(dict):
            def __missing__(self, name):
                self[name] = nc.alloc_semaphore(name)
                return self[name]

        sig = program(nc, A, out, Sems(), known)
        known = dict(sig.at)
    r = _run(nc, [arrays], core_ids=[0])
    return r.results[0]["out_0"]
```

```python
import math

import numpy as np
import concourse.bass as bass
from concourse import mybir

F32 = mybir.dt.float32
F32R = mybir.dt.float32r
U8 = mybir.dt.uint8
ALU = mybir.AluOpType
ACT = mybir.ActivationFunctionType
AX = mybir.AxisListType

P = 128
D = 1024
S = 256
NT = S // P
KD = D // P
LAYERS = 4
NMOD = 6
HD = 64
NH = 8
ROPE = HD // 4
TOPK = S // 4
PROJ1 = 3 * NH * HD * 2 + 8 * 64 + 64 + 8
PROJ2 = 512 + 256 * 2 + 512 * 2 + 16
FF = (2816, 2816, 3584, 3584)
NE = 8
CW = 256
SLOTS = 7
REGION = 20224
SLOT = KD * CW
NEG = -1e30
LOWEST = -3e38
TSPAN = 32
QI, KI, WI = 3072, 3584, 3648
ALPHA = float(np.float32((2.0 * 2) ** 0.25))
PROJ_ORDER = [12, 13, 14, 0, 1, 2, 3, 6, 7, 8, 9, 4, 5, 10, 11]
LEVELS = [64, 32, 16, 8, 4, 2, 1, 0]
DVE_UNITS = (7,)
GROUPS = FF[3] // CW
CAP = P
EXTRA = 2 * S // (CAP + 1)
TURNS = NE + EXTRA
assert S <= 2 * CAP
assert 3 * GROUPS % SLOTS == 0
UNITS1 = [(g, t, n) for g in (0, 1) for t in (0, 1) for n in range(4 if t else 2)]
PROW = {"b_ada": 0, "g_pre_mix": 48, "g_moba_out": 56, "g_dsa_out": 60, "g_pre_ffn": 64,
        "w_conv": 128, "b_conv": 194}
PROW2 = {"mod_b_2": 0, "s5_lam_re_2": 48, "s5_lam_im_2": 64, "s5_d_2": 80, "s5_b_glu_2": 84,
         "gla_b_alpha_2": 88, "gla_head_gain_2": 90, "s5_log_dt_2": 96}


def s5_rotated(l, u):
    return ("s5_h_dve" if u in DVE_UNITS else "s5_h", l, u)


def unit_heads(t, n):
    return [4 * (n // 2) + n % 2, 4 * (n // 2) + n % 2 + 2] if t else [n, n + 2, n + 4, n + 6]


def constants():
    p = np.arange(P)
    pos = np.arange(S, dtype=np.float32)
    inv = np.float32(500000.0) ** (-np.arange(0, ROPE, 2, dtype=np.float32) / np.float32(ROPE))
    ang = (pos[:, None] * inv[None, :]).astype(np.float32)
    key = np.arange(S)
    query = p[:, None] + P * np.arange(NT)[None, :]
    causal = np.where(key[None, None, :] <= query[:, :, None], 0.0, NEG).astype(np.float32)
    levels = np.zeros((P, len(LEVELS), P), np.float32)
    for n, half in enumerate(LEVELS):
        j, i = p[:, None], p[None, :]
        if half:
            levels[:, n] = (j // (2 * half) == i // (2 * half)) & (j % (2 * half) < half) & (i % (2 * half) >= half)
        else:
            levels[:, n] = j == i
    fold = lambda a: np.ascontiguousarray(a.reshape(NT, P, -1).transpose(1, 0, 2)).reshape(P, -1)
    return {
        "ident": np.eye(P, dtype=np.float32),
        "causal": causal.reshape(P, NT * S),
        "rope_cos": fold(np.cos(ang).astype(np.float32)),
        "rope_sin": fold(np.sin(ang).astype(np.float32)),
        "levels": levels.reshape(P, -1),
        "parity": (p[:, None] // 64 == (p[None, :] // 16) % 2).astype(np.float32),
        "earlier": (p[:, None] < p[None, :]).astype(np.float32),
        "iota": np.broadcast_to(p[None, :].astype(np.float32), (P, CAP)).copy(),
        "before": np.broadcast_to((np.arange(NE)[None, :] < np.arange(NE)[:, None]).astype(np.float32).reshape(1, -1), (P, NE * NE)).copy(),
    }


class Signals:

    def __init__(self, sems, known):
        self.sems, self.known = sems, known
        self.count, self.at, self.owner = {}, {}, {}

    def of(self, engine):
        return Done(self, engine)

    def until(self, *event):
        return self.sems[event[0]], self.known[event]

    def within(self, r, back, *event):
        name = event[0]
        each = self.known["each", name]
        return self.sems[name], r * each + max(self.known[event] - back * each, 0)


class Done:

    def __init__(self, signals, engine):
        self.signals, self.engine, self.last = signals, engine, None

    def begin(self):
        self.before = dict(self.signals.count)

    def end(self, *names):
        for n in names:
            self.signals.at["each", n] = self.signals.count[n] - self.before.get(n, 0)

    def __call__(self, *event):
        s, name = self.signals, event[0]
        assert s.owner.setdefault(name, self.engine) == self.engine and event not in s.at, event
        s.count[name] = s.count.get(name, 0) + 1
        s.at[event] = s.count[name]
        self.last = (s.sems[name], s.count[name])
        return s.sems[name], 1

    def prev(self):
        return self.last

    def dma(self, *event):
        s, name = self.signals, event[0]
        assert event not in s.at, event
        s.count[name] = s.count.get(name, 0) + 16
        s.at[event] = s.count[name]
        return s.sems[name], 16


def ffn_chunks(l):
    chunks, n = [], ffn_groups(l)
    for g in range(n + 1):
        chunks += [("up", l, 0, g, m) for m in (0, 1) if g < n]
        chunks += [("down", l, 0, g - 1)] if g else []
    return chunks


def chunk_used(key):
    kind, l, _, g = key[:4]
    if kind == "down":
        return ("pe_used", "down", l, 0, g)
    return ("pe_tile", "up", l, 0, 2 * g + 1) if key[4] else ("pe_used", "up", l, g)


def ffn_groups(l):
    return FF[l] // CW


def ada_in_ffn(l, g):
    if l + 1 >= LAYERS:
        return []
    n, chunks = ffn_groups(l), NMOD * D // CW
    return list(range(chunks * g // n, chunks * (g + 1) // n))


def chunk_plan():
    plan = [(("ada", 0, q), ("mod_sum", 0, q)) for q in range(8)]
    for l in range(LAYERS):
        if l < 2:
            for i, n in enumerate(PROJ_ORDER):
                plan.append((("in", l, n), ("pe_tile", "in", l, n)))
                if l == 0:
                    for q in ([8 + i] if i < 14 else [22, 23]):
                        plan.append((("ada", 0, q), ("mod_sum", 0, q)))
        else:
            for n in (8, 0, 1, 2, 3, 4, 5, 6, 7):
                plan.append((("in", l, n), ("pe_tile", "in", l, n)))
            plan.append((("glu", l), ("pe_tile", "glu", l, 1)))
        for n in range(4):
            plan.append((("out", l, n), ("pe_used", "out", l, n)))
        if l == LAYERS - 1:
            break
        groups = ffn_groups(l)
        for g in range(groups):
            for m in (0, 1):
                plan.append((("up", l, 0, g, m), chunk_used(("up", l, 0, g, m))))
            for q in ada_in_ffn(l, g):
                plan.append((("ada", l + 1, q), ("mod_sum", l + 1, q)))
            if g:
                plan.append((("down", l, 0, g - 1), chunk_used(("down", l, 0, g - 1))))
        plan.append((("down", l, 0, groups - 1), chunk_used(("down", l, 0, groups - 1))))
    for e in ("first", "loop"):
        for g in range(GROUPS):
            for m in (0, 1):
                plan.append((("up", 3, e, g, m), ("moe_tile", "up", g, e)))
            if g:
                plan.append((("down", 3, e, g - 1), ("moe_used", "down", g - 1, e)))
        plan.append((("down", 3, e, GROUPS - 1), ("moe_used", "down", GROUPS - 1, e)))
    return plan


def program(nc, A, out, sems, known):
    sig = Signals(sems, known)
    until, within = sig.until, sig.within
    sb = lambda name, cols, dt=F32: nc.alloc_sbuf_tensor(name, [P, cols], dt)[:, :]
    parts = {}

    def sb_split(name, cols):
        t = sb(name, cols)
        parts[name] = nc.alloc_sbuf_tensor_at(name + "_part", [P, cols], F32R, offset=nc.sbuf_base - 4 * cols)
        return t

    def split(ap):
        return bass.AP(parts[ap.tensor.name], ap.offset, ap.ap)

    def whole(ap):
        return split(ap).bitcast(F32)

    plan = chunk_plan()
    where = {key: i for i, (key, _) in enumerate(plan)}

    x = sb("x", NT * D).rearrange("p (t d) -> p t d", t=NT)
    xn = sb_split("xn", NT * D).rearrange("p (t d) -> p t d", t=NT)
    hT = sb_split("hT", KD * S).rearrange("p (k s) -> p k s", k=KD)
    ring = sb_split("ring", SLOTS * SLOT)
    mod_gate = sb("mod_gate", 3 * D).rearrange("p (m d) -> p m d", m=3)
    mod_col = sb("mod_col", 2 * 48).rearrange("p (b c) -> p b c", b=2)
    scale_col = sb("scale_col", 2 * KD).rearrange("p (b c) -> p b c", b=2)
    mod_acc = sb("mod_acc", 4 * CW).rearrange("p (b c) -> p b c", b=4)
    rows = sb("rows", 2 * D).rearrange("p (m d) -> p m d", m=2)
    hf = sb_split("hf", 4 * S).rearrange("p (b s) -> p b s", b=4)
    ffn_tmp = sb("ffn_tmp", 4 * S).rearrange("p (b s) -> p b s", b=4)
    ident = sb("ident_sb", P)
    causal = sb("causal_sb", NT * S).rearrange("p (t s) -> p t s", t=NT)
    cos = sb("cos_sb", NT * 8).rearrange("p (t f) -> p t f", t=NT)
    sin = sb("sin_sb", NT * 8).rearrange("p (t f) -> p t f", t=NT)
    levels = sb("levels_sb", len(LEVELS) * P, U8).rearrange("p (n i) -> p n i", n=len(LEVELS))
    parity = sb("parity_sb", P)
    before = sb("before_sb", NE * NE).rearrange("p (a b) -> p a b", a=NE)
    ones = sb("ones", P)
    prow = sb_split("prow", 6 * P).rearrange("p (n c) -> p n c", n=6)
    pcol = sb("pcol", 6 * P).rearrange("p (n c) -> p n c", n=6)
    crow = sb("crow", P)
    dt_row = sb("dt_row", 4).rearrange("p (l g) -> p l g", l=2)
    c_act = sb("c_act", 2 * KD).rearrange("p (b k) -> p b k", b=2)
    s5p = sb("s5p", 2 * 5 * 16).rearrange("p (l v j) -> p l v j", l=2, v=5)
    s5t = sb("s5t", 12 * 16).rearrange("p (v j) -> p v j", v=12)
    stat = sb("stat", 64)
    minus_half = sb("minus_half", 4)
    w_alpha = sb("w_alpha", S)
    router = sb("router", KD * NE).rearrange("p (k e) -> p k e", k=KD)
    router_b = sb("router_b", NE)
    moe = sb("moe", 12 * NE * NT).rearrange("p (v t e) -> p v t e", v=12, t=NT)
    moe_pair = sb("moe_pair", 2 * NE * NE).rearrange("p (v a b) -> p v a b", v=2, a=NE)
    region = sb_split("region", REGION)

    class Carve:
        def __init__(self, at=0):
            self.at = at

        def __call__(self, pattern, **sizes):
            n = math.prod(sizes.values())
            v = region[:, self.at:self.at + n]
            self.at += n
            assert self.at <= REGION, self.at
            names = " ".join(sizes)
            return v.rearrange(f"p ({names}) -> p {names}", **dict(list(sizes.items())[:-1])) if len(sizes) > 1 else v

    c1 = Carve()
    proj = c1("", t=NT, n=PROJ1)
    qk = c1("", b=4, c=4, s=S)
    kiT = c1("", s=S)
    kidup = c1("", t=NT, n=P)
    idx_r = c1("", b=2, s=512)
    idx_acc = c1("", t=NT, s=S)
    idx_work = c1("", t=NT, s=S)
    dsa_mask = c1("", t=NT, s=S)
    att_s = c1("", b=2, s=512)
    att_p = c1("", b=2, s=512)
    att_pT = c1("", b=2, s=512)
    rope_t = c1("", v=4, t=NT, h=16, f=8)
    top8 = c1("", t=NT, n=8)
    w_idx = c1("", t=NT, n=8)
    att_nm = c1("", u=12, h=4)
    att_rs = c1("", g=2, t=NT, h=NH)
    att_ri = c1("", g=2, t=NT, h=NH)

    c2 = Carve()
    eC = c2("", j=16, s=S)
    eS = c2("", j=16, s=S)
    uT = c2("", c=4, s=S)
    gqT = c2("", c=2, s=S)
    gkT = c2("", c=2, s=S)
    aT = c2("", s=S)
    Bst = c2("", r=2, c=4, n=P)
    Cst = c2("", r=2, c=4, n=P)
    gb = c2("", c=2, s=S)
    work_at = c2.at
    w5 = c2("", r=2, j=2, s=S)
    t5 = c2("", r=2, j=2, s=S)
    g5 = c2("", b=2, r=2, j=2, s=S)
    h5 = c2("", b=2, r=2, j=2, s=S)
    p5 = c2("", r=2, j=2, s=S)
    cw = Carve(work_at)
    e_tmp = cw("", r=2, j=16, s=TSPAN)
    Bnat = cw("", r=2, j=16, c=32)
    Cnat = cw("", r=2, c=4, n=P)
    Cmask = cw("", r=2, c=4, n=P)
    assert cw.at <= c2.at
    low, high = Carve(8192), Carve(work_at + 3 * 1024)
    w_hi = [low("", n=SLOT), low("", n=SLOT), high("", n=SLOT), high("", n=SLOT)]
    hf_hi = [prow.rearrange("p n c -> p (n c)")[:, i * S:(i + 1) * S] for i in range(2)] + [low("", s=S), low("", s=S)]
    assert low.at <= work_at and high.at <= REGION
    hT_hi = xn.rearrange("p t d -> p (t d)").rearrange("p (k s) -> p k s", k=KD)
    cg = Carve(work_at)
    gz = cg("", v=3, c=2, s=S)
    gD = cg("", b=2, n=512)
    gQ = cg("", b=2, n=512)
    gK = cg("", b=2, n=512)
    scT = cg("", b=2, j=2, c=2, i=P)
    scO = cg("", b=2, c=2, i=P)
    o_gla = cg("", t=NT, n=512)
    assert cg.at <= REGION
    vg = xn
    cm = Carve()
    earlier = cm("", n=P)
    iota = cm("", n=CAP)
    xg = cm("", k=KD, n=CAP)
    pick = cm("", t=NT, n=CAP)
    pick_w = cm("", t=NT, n=CAP)
    spread = cm("", n=S)
    moe_h = cm("", b=2, i=2, n=CAP)
    moe_hi = cm("", b=2, i=2, n=CAP)
    moe_down_hi = cm("", b=2, k=2, n=D)
    moe_s = cm("", b=2, i=2, n=CAP)
    moe_y = cm("", n=D)
    place = cm("", t=NT, n=TURNS + 1)
    weight = cm("", t=NT, n=TURNS + 1)
    turns = nc.alloc_sbuf_tensor("turns", [P, TURNS], mybir.dt.int32)[:, :]
    junk = ffn_tmp.rearrange("p b s -> p (b s)")

    psum = [nc.alloc_psum_tensor(f"bank{i}", [P, 512], F32)[:, :] for i in range(8)]
    bank_of = {}
    sig_pe, sig_act, sig_dve, sig_pool, sig_sp = (sig.of(e) for e in ("pe", "act", "dve", "pool", "sp"))

    def slot(key):
        i = where[key] % SLOTS
        return ring[:, i * SLOT:(i + 1) * SLOT]

    def loaded(key, r=None):
        i = where[key]
        n = 16 * (i // SLOTS + 1)
        return sems[f"slot_loaded{i % SLOTS}"], n if r is None else r * (16 * 3 * GROUPS // SLOTS) + n

    def col(l, name, n=1, at=0):
        r = (PROW if l < 2 else PROW2)[name] + at
        b = 2 * l + r // P if l < 2 else 4 + l - 2
        return pcol[:, b, r % P:r % P + n]

    def source(key, turn=None):
        kind, l = key[0], key[1]
        li = l % 2
        if kind in ("ada", "in"):
            name = {("ada", 0): "w_ada", ("ada", 1): "mod_w_2", ("in", 0): "w_in", ("in", 1): "w_in_2"}[kind, l // 2]
            w = A[name][li]
            n = min(CW, w.shape[1] - key[2] * CW)
            return w[:, key[2] * CW:key[2] * CW + n].rearrange("(k p) n -> p k n", p=P), KD, n
        if kind == "glu":
            return A["s5_w_glu_2"][li].rearrange("(k p) n -> p k n", p=P), 4, 512
        if kind == "out":
            w = A["w_out" if l < 2 else "w_out_2"][li]
            return w[key[2] * 256:(key[2] + 1) * 256, :].rearrange("(k p) n -> p k n", p=P), 2, D
        e, g = key[2], key[3]
        if kind == "up":
            if l < 2:
                w = A[("w_up_act", "w_up_lin")[key[4]]][li]
            elif l == 2:
                w = A[("ffn_w_gate_2", "ffn_w_up_2")[key[4]]][0]
            else:
                w = A[("moe_w_gate_2", "moe_w_up_2")[key[4]]][0]
                w = w[0] if turn is None else w[bass.ds(turn, 1)].rearrange("e k n -> (e k) n")
            return w[:, g * CW:(g + 1) * CW].rearrange("(k p) n -> p k n", p=P), KD, CW
        w = A["w_down"][li] if l < 2 else A["ffn_w_down_2"][0] if l == 2 else A["moe_w_down_2"][0]
        if l == 3:
            w = w[0] if turn is None else w[bass.ds(turn, 1)].rearrange("e k n -> (e k) n")
        return w[g * CW:(g + 1) * CW, :].rearrange("(k p) n -> p k n", p=P), 2, D

    def chunk(key):
        _, k, n = source(key)
        return slot(key)[:, 0:k * n].rearrange("p (k n) -> p k n", k=k)

    def hi_part(key):
        _, k, n = source(key)
        i = ffn_chunks(key[1]).index(key)
        return w_hi[i % len(w_hi)].rearrange("p (k n) -> p k n", k=k)

    def x_ready(l, stage):
        if stage == "ffn":
            return ("x_new", l, "mix")
        return ("x_new", l - 1, "ffn") if l else ("x_loaded",)

    with nc.Block() as block:

        @block.tensor
        def _(pe):
            done = sig_pe
            user = [None] * 8
            turn = [0]

            def bank(key, freed, among=range(8)):
                b = among[turn[0] % len(among)]
                turn[0] += 1
                if user[b]:
                    pe.wait_ge(*until(*user[b]))
                user[b] = freed
                bank_of[key] = b
                return psum[b]

            def transposes(key, freed, pieces, among=range(8)):
                o = bank(key, freed, among)
                for c, piece in pieces:
                    m = nc.tensor.transpose(o[0:piece.shape[1], c:c + P], piece, ident)
                m.then_inc(*done("pe_tile", *key))

            def mod_tile(l, q, among=range(8)):
                pe.wait_ge(*until("mod_sum", l, q))
                o = bank(("mod", l, q), ("mod_out", l, q), among)
                if q // 4 in (2, 5):
                    m = nc.tensor.matmul(o[:, 0:CW], ones, mod_acc[:, q % 4, :], start=True, stop=True)
                else:
                    for i in range(2):
                        m = nc.tensor.matmul(o[:, i:i + 1], mod_acc[:, q % 4, i * P:(i + 1) * P], ones[:, 0:1],
                                             start=True, stop=True)
                m.then_inc(*done("pe_tile", "mod", l, q))

            def norm_tiles(l, stage):
                src = xn if l < 2 else x
                for b in range(4):
                    if b == 0:
                        pe.wait_ge(*(until("xn", l, stage) if l < 2 else until(*x_ready(l, stage))))
                    key = ("norm", l, stage, b)
                    transposes(key, ("hT", l, stage, b) if b % 2 == 0 else ("hTd", l, stage, b),
                               [(i * S + t * P, src[:, t, (2 * b + i) * P:(2 * b + i + 1) * P])
                                for i in range(2) for t in range(NT)])

            def hT_ready(l, stage):
                pe.wait_ge(*until("hT", l, stage, 2))
                pe.wait_ge(*until("hTd", l, stage, 3))

            def in_tokens(l, n):
                key = ("in", l, n)
                pe.wait_ge(*loaded(key))
                w = chunk(key)
                nn = w.shape[2]
                o = bank(key, ("in_out", l, n)).rearrange("p (t n) -> p t n", t=NT)
                for t in range(NT):
                    for k in range(KD):
                        m = nc.tensor.matmul(o[:, t, 0:nn], hT[:, k, t * P:(t + 1) * P], w[:, k, :],
                                             start=k == 0, stop=k == KD - 1)
                m.then_inc(*done("pe_tile", *key))

            def in_features(l, n):
                key = ("in", l, n)
                pe.wait_ge(*loaded(key))
                w = chunk(key)
                nn = w.shape[2]
                o = bank(key, ("in_out", l, n)).rearrange("p (t n) -> p t n", t=NT)
                for i in range(-(-nn // P)):
                    r = min(P, nn - i * P)
                    for k in range(KD):
                        m = nc.tensor.matmul(o[0:r, i, :], w[:, k, i * P:i * P + r], hT[:, k, :],
                                             start=k == 0, stop=k == KD - 1)
                m.then_inc(*done("pe_tile", *key))

            def qk_tiles(l, b, c0, evac, among=range(8)):
                for i in range(2):
                    transposes(("qk", l, b, evac, i), ("qk_out", l, evac, i),
                               [(j * S + t * P, proj[:, t, c0 + (2 * i + j) * P:c0 + (2 * i + j + 1) * P])
                                for j in range(2) for t in range(NT)], among)

            def indexer(l):
                pe.wait_ge(*until("rope", l, 2))
                qk_tiles(l, 0, QI, "qi")
                pe.wait_ge(*until("kidup", l))
                transposes(("kiT", l), ("kiT_out", l), [(t * P, kidup[:, t, :]) for t in range(NT)])

            def indexer_logits(l):
                pe.wait_ge(*until("kiT_out", l))
                for t in range(NT):
                    for n in range(4 if t else 2):
                        o = bank(("idx", l, t, n), ("idx_relu", l, t, n))
                        kn = (t + 1) * P
                        for i, h in enumerate(unit_heads(t, n)):
                            r = 64 * (h % 2)
                            m = nc.tensor.matmul(o[:, i * kn:(i + 1) * kn], qk[r:r + 64, 0, h // 2, t * P:(t + 1) * P],
                                                 kiT[r:r + 64, 0:kn], start=True, stop=True)
                        m.then_inc(*done("pe_tile", "idx", l, t, n))

            def attention(l):
                o = {}
                for u in range(len(UNITS1) + 2):
                    if u < len(UNITS1):
                        g, t, n = UNITS1[u]
                        kn = (t + 1) * P
                        if (t, n) == (0, 0):
                            if g:
                                pe.wait_ge(*until("rope", l, 1))
                                qk_tiles(l, 0, 1536, "dq", range(6))
                                qk_tiles(l, 3, 2048, "dk", range(6))
                            pe.wait_ge(*until("qk_out", l, ("mk", "dk")[g], 1))
                        s = bank(("sc", l, u), ("att_mask", l, u), range(6))
                        for i, h in enumerate(unit_heads(t, n)):
                            r = 64 * (h % 2)
                            m = nc.tensor.matmul(s[:, i * kn:(i + 1) * kn],
                                                 qk[r:r + 64, (1, 0)[g], h // 2, t * P:(t + 1) * P],
                                                 qk[r:r + 64, (2, 3)[g], h // 2, 0:kn], start=True, stop=True)
                        m.then_inc(*done("pe_tile", "sc", l, u))
                    if 1 <= u <= len(UNITS1):
                        g, t, n = UNITS1[u - 1]
                        pe.wait_ge(*until("att_exp", l, u - 1))
                        transposes(("pT", l, u - 1), ("att_pT", l, u - 1),
                                   [(i * P, att_p[:, (u - 1) % 2, i * P:(i + 1) * P]) for i in range(4)], range(6))
                    if u >= 2:
                        g, t, n = UNITS1[u - 2]
                        heads = unit_heads(t, n)
                        if n == 0:
                            b = 6 + (2 * g + t) % 2
                            if user[b]:
                                pe.wait_ge(*until(*user[b]))
                            user[b] = ("att_o", l, g, t)
                            bank_of[("o", l, g, t)] = b
                            o[g, t] = psum[b]
                        pe.wait_ge(*until("att_pT", l, u - 2))
                        for i, h in enumerate(heads):
                            for kb in range(t + 1):
                                at = (i * (t + 1) + kb) * P
                                vc = 1536 * g + 1024 + h * HD
                                m = nc.tensor.matmul(o[g, t][:, h * HD:(h + 1) * HD], att_pT[:, (u - 2) % 2, at:at + P],
                                                     proj[:, kb, vc:vc + HD], start=kb == 0, stop=kb == t)
                        m.then_inc(*done("pe_tile", "pv", l, u - 2))

            def o_transposes(l):
                for b in range(4):
                    pe.wait_ge(*until("att_on", l, b // 2, 1))
                    transposes(("oT", l, b), ("oT_out", l, b),
                               [(i * S + t * P, xn[:, t, (2 * b + i) * P:(2 * b + i + 1) * P])
                                for i in range(2) for t in range(NT)])

            def out_projection(l):
                tiles = [bank(("y", l, "mix", i), ("post", l, "mix", i), range(4, 8)) for i in range(4)]
                for n in range(4):
                    key = ("out", l, n)
                    pe.wait_ge(*loaded(key))
                    w = chunk(key)
                    for k in range(2):
                        kk = 2 * n + k
                        for i in range(4):
                            t, c = i // 2, i % 2
                            m = nc.tensor.matmul(tiles[i], hT[:, kk, t * P:(t + 1) * P], w[:, k, c * 512:(c + 1) * 512],
                                                 start=kk == 0, stop=kk == KD - 1, skip_group_check=True)
                    m.then_inc(*done("pe_used", *key))

            def product(o, a_hi, a_lo, b_hi, b_lo, start, stop):
                nc.tensor.matmul(o, split(a_hi), split(b_hi), start=start, stop=False, skip_group_check=True)
                nc.tensor.matmul(o, split(a_lo), split(b_hi), start=False, stop=False, skip_group_check=True)
                return nc.tensor.matmul(o, split(a_hi), split(b_lo), start=False, stop=stop, skip_group_check=True)

            def ffn(l):
                tiles = [None] * 4
                up_banks = range(4)

                def up(g):
                    o = [bank(("up", l, 0, 2 * g + i), ("up_out", l, 0, 2 * g + i), up_banks) for i in range(2)]
                    for m in (0, 1):
                        key = ("up", l, 0, g, m)
                        pe.wait_ge(*until("w_lo", *key))
                        w, wh = chunk(key), hi_part(key)
                        for i in range(2):
                            for k in range(KD):
                                sl = slice(i * P, (i + 1) * P)
                                if (g, m, i, k) == (0, 0, 0, KD // 2):
                                    pe.wait_ge(*until("hT_lo", l, 1))
                                last = product(o[i][:, m * S:(m + 1) * S], wh[:, k, sl], w[:, k, sl], hT_hi[:, k, :], hT[:, k, :],
                                               k == 0, k == KD - 1)
                            if m == 1:
                                last.then_inc(*done("pe_tile", "up", l, 0, 2 * g + i))
                            elif i == 1:
                                last.then_inc(*done("pe_used", "up", l, g))

                def down(g):
                    key = ("down", l, 0, g)
                    pe.wait_ge(*until("w_lo_down", l, g))
                    w, wh = chunk(key), hi_part(key)
                    for i in range(2):
                        f = 2 * g + i
                        pe.wait_ge(*until("up_out", l, 0, f))
                        for j in range(4):
                            t, c = j // 2, j % 2
                            ts, cs = slice(t * P, (t + 1) * P), slice(c * 512, (c + 1) * 512)
                            last = product(tiles[j], hf_hi[f % 4][:, ts], hf[:, f % 4, ts], wh[:, i, cs], w[:, i, cs],
                                           f == 0, f == FF[l] // P - 1)
                    last.then_inc(*done("pe_used", "down", l, 0, g))

                pe.wait_ge(*until("hT_lo", l, 0))
                turn[0] = 0
                for j in range(4):
                    b = 4 + j
                    if user[b]:
                        pe.wait_ge(*until(*user[b]))
                    user[b] = ("post", l, "ffn", j)
                    bank_of["y", l, "ffn", j] = b
                    tiles[j] = psum[b]
                groups = ffn_groups(l)
                for g in range(groups + 1):
                    if g:
                        for q in ada_in_ffn(l, g - 1):
                            mod_tile(l + 1, q, up_banks)
                    if g < groups:
                        up(g)
                    if g:
                        down(g - 1)

            def mixer_two(l):
                norm_tiles(l, "mix")
                hT_ready(l, "mix")
                for n in (8, 0, 1, 2, 3):
                    in_features(l, n)
                pe.wait_ge(*until("b_masked", l))
                for r in range(2):
                    transposes(("BT", l, r), ("bst", l, r), [(q * P, Bnat[:, r, 4 * q:4 * q + 4, :].rearrange("p j c -> p (j c)")) for q in range(4)])
                for r in range(2):
                    transposes(("CT", l, r), ("c_masked", l, r), [(q * P, Cnat[:, r, q, :]) for q in range(4)])
                o = bank(("lg", l), ("gla_z", l))
                pe.wait_ge(*until("w_alpha", l))
                pe.wait_ge(*until("in_out", l, 8))
                for i in range(2):
                    m = nc.tensor.matmul(o[:, i * S:(i + 1) * S], w_alpha[0:16, i * P:(i + 1) * P], aT[0:16, :],
                                         start=True, stop=True)
                m.then_inc(*done("pe_tile", "lg", l))

                def s5_in(u):
                    qq, i = u // 4, u % 4
                    for r in range(2):
                        o = bank(("bu", l, u, r), ("s5_w", l, u), range(6))
                        for jj in range(2):
                            q = 2 * qq + jj
                            m = nc.tensor.matmul(o[:, jj * S:(jj + 1) * S], Bst[32 * i:32 * i + 32, r, q, :],
                                                 uT[32 * i:32 * i + 32, q, :], start=True, stop=True)
                        m.then_inc(*done("pe_tile", "bu", l, u, r))

                ys = {}

                def s5_out(u):
                    qq, i = u // 4, u % 4
                    if i == 0:
                        b = 6 + qq
                        if user[b]:
                            pe.wait_ge(*until(*user[b]))
                        user[b] = ("s5_y", l, qq)
                        bank_of["s5y", l, qq] = b
                        ys[qq] = psum[b]
                    pe.wait_ge(*until(*s5_rotated(l, u)))
                    if u == 0:
                        pe.wait_ge(*until("cst", l))
                    for jj in range(2):
                        for r in range(2):
                            m = nc.tensor.matmul(ys[qq][32 * i:32 * i + 32, jj * S:(jj + 1) * S],
                                                 Cst[:, r, 2 * qq + jj, 32 * i:32 * i + 32], h5[:, u % 2, r, jj, :],
                                                 start=r == 0, stop=r == 1)
                    m.then_inc(*done("pe_tile", "s5o", l, u))

                pe.wait_ge(*until("bst", l, 1))
                pe.wait_ge(*until("in_out", l, 1))
                s5_in(0)
                s5_in(1)
                for u in range(2, 10):
                    if u in (2, 3, 4, 5):
                        n = u + 2
                        key = ("in", l, n)
                        pe.wait_ge(*loaded(key))
                        w = chunk(key)
                        o = bank(key, ("in_out", l, n), range(6)).rearrange("p (t n) -> p t n", t=NT)
                        for t in range(NT):
                            for k in range(KD):
                                m = nc.tensor.matmul(o[:, t, :], hT[:, k, t * P:(t + 1) * P], w[:, k, :],
                                                     start=k == 0, stop=k == KD - 1)
                        m.then_inc(*done("pe_tile", *key))
                    if u < 8:
                        s5_in(u)
                    s5_out(u - 2)
                key = ("glu", l)
                pe.wait_ge(*loaded(key))
                pe.wait_ge(*until("s5_gelu", l, 1))
                w = chunk(key)
                for b in range(2):
                    o = bank(("glu", l, b), ("s5_sig", l, b))
                    for i in range(2):
                        for k in range(4):
                            m = nc.tensor.matmul(o[:, i * S:(i + 1) * S], w[:, k, (2 * b + i) * P:(2 * b + i + 1) * P],
                                                 uT[:, k, :], start=k == 0, stop=k == 3)
                    m.then_inc(*done("pe_tile", "glu", l, b))
                pe.wait_ge(*until("gla_k", l, 128))
                for par in range(2):
                    r = 64 * par
                    o = bank(("off", l, par), ("off_out", l, par))
                    for c in range(2):
                        m = nc.tensor.matmul(o[:, c * P:(c + 1) * P], gK[r:r + 64, 0, c * S:c * S + P],
                                             gQ[r:r + 64, 0, c * S + P:c * S + S], start=True, stop=True)
                    m.then_inc(*done("pe_tile", "off", l, par))
                for n, half in enumerate(LEVELS):
                    if half:
                        pe.wait_ge(*until("gla_k", l, half))
                    for par in range(2):
                        r = 64 * par
                        o = bank(("lv", l, n, par), ("lv_out", l, n, par))
                        for t in range(NT):
                            for c in range(2):
                                at = c * S + t * P
                                kk = gK[r:r + 64, (n + 1) % 2, at:at + P] if half else gkT[r:r + 64, c, t * P:(t + 1) * P]
                                qq = gQ[r:r + 64, (n + 1) % 2, at:at + P] if half else gqT[r:r + 64, c, t * P:(t + 1) * P]
                                m = nc.tensor.matmul(o[:, (2 * t + c) * P:(2 * t + c + 1) * P], kk, qq, start=True, stop=True)
                        m.then_inc(*done("pe_tile", "lv", l, n, par))
                pe.wait_ge(*until("off_out", l, 1))
                pe.wait_ge(*until("lv_out", l, len(LEVELS) - 1, 1))
                pe.wait_ge(*until("in_out", l, 5))
                for t in range(NT):
                    o = bank(("go", l, t), ("gla_o", l, t))
                    for h in range(4):
                        for j in range(t + 1):
                            lhs = scT[:, h % 2, j, h // 2, :] if j == t else scO[:, h % 2, h // 2, :]
                            m = nc.tensor.matmul(o[:, h * P:(h + 1) * P], lhs, vg[:, j, h * P:(h + 1) * P],
                                                 start=j == 0, stop=j == t)
                    m.then_inc(*done("pe_tile", "go", l, t))
                pe.wait_ge(*until("gla_o", l, 1))
                for b in range(2):
                    transposes(("goT", l, b), ("goT_out", l, b),
                               [(i * S + t * P, o_gla[:, t, (2 * b + i) * P:(2 * b + i + 1) * P])
                                for i in range(2) for t in range(NT)])
                pe.wait_ge(*until("goT_out", l, 1))
                pe.wait_ge(*until("s5_done", l))

            def mixture():
                up_b, pick_b, y_b, z_b = psum[0:2], psum[2:4], psum[4:6], psum[6:8]

                def pick_tiles(e, r):
                    for b in range(2):
                        if b == 0:
                            pe.wait_ge(*(within(r, 0, "moe_vec", "pick", e) if r is not None else until("moe_vec", "pick", e)))
                        for i in range(4):
                            k = 4 * b + i
                            for t in range(NT):
                                m = nc.tensor.matmul(pick_b[b][:, i * CAP:(i + 1) * CAP], x[:, t, k * P:(k + 1) * P], pick[:, t, :],
                                                     start=t == 0, stop=t == NT - 1)
                        m.then_inc(*done("moe_tile", "pick", b, e))

                def spread_y(e, w_y, w_add):
                    pe.wait_ge(*w_y)
                    for i in range(4):
                        t, c = i // 2, i % 2
                        if i >= 2:
                            pe.wait_ge(*w_add(i - 2))
                        nc.tensor.matmul(z_b[i % 2], spread[:, t * P:(t + 1) * P], moe_y[:, c * 512:(c + 1) * 512],
                                         start=True, stop=True).then_inc(*done("moe_tile" if e != "tail" else "moe_tail", "z", i, e))

                def body(e, r):
                    now = (lambda *ev: until(*ev, e)) if r is None else (lambda *ev: within(r, 0, *ev, e))

                    def up(g):
                        if g >= 2:
                            pe.wait_ge(*now("moe_vec", "h", g - 2))
                        elif r is not None:
                            pe.wait_ge(*within(r, 1, "moe_vec", "h", GROUPS - 2 + g, e))
                        if g == 0:
                            pe.wait_ge(*(until("moe_act", "xg", "start") if r is None else within(r, 1, "moe_act", "xg", e)))
                        o = up_b[g % 2]
                        for m in (0, 1):
                            key = ("up", 3, e, g, m)
                            pe.wait_ge(*loaded(key, r))
                            w = chunk(key)
                            for i in range(2):
                                at = (2 * m + i) * CAP
                                for k in range(KD):
                                    last = nc.tensor.matmul(o[:, at:at + CAP], w[:, k, i * P:(i + 1) * P], xg[:, k, :],
                                                            start=k == 0, stop=k == KD - 1)
                        last.then_inc(*done("moe_tile", "up", g, e))

                    def down(g):
                        key = ("down", 3, e, g)
                        pe.wait_ge(*now("moe_vec", "h", g))
                        pe.wait_ge(*now("moe_vec", "down_lo", g))
                        w, wh = chunk(key), moe_down_hi[:, g % 2]
                        for i in range(2):
                            for c in range(2):
                                cs = slice(c * 512, (c + 1) * 512)
                                last = product(y_b[c], moe_hi[:, g % 2, i, :], moe_h[:, g % 2, i, :], wh[:, i, cs], w[:, i, cs],
                                               g + i == 0, g == GROUPS - 1 and i == 1)
                        last.then_inc(*done("moe_used", "down", g, e))

                    up(0)
                    up(1)
                    if r is not None:
                        spread_y(e, within(r, 1, "moe_act", "y", e), lambda i: now("moe_vec", "z", i))
                    if r is None:
                        pe.wait_ge(*until("moe_vec", "pick", "start"))
                    for t in range(NT):
                        m = nc.tensor.transpose(pick_b[0][:, t * P:(t + 1) * P], pick_w[:, t, :], ident)
                    m.then_inc(*done("moe_tile", "spread", e))
                    for g in range(GROUPS):
                        if 2 <= g + 1 < GROUPS:
                            up(g + 1)
                        if g == GROUPS - 2:
                            pe.wait_ge(*now("moe_act", "spread"))
                            pick_tiles(e, r)
                        down(g)

                pe.wait_ge(*until("chosen"))
                pe.wait_ge(*until("const_moe", 1))
                o = bank(("places",), ("placed",))
                sel = moe[:, 8]
                nc.tensor.matmul(o[:, 0:NE], earlier, sel[:, 0, :], start=True, stop=True)
                for part, lhs in ((1, earlier), (2, ones)):
                    nc.tensor.matmul(o[:, part * NE:(part + 1) * NE], ones, sel[:, 0, :], start=True, stop=False)
                    m = nc.tensor.matmul(o[:, part * NE:(part + 1) * NE], lhs, sel[:, 1, :], start=False, stop=True)
                m.then_inc(*done("pe_tile", "places"))
                pe.wait_ge(*until("placed"))
                pick_tiles("start", None)
                body("first", None)
                pe.wait_ge(*until("turns"))
                n = pe.value_load(turns[0:1, 0:1], min_val=NE - 1, max_val=TURNS - 1)
                done.begin()
                with pe.Fori(0, n) as r:
                    body("loop", r)
                done.end("moe_tile", "moe_used")
                spread_y("tail", within(n, 1, "moe_act", "y", "loop"), lambda i: until("moe_last", "z", i))

            pe.wait_ge(*until("c_here"))
            transposes(("cT",), ("c_raw",), [(0, crow)])
            pe.wait_ge(*until("memset_ones"))
            for q in range(4):
                mod_tile(0, q)
            pe.wait_ge(*until("const", "ident"))
            pe.wait_ge(*until("param_rows"))
            pe.wait_ge(*until("dt_rows", 3))
            for b in range(2):
                transposes(("param", b), ("pcol", b), [(i * P, prow[:, 4 * b + i, :]) for i in range(4 if b == 0 else 2)])
            for q in range(4, 8):
                mod_tile(0, q)
            for l in range(LAYERS):
                if l < 2:
                    norm_tiles(l, "mix")
                    hT_ready(l, "mix")
                    for i, n in enumerate(PROJ_ORDER):
                        in_tokens(l, n)
                        if l == 0:
                            for q in ([8 + i] if i < 14 else [22, 23]):
                                mod_tile(0, q)
                        if i == 4:
                            indexer(l)
                        if i == 6:
                            indexer_logits(l)
                    pe.wait_ge(*until("rope", l, 0))
                    qk_tiles(l, 1, 0, "mq")
                    qk_tiles(l, 2, 512, "mk")
                    attention(l)
                    o_transposes(l)
                    pe.wait_ge(*until("oT_out", l, 3))
                else:
                    mixer_two(l)
                out_projection(l)
                norm_tiles(l, "ffn")
                if l == 3:
                    hT_ready(l, "ffn")
                    pe.wait_ge(*until("router_loaded"))
                    pe.wait_ge(*until("router_b_loaded"))
                    o = bank(("router",), ("logits",))
                    for t in range(NT):
                        for k in range(KD):
                            nc.tensor.matmul(o[:, t * NE:(t + 1) * NE], hT[:, k, t * P:(t + 1) * P], router[:, k, :],
                                             start=k == 0, stop=False)
                        m = nc.tensor.matmul(o[:, t * NE:(t + 1) * NE], ones[0:1, :], router_b[0:1, :],
                                             start=False, stop=True)
                    m.then_inc(*done("pe_tile", "router"))
                    mixture()
                else:
                    ffn(l)

        @block.sync
        def _(sp):
            body = where["up", 3, "loop", 0, 0]
            for i, (key, _) in enumerate(plan[:body]):
                if i >= SLOTS:
                    sp.wait_ge(*until(*plan[i - SLOTS][1]))
                src, _, _ = source(key)
                sp.dma_start(chunk(key), src).then_inc(sems[f"slot_loaded{i % SLOTS}"], 16)
            sp.wait_ge(*until("turns"))
            n = sp.value_load(turns[0:1, 0:1], min_val=NE - 1, max_val=TURNS - 1)
            with sp.Fori(0, n) as r:
                turn = sp.value_load(turns[0:1, bass.ds(r + 1, 1)], min_val=0, max_val=NE - 1)
                for c in range(3 * GROUPS):
                    key = plan[body + c][0]
                    src, _, _ = source(key, turn)
                    sp.wait_ge(*(within(r, 0, *plan[body + c - SLOTS][1]) if c >= SLOTS
                                 else within(r, 1, *plan[body + c - SLOTS + 3 * GROUPS][1])))
                    sp.dma_start(chunk(key), src).then_inc(sems[f"slot_loaded{(body + c) % SLOTS}"], 16)
            for i in range(4):
                t, c = i // 2, i % 2
                if c == 0:
                    sp.wait_ge(*until("x_new_pool", LAYERS - 1, "ffn") if t == 0 else until("x_new", LAYERS - 1, "ffn"))
                    sp.dma_start(out[0, t * P:(t + 1) * P, :], x[:, t, :]).then_inc(*sig_sp.dma("stored", t))
            sp.wait_ge(*until("stored", 1))

        @block.gpsimd
        def _(pool):
            done = sig_pool
            nc.gpsimd.memset(minus_half, -0.5).then_inc(*done("pool_chain", "half"))
            nc.gpsimd.memset(ones, 1.0).then_inc(*done("memset_ones"))
            pool.wait_ge(*done.prev())

            def table_start(l):
                nc.gpsimd.tensor_copy(eC[:, :, 0:1], s5p[:, l - 2, 1, :].unsqueeze(2)).then_inc(*done("pool_chain", l, "c0"))
                nc.gpsimd.tensor_copy(eS[:, :, 0:1], s5p[:, l - 2, 2, :].unsqueeze(2)).then_inc(*done("pool_chain", l, "s0"))

            def table_step(l, k, h0):
                w = min(TSPAN, k)
                ca, sa = eC[:, :, h0:h0 + w], eS[:, :, h0:h0 + w]
                cb = eC[:, :, k - 1:k].broadcast_to([P, 16, w])
                sb_ = eS[:, :, k - 1:k].broadcast_to([P, 16, w])
                oc, os_ = eC[:, :, k + h0:k + h0 + w], eS[:, :, k + h0:k + h0 + w]
                ta, tb = e_tmp[:, 0, :, 0:w], e_tmp[:, 1, :, 0:w]
                pool.wait_ge(*done.prev())
                nc.gpsimd.tensor_tensor(oc, ca, cb, ALU.mult).then_inc(*done("pool_chain", l, k, h0, 0))
                nc.gpsimd.tensor_tensor(ta, sa, sb_, ALU.mult).then_inc(*done("pool_chain", l, k, h0, 1))
                nc.gpsimd.tensor_tensor(os_, sa, cb, ALU.mult).then_inc(*done("pool_chain", l, k, h0, 2))
                nc.gpsimd.tensor_tensor(tb, ca, sb_, ALU.mult).then_inc(*done("pool_chain", l, k, h0, 3))
                pool.wait_ge(*done.prev())
                nc.gpsimd.tensor_tensor(oc, oc, ta, ALU.subtract).then_inc(*done("pool_chain", l, k, h0, 4))
                nc.gpsimd.tensor_tensor(os_, os_, tb, ALU.add).then_inc(*done("pool_chain", l, k, h0, 5))

            TABLE_STEPS = [(1 << i, h0) for i in range(8) for h0 in range(0, 1 << i, TSPAN)]

            def ffn(l):
                if l:
                    pool.wait_ge(*until("post", l, "mix", 3))
                    if l == 1:
                        pool.wait_ge(*until("s5_params"))
                    table_start(l + 1)
                steps = list(TABLE_STEPS) if l else []
                for g in range(ffn_groups(l)):
                    key = ("down", l, 0, g)
                    pool.wait_ge(*until("w_hi", *key))
                    nc.gpsimd.tensor_tensor(split(chunk(key)), chunk(key), whole(hi_part(key)), ALU.subtract).then_inc(*done("w_lo_down", l, g))
                    for k, h0 in steps[:4 if g == 0 else 1]:
                        table_step(l + 1, k, h0)
                    steps = steps[4 if g == 0 else 1:]
                if l:
                    assert not steps
                    pool.wait_ge(*done.prev())
                    nc.gpsimd.memset(stat[:, 63:64], 0.0).then_inc(*done("tables", l + 1))

            def rotate(l, u):
                qq, i = u // 4, u % 4
                c, s = eC[:, 8 * qq + i:8 * qq + i + 5:4, :], eS[:, 8 * qq + i:8 * qq + i + 5:4, :]
                g, h = g5[:, u % 2], h5[:, u % 2]
                pool.wait_ge(*until("s5_g", l, u))
                if u >= 2:
                    pool.wait_ge(*until("pe_tile", "s5o", l, u - 2))
                nc.gpsimd.tensor_tensor(h[:, 0], c, g[:, 0], ALU.mult).then_inc(*done("pool_chain", l, "r", u, 0))
                nc.gpsimd.tensor_tensor(p5[:, 0], s, g[:, 1], ALU.mult).then_inc(*done("pool_chain", l, "r", u, 1))
                nc.gpsimd.tensor_tensor(h[:, 1], s, g[:, 0], ALU.mult).then_inc(*done("pool_chain", l, "r", u, 2))
                nc.gpsimd.tensor_tensor(p5[:, 1], c, g[:, 1], ALU.mult).then_inc(*done("pool_chain", l, "r", u, 3))
                pool.wait_ge(*done.prev())
                nc.gpsimd.tensor_tensor(h[:, 0], h[:, 0], p5[:, 0], ALU.subtract).then_inc(*done("pool_chain", l, "r", u, 4))
                nc.gpsimd.tensor_tensor(h[:, 1], h[:, 1], p5[:, 1], ALU.add).then_inc(*done("s5_h", l, u))
                pool.wait_ge(*done.prev())

            def power(dst, *key):
                pool.wait_ge(*until("variance", *key))
                nc.gpsimd.tensor_tensor(dst, dst, minus_half[:, 0:dst.shape[1]], ALU.pow).then_inc(*done("rstd", *key))

            def post(l, stage):
                power(stat[:, 58:59], l, "post", stage, 0)
                pool.wait_ge(*until("normed", l, stage))
                pool.wait_ge(*until(f"rows_{stage}{l}", 1))
                nc.gpsimd.tensor_tensor(xn[:, 0, :], xn[:, 0, :], rows[:, 0, :], ALU.mult).then_inc(*done("pool_chain", l, stage, "gain"))
                power(stat[:, 58:59], l, "post", stage, 1)
                pool.wait_ge(*until("pool_chain", l, stage, "gain"))
                nc.gpsimd.tensor_tensor(x[:, 0, :], xn[:, 0, :], rows[:, 1, :], ALU.add).then_inc(*done("x_new_pool", l, stage))

            for l in range(LAYERS):
                if l < 2:
                    power(stat[:, 32:34], l, "norm", "mix")
                    power(stat[:, 36:40], l, "o")
                    power(stat[:, 42:44], l, "post", "mix")
                    power(stat[:, 32:34], l, "norm", "ffn")
                else:
                    for u in range(8):
                        if u not in DVE_UNITS:
                            rotate(l, u)
                    pool.wait_ge(*until("s5_y", l, 1))
                    nc.gpsimd.memset(scT, 0.0).then_inc(*done("gla_zero", l, 0))
                    nc.gpsimd.memset(gQ, 0.0).then_inc(*done("gla_zero", l, 1))
                    nc.gpsimd.memset(gK, 0.0).then_inc(*done("gla_zero", l, 2))
                    for t in range(NT):
                        power(stat[:, 36:40], l, "gla", t)
                    post(l, "mix")
                if l < 3:
                    ffn(l)
                if l < 2:
                    power(stat[:, 42:44], l, "post", "ffn")
                else:
                    post(l, "ffn")

        @block.scalar
        def _(act):
            done = sig_act

            def tile(*key):
                act.wait_ge(*until("pe_tile", *key))
                return psum[bank_of[key]]

            def run(out_, in_, func, *event, **kw):
                return nc.scalar.activation(out_, in_, func, **kw).then_inc(*done(*event))

            def load(dst, src, *event):
                return act.dma_start(dst, src).then_inc(*done.dma(*event))

            def squares(l, stage):
                for t in range(NT):
                    ready = x_ready(l, stage)
                    act.wait_ge(*until(*(("x_new_t", *ready[1:], 0) if t == 0 and ready[0] == "x_new" else ready)))
                    if t:
                        act.wait_ge(*done.prev())
                    run(junk, x[:, t, :], ACT.Square, "ssq", l, stage, t, accum_out=stat[:, 2 * (stage == "ffn") + t:2 * (stage == "ffn") + t + 1])

            def norm_out(l, stage):
                act.wait_ge(*until("scales", l, stage))
                b0 = 24 * (stage == "ffn")
                for b in (0, 2):
                    p_ = tile("norm", l, stage, b)
                    for i in range(2):
                        k = 2 * b + i
                        name = ("hT", l, stage, b) if i else ("hT_half", l, stage, b)
                        run(hT[:, k, :], p_[:, i * S:(i + 1) * S], ACT.Identity, *name,
                            scale=scale_col[:, int(stage == "ffn"), k:k + 1], bias=mod_col[:, l % 2, b0 + k:b0 + k + 1])

            def in_out(l, n):
                p_ = tile("in", l, n).rearrange("p (t n) -> p t n", t=NT)
                nn = min(CW, PROJ1 - n * CW)
                run(proj[:, :, n * CW:n * CW + nn], p_[:, :, 0:nn], ACT.Copy, "in_out", l, n)

            def post_squares(l, stage):
                for i in range(4):
                    if i:
                        act.wait_ge(*done.prev())
                    act.wait_ge(*until("pe_used", "out", l, 3) if stage == "mix" else until("pe_used", "down", l, 0, ffn_groups(l) - 1))
                    run(junk[:, 0:512], psum[bank_of["y", l, stage, i]], ACT.Square, "y_ssq", l, stage, i,
                        accum_out=stat[:, 8 + i:9 + i])

            def s5_params():
                for l in (2, 3):
                    act.wait_ge(*done.prev())
                    run(s5t[:, l - 2, :], col(l, "s5_log_dt_2", 16), ACT.Exp, "s5_dt", l)
                for l in (2, 3):
                    act.wait_ge(*until("s5_angle", l))
                    run(s5p[:, l - 2, 0, :], s5t[:, 2, :], ACT.Exp, "s5_exp", l)
                    run(s5p[:, l - 2, 2, :], s5t[:, 4, :], ACT.Sin, "act_chain", l, "s5sin")
                    run(s5t[:, 5, :], s5t[:, 4, :], ACT.Sin, "s5_sin", l, scale=0.5)

            def mixer_one(l):
                squares(l, "mix")
                norm_out(l, "mix")
                if l == 0:
                    s5_params()
                for i, n in enumerate(PROJ_ORDER):
                    in_out(l, n)
                    if i == 4:
                        for j in range(2):
                            p_ = tile("qk", l, 0, "qi", j)
                            run(qk[:, 0, 2 * j:2 * j + 2, :].rearrange("p c s -> p (c s)"), p_, ACT.Copy, "qk_out", l, "qi", j)
                        p_ = tile("kiT", l)
                        run(kiT, p_[:, 0:S], ACT.Copy, "kiT_out", l)
                    if i == 6:
                        for t in range(NT):
                            for n2 in range(4 if t else 2):
                                p_ = tile("idx", l, t, n2)
                                m = n2 if t else n2
                                order = n2 + (2 if t else 0)
                                if order >= 2:
                                    act.wait_ge(*until("idx_sum", l, order - 2))
                                run(idx_r[:, order % 2, :], p_, ACT.Relu, "idx_relu", l, t, n2, scale=0.125)
                for b, name in ((1, "mq"), (2, "mk")):
                    for j in range(2):
                        p_ = tile("qk", l, b, name, j)
                        run(qk[:, b, 2 * j:2 * j + 2, :].rearrange("p c s -> p (c s)"), p_, ACT.Copy, "qk_out", l, name, j,
                            scale=0.125 if b == 1 else 1.0)
                for u, (g, t, n) in enumerate(UNITS1):
                    if g == 1 and (t, n) == (0, 0):
                        for b, name in ((0, "dq"), (3, "dk")):
                            for j in range(2):
                                p_ = tile("qk", l, b, name, j)
                                run(qk[:, b, 2 * j:2 * j + 2, :].rearrange("p c s -> p (c s)"), p_, ACT.Copy, "qk_out", l, name, j,
                                    scale=0.125 if b == 0 else 1.0)
                    act.wait_ge(*until("att_max", l, u))
                    if u >= 2:
                        act.wait_ge(*until("pe_tile", "pT", l, u - 2))
                    kn = (t + 1) * P
                    heads = unit_heads(t, n)
                    for i, h in enumerate(heads):
                        event = ("att_exp", l, u) if i == len(heads) - 1 else ("act_chain", l, "exp", u, i)
                        run(att_p[:, u % 2, i * kn:(i + 1) * kn], att_s[:, u % 2, i * kn:(i + 1) * kn], ACT.Exp, *event,
                            bias=att_nm[:, u, i:i + 1], accum_out=att_rs[:, g, t, h:h + 1])
                for g in range(2):
                    for t in range(NT):
                        act.wait_ge(*until("att_o", l, g, t))
                        act.wait_ge(*done.prev())
                        run(junk[:, 0:512], xn[:, t, g * 512:(g + 1) * 512], ACT.Square, "o_ssq", l, g, t,
                            accum_out=stat[:, 16 + 2 * g + t:17 + 2 * g + t])
                for b in range(4):
                    p_ = tile("oT", l, b)
                    for i in range(2):
                        k = 2 * b + i
                        name = ("oT_out", l, b) if i else ("act_chain", l, "oT", b)
                        run(hT[:, k, :], p_[:, i * S:(i + 1) * S], ACT.Copy, *name, scale=col(l, "g_moba_out", 1, k))

            def mixer_two(l):
                norm_out(l, "mix")
                feats = {8: aT[0:16, :], 0: uT[:, 0:2, :], 1: uT[:, 2:4, :], 2: gqT, 3: gkT}
                for n in (8, 0, 1, 2, 3):
                    p_ = tile("in", l, n)
                    dst = feats[n] if n == 8 else feats[n].rearrange("p c s -> p (c s)")
                    run(dst, p_[0:16, 0:S] if n == 8 else p_, ACT.Copy, "in_out", l, n, scale=0.125 if n == 2 else 1.0)
                for r in range(2):
                    p_ = tile("BT", l, r)
                    run(Bst[:, r].rearrange("p c n -> p (c n)"), p_, ACT.Copy, "bst", l, r)
                for n in (4, 5, 6, 7):
                    p_ = tile("in", l, n).rearrange("p (t n) -> p t n", t=NT)
                    run(vg[:, :, (n - 4) * CW:(n - 3) * CW], p_, ACT.Copy if n < 6 else ACT.Silu, "in_out", l, n)
                for qq in range(2):
                    act.wait_ge(*until("s5_y", l, qq))
                    v = uT[:, 2 * qq:2 * qq + 2, :].rearrange("p c s -> p (c s)")
                    run(v, v, ACT.Gelu_apprx_tanh, "s5_gelu", l, qq)
                for b in range(2):
                    p_ = tile("glu", l, b)
                    for i in range(2):
                        c = 2 * b + i
                        name = ("s5_sig", l, b) if i else ("act_chain", l, "sig", b)
                        run(hT[:, c, :], p_[:, i * S:(i + 1) * S], ACT.Sigmoid, *name, bias=col(l, "s5_b_glu_2", 1, c))
                act.wait_ge(*until("gla_abs", l))
                run(gz[:, 1], gz[:, 1], ACT.Exp, "act_chain", l, "lse")
                act.wait_ge(*done.prev())
                run(gz[:, 1], gz[:, 1], ACT.Ln, "gla_ln", l, bias=1.0)
                for m, half in enumerate([P] + LEVELS[:-1]):
                    act.wait_ge(*until("gla_d", l, half))
                    run(gD[:, m % 2, :], gD[:, m % 2, :], ACT.Exp, "gla_e", l, half)
                    if m == 0:
                        for par in range(2):
                            p_ = tile("off", l, par)
                            run(scO[:, par].rearrange("p c i -> p (c i)"), p_[:, 0:S], ACT.Copy, "off_out", l, par)
                for t in range(NT):
                    p_ = tile("go", l, t)
                    for h in range(4):
                        act.wait_ge(*done.prev())
                        run(junk[:, 0:P], p_[:, h * P:(h + 1) * P], ACT.Square, "go_ssq", l, t, h,
                            accum_out=stat[:, 20 + 4 * t + h:21 + 4 * t + h])
                for b in range(2):
                    p_ = tile("goT", l, b)
                    for i in range(2):
                        k = 2 * b + i
                        name = ("goT_out", l, b) if i else ("act_chain", l, "goT", b)
                        run(hT[:, 4 + k, :], p_[:, i * S:(i + 1) * S], ACT.Copy, *name, scale=col(l, "gla_head_gain_2", 1, k))

            def load_rows(l, stage):
                if (l, stage) != (0, "mix"):
                    act.wait_ge(*until("x_new", *((l, "mix") if stage == "ffn" else (l - 1, "ffn"))))
                if l < 2:
                    load(rows[:, 0, :], A["g_post_" + stage][l].partition_broadcast(P), f"rows_{stage}{l}", 0)
                else:
                    for i, g in enumerate("gb"):
                        load(rows[:, i, :], A[f"ln_{stage}_{g}_2"][l - 2].partition_broadcast(P), f"rows_{stage}{l}", i)

            def load_gate_bias(l):
                b = A["b_ada"][l] if l < 2 else A["mod_b_2"][l - 2]
                if l:
                    act.wait_ge(*until("x_new", l - 1, "mix"))
                load(mod_gate[:, 0, :], b[2 * D:3 * D].partition_broadcast(P), f"gate_bias_mix{l}")
                load(mod_gate[:, 1 + l % 2, :], b[5 * D:6 * D].partition_broadcast(P), f"gate_bias_ffn{l}")

            def mixture():
                def picked(e, r):
                    for b in range(2):
                        act.wait_ge(*(until("moe_tile", "pick", b, e) if r is None else within(r, 0, "moe_tile", "pick", b, e)))
                        for i in range(4):
                            k = 4 * b + i
                            run(xg[:, k, :], psum[2 + b][:, i * CAP:(i + 1) * CAP], ACT.Identity,
                                *(("moe_act", "xg", e) if k == KD - 1 else ("moe_act", "xg", k, e)),
                                scale=scale_col[:, 1, k:k + 1], bias=mod_col[:, 1, 24 + k:25 + k])

                def body(e, r):
                    now = (lambda *ev: until(*ev, e)) if r is None else (lambda *ev: within(r, 0, *ev, e))
                    for g in range(GROUPS):
                        act.wait_ge(*now("moe_tile", "up", g))
                        if g >= 2:
                            act.wait_ge(*now("moe_vec", "h", g - 2))
                        elif r is not None:
                            act.wait_ge(*within(r, 1, "moe_vec", "h", GROUPS - 2 + g, e))
                        run(moe_s[:, g % 2].rearrange("p i n -> p (i n)"), psum[g % 2][:, 0:2 * CAP], ACT.Silu, "moe_act", "silu", g, e)
                        key = ("down", 3, e, g)
                        act.wait_ge(*loaded(key, r))
                        if g >= 2:
                            act.wait_ge(*now("moe_used", "down", g - 2))
                        elif r is not None:
                            act.wait_ge(*within(r, 1, "moe_used", "down", GROUPS - 2 + g, e))
                        run(split(moe_down_hi[:, g % 2]), chunk(key), ACT.Copy, "moe_act", "down_hi", g, e)
                        if g == 1:
                            act.wait_ge(*now("moe_tile", "spread"))
                            run(spread, psum[2][:, 0:S], ACT.Copy, "moe_act", "spread", e)
                    picked(e, r)
                    act.wait_ge(*now("moe_used", "down", GROUPS - 1))
                    for c in range(2):
                        run(moe_y[:, c * 512:(c + 1) * 512], psum[4 + c], ACT.Copy, *(("moe_act", "y", e) if c else ("moe_act", "y0", e)))

                picked("start", None)
                body("first", None)
                act.wait_ge(*until("turns"))
                n = act.value_load(turns[0:1, 0:1], min_val=NE - 1, max_val=TURNS - 1)
                done.begin()
                with act.Fori(0, n) as r:
                    body("loop", r)
                done.end("moe_act")

            def leading(key):
                chunks = ffn_chunks(key[1])
                i = chunks.index(key)
                act.wait_ge(*loaded(key))
                if i >= len(w_hi):
                    act.wait_ge(*until(*chunk_used(chunks[i - len(w_hi)])))
                run(split(hi_part(key)), chunk(key), ACT.Copy, "w_hi", *key)

            def ffn(l):
                act.wait_ge(*until("hTd", l, "ffn", 3))
                act.wait_ge(*done.prev())
                for i in range(2):
                    run(split(hT_hi[:, 4 * i:4 * i + 4, :]), hT[:, 4 * i:4 * i + 4, :], ACT.Copy, "hT_hi", l, i)
                groups = ffn_groups(l)
                for g in range(groups):
                    if g + 1 < groups:
                        for m in (0, 1):
                            leading(("up", l, 0, g + 1, m))
                    fs = (2 * g, 2 * g + 1)
                    if l < 2:
                        for f in fs:
                            if g:
                                act.wait_ge(*until("up_act", l, 0, f - 2))
                            p_ = tile("up", l, 0, f)
                            run(ffn_tmp[:, f % 2, :], p_[:, 0:S], ACT.Identity, "tap", l, f,
                                scale=col(l, "w_conv", 1, 44 + f), bias=col(l, "b_conv", 1, f))
                    for f in fs:
                        if g:
                            act.wait_ge(*until("up_out", l, 0, f - 2))
                        if l < 2:
                            act.wait_ge(*until("conv", l, f))
                            run(ffn_tmp[:, 2 + f % 2, :], ffn_tmp[:, f % 2, :], ACT.Gelu_apprx_tanh, "up_act", l, 0, f)
                        else:
                            p_ = tile("up", l, 0, f)
                            run(ffn_tmp[:, 2 + f % 2, :], p_[:, 0:S], ACT.Silu, "up_act", l, 0, f)
                    leading(("down", l, 0, g))

            act.dma_start(ident, A["const_ident"]).then_inc(*done.dma("ident_loaded"))
            act.wait_ge(*until("prow_zero"))
            act.dma_start(crow[0:KD, :], A["c"][0].rearrange("(k p) -> k p", p=P)).then_inc(*done.dma("c_rows", 0))
            act.dma_start(crow[32:32 + KD, :], A["c_2"][0].rearrange("(k p) -> k p", p=P)).then_inc(*done.dma("c_rows", 1))
            act.wait_ge(*until("ident_loaded"))
            act.wait_ge(*until("c_rows", 1))
            run(stat[:, 60:61], ident[:, 0:1], ACT.Copy, "c_here")
            p_ = tile("cT")
            run(c_act.rearrange("p b k -> p (b k)")[:, 0:KD], p_[:, 0:KD], ACT.Silu, "act_chain", "silu_c")
            run(c_act.rearrange("p b k -> p (b k)")[:, KD:2 * KD], p_[:, 32:32 + KD], ACT.Silu, "c_raw")
            for name, t_ in (("parity", parity), ("causal", causal.rearrange("p t s -> p (t s)")),
                             ("rope_cos", cos.rearrange("p t f -> p (t f)")), ("rope_sin", sin.rearrange("p t f -> p (t f)")),
                             ("levels", xn[:, 0, :]), ("before", before.rearrange("p a b -> p (a b)"))):
                act.dma_start(t_, A["const_" + name]).then_inc(*done.dma("const_dma", name))
            act.dma_start(x, A["x"][0].rearrange("(t p) d -> p t d", p=P)).then_inc(*done.dma("x_loaded"))
            n_rows = 0
            for l in range(LAYERS):
                for name, r in (PROW if l < 2 else PROW2).items():
                    a = A[name][l % 2]
                    if name == "s5_log_dt_2":
                        load(dt_row[r:r + 16, l - 2, :], a.rearrange("(j g) -> j g", g=2), f"dt_loaded{l}")
                        continue
                    elif name == "w_conv":
                        src = a.rearrange("w (c p) -> (w c) p", p=P)
                    elif len(a.shape) == 2:
                        src = a.rearrange("(j g) p -> j (g p)", g=2)
                    else:
                        src = a.rearrange("(r p) -> r p", p=P)
                    n = src.shape[0]
                    at = 0
                    while at < n:
                        row = r + at
                        b = 2 * l + row // P if l < 2 else 4 + l - 2
                        take = min(n - at, P - row % P)
                        dst = prow[row % P:row % P + take, b, :]
                        act.dma_start(dst, src[at:at + take]).then_inc(*done.dma("param_dma", l, name, at))
                        n_rows += 1
                        last_param = ("param_dma", l, name, at)
                        at += take
            load_gate_bias(0)
            act.wait_ge(*until("const_dma", "before"))
            run(stat[:, 62:63], ident[:, 0:1], ACT.Copy, "const", "ident")
            act.wait_ge(*until(*last_param))
            run(stat[:, 61:62], ident[:, 0:1], ACT.Copy, "param_rows")
            for b in range(2):
                p_ = tile("param", b)
                n = 512 if b == 0 else 256
                run(pcol[:, 4 * b:4 * b + n // P, :].rearrange("p n c -> p (n c)"), p_[:, 0:n], ACT.Copy, "pcol", b)
            for l in range(LAYERS):
                load_rows(l, "mix")
                if l < 2:
                    mixer_one(l)
                    post_squares(l, "mix")
                else:
                    mixer_two(l)
                if l < 3:
                    for m in (0, 1):
                        leading(("up", l, 0, 0, m))
                load_rows(l, "ffn")
                if l < 3:
                    load_gate_bias(l + 1)
                if l < 2:
                    squares(l, "ffn")
                if 1 <= l < 3:
                    act.wait_ge(*until("post", l, "mix", 3))
                    n = l + 1
                    for r, name in enumerate(("re", "im")):
                        b5 = A[f"s5_b_{name}_2"][n - 2].rearrange("g p h -> (g p) h").rearrange("(j q) h -> q j h", q=P)
                        c5 = A[f"s5_c_{name}_2"][n - 2].rearrange("g h p -> (g h) p").rearrange("(c q) p -> q c p", q=P)
                        for i in range(2):
                            load(Bnat[:, r, :, 16 * i:16 * i + 16], b5, f"s5_load{n}", r, i, 0)
                            load(Cnat[:, r, :, HD * i:HD * i + HD], c5, f"s5_load{n}", r, i, 1)
                    load(w_alpha[0:16, :], A["gla_w_alpha_up_2"][n - 2], "w_alpha", n)
                if l == 0:
                    load(router, A["moe_w_router_2"][0].rearrange("(k p) e -> p k e", p=P), "router_loaded")
                    load(router_b[0:1, :], A["moe_b_router_2"][0:1, :], "router_b_loaded")
                norm_out(l, "ffn")
                if l == 3:
                    load(earlier, A["const_earlier"], "const_moe", 0)
                    load(iota, A["const_iota"], "const_moe", 1)
                    act.wait_ge(*until("moe_shift"))
                    run(moe[:, 7], moe[:, 6], ACT.Exp, "moe_exp")
                    mixture()
                    continue
                ffn(l)
                if l < 2:
                    post_squares(l, "ffn")

        @block.vector
        def _(dve):
            done = sig_dve
            v = nc.vector

            def tile(*key):
                dve.wait_ge(*until("pe_tile", *key))
                return psum[bank_of[key]]

            def after():
                dve.wait_ge(*done.prev())

            chain = [0]

            def link():
                chain[0] += 1
                return done("dve_chain", chain[0])

            def mod_sum(l, q):
                key = ("ada", l, q)
                dve.wait_ge(*loaded(key))
                if q >= 4:
                    dve.wait_ge(*until("pe_tile", "mod", l, q - 4))
                w, acc, ca = chunk(key), mod_acc[:, q % 4, :], c_act[:, l // 2, :]
                v.tensor_scalar(acc, w[:, 0, :], ca[:, 0:1], None, ALU.mult).then_inc(*link())
                for k in range(1, KD):
                    after()
                    v.scalar_tensor_tensor(acc, w[:, k, :], ca[:, k:k + 1], acc, ALU.mult, ALU.add)\
                        .then_inc(*(done("mod_sum", l, q) if k == KD - 1 else link()))

            def mod_out(l, q):
                p_ = tile("mod", l, q)
                m, c = q // 4, q % 4
                if m in (2, 5):
                    dve.wait_ge(*until(f"gate_bias_{'mix' if m == 2 else 'ffn'}{l}"))
                    dst = mod_gate[:, 0 if m == 2 else 1 + l % 2, c * CW:(c + 1) * CW]
                    v.tensor_tensor(dst, p_[:, 0:CW], dst, ALU.add).then_inc(*done("mod_out", l, q))
                else:
                    at = 8 * m + 2 * c
                    v.tensor_tensor(mod_col[:, l % 2, at:at + 2], p_[:, 0:2], col(l, "b_ada" if l < 2 else "mod_b_2", 2, at),
                                    ALU.add).then_inc(*done("mod_out", l, q))

            def rstd(dst, src, scale, eps, *key):
                v.tensor_scalar(dst, src, scale, eps, ALU.mult, ALU.add).then_inc(*done("variance", *key))
                dve.wait_ge(*until("rstd", *key))

            def scales(l, stage):
                b0 = 24 * (stage == "ffn")
                s = mod_col[:, l % 2, b0 + 8:b0 + 16]
                dst = scale_col[:, int(stage == "ffn"), :]
                after()
                if l < 2:
                    v.scalar_tensor_tensor(dst, s, 1.0, col(l, "g_pre_" + stage, 8), ALU.add, ALU.mult).then_inc(*done("scales", l, stage))
                else:
                    v.tensor_scalar(dst, s, 1.0, None, ALU.add).then_inc(*done("scales", l, stage))

            def rest(key):
                dve.wait_ge(*until("w_hi", *key))
                v.tensor_tensor(split(chunk(key)), chunk(key), whole(hi_part(key)), ALU.subtract).then_inc(*done("w_lo", *key))

            def norm(l, stage):
                first = (l < 3 and stage == "ffn")
                if first:
                    rest(("up", l, 0, 0, 0))
                if l < 2:
                    st = 2 * (stage == "ffn")
                    dve.wait_ge(*until("ssq", l, stage, 1))
                    rstd(stat[:, 32:34], stat[:, st:st + 2], 1.0 / D, 1e-6, l, "norm", stage)
                    for t in range(NT):
                        v.tensor_scalar(xn[:, t, :], x[:, t, :], stat[:, 32 + t:33 + t], None, ALU.mult)\
                            .then_inc(*(done("xn", l, stage) if t else link()))
                if first:
                    rest(("up", l, 0, 0, 1))
                after()
                b0 = 24 * (stage == "ffn")
                for b in (1, 3):
                    p_ = tile("norm", l, stage, b)
                    for i in range(2):
                        k = 2 * b + i
                        v.tensor_scalar(hT[:, k, :], p_[:, i * S:(i + 1) * S], scale_col[:, int(stage == "ffn"), k:k + 1],
                                        mod_col[:, l % 2, b0 + k:b0 + k + 1], ALU.mult, ALU.add)\
                            .then_inc(*(done("hTd", l, stage, b) if i else link()))

            def rope(l, c0, heads, *event):
                a = proj[:, :, c0:c0 + heads * HD].rearrange("p t (h d) -> p t h d", d=HD)
                x1, x2 = a[:, :, :, 0:8], a[:, :, :, 8:16]
                for t in range(NT):
                    y1, y2 = x1[:, t], x2[:, t]
                    c = cos[:, t].unsqueeze(1).broadcast_to([P, heads, 8])
                    s = sin[:, t].unsqueeze(1).broadcast_to([P, heads, 8])
                    ta, tb, tc, td = (rope_t[:, i, t, 0:heads, :] for i in range(4))
                    v.tensor_tensor(ta, y1, c, ALU.mult).then_inc(*link())
                    v.tensor_tensor(tb, y2, s, ALU.mult).then_inc(*link())
                    v.tensor_tensor(tc, y2, c, ALU.mult).then_inc(*link())
                    v.tensor_tensor(td, y1, s, ALU.mult).then_inc(*link())
                    after()
                    v.tensor_tensor(y1, ta, tb, ALU.subtract).then_inc(*link())
                    v.tensor_tensor(y2, tc, td, ALU.add).then_inc(*(done(*event) if t else link()))

            def indexer_sum(l):
                order = 0
                for t in range(NT):
                    kn = (t + 1) * P
                    acc = idx_acc[:, t, 0:kn]
                    first = True
                    for n in range(4 if t else 2):
                        dve.wait_ge(*until("idx_relu", l, t, n))
                        heads = unit_heads(t, n)
                        for i, h in enumerate(heads):
                            r = idx_r[:, order % 2, i * kn:(i + 1) * kn]
                            last = i == len(heads) - 1
                            ev = done("idx_sum", l, order) if last else link()
                            if first:
                                v.tensor_scalar(acc, r, w_idx[:, t, h:h + 1], None, ALU.mult).then_inc(*ev)
                            else:
                                v.scalar_tensor_tensor(acc, r, w_idx[:, t, h:h + 1], acc, ALU.mult, ALU.add).then_inc(*ev)
                            after()
                            first = False
                        order += 1
                    v.tensor_tensor(idx_work[:, t, 0:kn], acc, causal[:, t, 0:kn], ALU.add).then_inc(*link())

            def top_keys(l):
                for r in range(TOPK // 8):
                    for t in range(NT):
                        kn = (t + 1) * P
                        after()
                        v.max(top8[:, t, :], idx_work[:, t, 0:kn]).then_inc(*link())
                        after()
                        v.match_replace(idx_work[:, t, 0:kn], top8[:, t, :], idx_work[:, t, 0:kn], LOWEST).then_inc(*link())
                for t in range(NT):
                    kn = (t + 1) * P
                    after()
                    v.tensor_scalar(dsa_mask[:, t, 0:kn], idx_work[:, t, 0:kn], -2e38, NEG, ALU.is_gt, ALU.mult).then_inc(*link())
                    after()
                    v.tensor_tensor(dsa_mask[:, t, 0:kn], dsa_mask[:, t, 0:kn], causal[:, t, 0:kn], ALU.min).then_inc(*link())

            def attention(l):
                n_units = len(UNITS1)
                for u in range(n_units + 2):
                    if u < n_units:
                        g, t, n = UNITS1[u]
                        kn, nh = (t + 1) * P, 2 if t else 4
                        p_ = tile("sc", l, u)
                        if u >= 2:
                            dve.wait_ge(*until("att_exp", l, u - 2))
                        s = att_s[:, u % 2, :].rearrange("p (h k) -> p h k", h=nh)
                        mask = (dsa_mask if g else causal)[:, t, 0:kn].unsqueeze(1).broadcast_to([P, nh, kn])
                        v.tensor_tensor(s, p_.rearrange("p (h k) -> p h k", h=nh), mask, ALU.add).then_inc(*done("att_mask", l, u))
                        after()
                        v.tensor_reduce(att_nm[:, u, 0:nh], s, AX.X, ALU.max, negate=True).then_inc(*done("att_max", l, u))
                    if 1 <= u <= n_units:
                        p_ = tile("pT", l, u - 1)
                        if u >= 3:
                            dve.wait_ge(*until("pe_tile", "pv", l, u - 3))
                        v.tensor_copy(att_pT[:, (u - 1) % 2, :], p_).then_inc(*done("att_pT", l, u - 1))
                    if u >= 2:
                        g, t, n = UNITS1[u - 2]
                        if n == (3 if t else 1):
                            dve.wait_ge(*until("pe_tile", "pv", l, u - 2))
                            v.reciprocal(att_ri[:, g, t, :], att_rs[:, g, t, :]).then_inc(*link())
                            after()
                            o = psum[bank_of["o", l, g, t]].rearrange("p (h d) -> p h d", d=HD)
                            v.tensor_tensor(xn[:, t, g * 512:(g + 1) * 512].rearrange("p (h d) -> p h d", d=HD), o,
                                            att_ri[:, g, t, :].unsqueeze(2).broadcast_to([P, NH, HD]), ALU.mult)\
                                .then_inc(*done("att_o", l, g, t))
                dve.wait_ge(*until("o_ssq", l, 1, 1))
                rstd(stat[:, 36:40], stat[:, 16:20], 1.0 / 512, 1e-6, l, "o")
                for g in range(2):
                    for t in range(NT):
                        o = xn[:, t, g * 512:(g + 1) * 512]
                        v.tensor_scalar(o, o, stat[:, 36 + 2 * g + t:37 + 2 * g + t], None, ALU.mult).then_inc(*done("att_on", l, g, t))

            def post(l, stage):
                gate = mod_gate[:, 0 if stage == "mix" else 1 + l % 2, :]
                dve.wait_ge(*until(f"rows_{stage}{l}", 0 if l < 2 else 1))
                y_done = ("pe_used", "out", l, 3) if stage == "mix" else ("pe_used", "down", l, 0, ffn_groups(l) - 1)
                if l < 2:
                    after()
                    v.tensor_tensor(gate, gate, rows[:, 0, :], ALU.mult).then_inc(*link())
                    dve.wait_ge(*until("y_ssq", l, stage, 3))
                    v.tensor_reduce(stat[:, 40:42], stat[:, 8:12].rearrange("p (t c) -> p t c", c=2), AX.X, ALU.add).then_inc(*link())
                    after()
                    rstd(stat[:, 42:44], stat[:, 40:42], 1.0 / D, 1e-6, l, "post", stage)
                    for t in range(NT):
                        for c in range(2):
                            i = 2 * t + c
                            sl = slice(c * 512, (c + 1) * 512)
                            y = psum[bank_of["y", l, stage, i]]
                            v.scalar_tensor_tensor(xn[:, t, sl], y, stat[:, 42 + t:43 + t], gate[:, sl], ALU.mult, ALU.mult)\
                                .then_inc(*done("post", l, stage, i))
                        after()
                        v.tensor_tensor(x[:, t, :], x[:, t, :], xn[:, t, :], ALU.add)\
                            .then_inc(*done(*(("x_new", l, stage) if t else ("x_new_t", l, stage, 0))))
                    return
                experts = (l, stage) == (3, "ffn")
                dve.wait_ge(*(done.prev() if experts else until(*y_done)))
                for i in range(4):
                    t, c = i // 2, i % 2
                    sl = slice(c * 512, (c + 1) * 512)
                    y = xn[:, t, sl] if experts else psum[bank_of["y", l, stage, i]]
                    v.scalar_tensor_tensor(xn[:, t, sl], gate[:, sl], 1.0, y, ALU.add, ALU.mult).then_inc(*done("post", l, stage, i))
                for t in range(NT):
                    after()
                    v.scalar_tensor_tensor(x[:, t, :], x[:, t, :], ALPHA, xn[:, t, :], ALU.mult, ALU.add).then_inc(*link())
                    after()
                    for c in range(2):
                        v.bn_stats(stat[:, 44 + 6 * c:50 + 6 * c], x[:, t, c * 512:(c + 1) * 512]).then_inc(*link())
                    after()
                    v.bn_aggr(stat[:, 56:58], stat[:, 44:56]).then_inc(*link())
                    after()
                    rstd(stat[:, 58:59], stat[:, 57:58], 1.0, 1e-5, l, "post", stage, t)
                    v.tensor_scalar(xn[:, t, :], x[:, t, :], stat[:, 56:57], stat[:, 58:59], ALU.subtract, ALU.mult)\
                        .then_inc(*(link() if t else done("normed", l, stage)))
                    after()
                    if t == 0:
                        continue
                    v.tensor_tensor(xn[:, t, :], xn[:, t, :], rows[:, 0, :], ALU.mult).then_inc(*link())
                    after()
                    dve.wait_ge(*until("x_new_pool", l, stage))
                    v.tensor_tensor(x[:, t, :], xn[:, t, :], rows[:, 1, :], ALU.add).then_inc(*done("x_new", l, stage))

            def mixture():
                sel, cb = moe[:, 8], moe[:, 9]
                v.memset(place, -1.0).then_inc(*link())
                v.memset(weight, 0.0).then_inc(*link())
                v.memset(xn, 0.0).then_inc(*link())
                p_ = tile("places")
                after()
                pl = p_[:, 0:NT * NE].rearrange("p (t e) -> p t e", t=NT)
                v.scalar_tensor_tensor(place[:, :, 0:NE], pl, 1.0, sel, ALU.add, ALU.mult).then_inc(*link())
                over, rank, hot, mine = moe[:, 4, 0, :], moe[:, 5, 0, :], moe[:, 10], moe[:, 11]
                v.tensor_scalar(over, p_[:, 2 * NE:3 * NE], CAP + 0.5, None, ALU.is_gt).then_inc(*link())
                after()
                v.tensor_scalar(place[:, :, 0:NE], place[:, :, 0:NE], -1.0, None, ALU.add).then_inc(*link())
                v.tensor_tensor_scan(rank, ones[:, 0:1].broadcast_to([P, NE]), over, 0.0, ALU.mult, ALU.add).then_inc(*link())
                v.tensor_copy(weight[:, :, 0:NE], cb).then_inc(*link())
                after()
                v.memset(stat[:, 60:61], 0.0).then_inc(*done("placed"))
                dve.wait_ge(*until("const_moe", 1))
                v.tensor_copy(turns[:, 1:NE], iota[:, 1:NE]).then_inc(*link())
                for j in range(EXTRA):
                    is_jth = hot[:, 0, :]
                    after()
                    v.scalar_tensor_tensor(is_jth, rank, float(j + 1), over, ALU.is_equal, ALU.mult).then_inc(*link())
                    after()
                    v.tensor_tensor(hot[:, 1, :], is_jth, iota[:, 0:NE], ALU.mult).then_inc(*link())
                    after()
                    v.tensor_reduce(stat[:, 48:49], hot[:, 1, :], AX.X, ALU.add).then_inc(*link())
                    after()
                    v.tensor_copy(turns[:, NE + j:NE + j + 1], stat[:, 48:49]).then_inc(*link())
                    for what in (place, weight):
                        after()
                        v.tensor_tensor(mine, what[:, :, 0:NE], is_jth.unsqueeze(1).broadcast_to([P, NT, NE]), ALU.mult).then_inc(*link())
                        after()
                        v.tensor_reduce(what[:, :, NE + j], mine, AX.X, ALU.add).then_inc(*link())
                after()
                v.tensor_scalar(place[:, :, NE:TURNS], place[:, :, NE:TURNS], float(-CAP), None, ALU.add).then_inc(*link())
                after()
                v.tensor_scalar(turns[:, 0:1], rank[:, NE - 1:NE], NE - 1.0, None, ALU.add).then_inc(*done("turns"))

                def picks(e, at):
                    for t in range(NT):
                        v.tensor_scalar(pick[:, t, :], iota, place[:, t, at], None, ALU.is_equal).then_inc(*done("moe_vec", "p", t, e))
                        v.tensor_scalar(pick_w[:, t, :], iota, place[:, t, at], weight[:, t, at], ALU.is_equal, ALU.mult)\
                            .then_inc(*(done("moe_vec", "pick", e) if t else done("moe_vec", "w", t, e)))

                def add_z(name, e, i, *wait):
                    t, c = i // 2, i % 2
                    dve.wait_ge(*wait)
                    o = xn[:, t, c * 512:(c + 1) * 512]
                    v.tensor_tensor(o, psum[6 + i % 2], o, ALU.add).then_inc(*done(name, "z", i, *e))

                def body(e, r):
                    now = (lambda *ev: until(*ev, e)) if r is None else (lambda *ev: within(r, 0, *ev, e))
                    for g in range(GROUPS):
                        dve.wait_ge(*now("moe_act", "silu", g))
                        h, hi, s_ = (a[:, g % 2].rearrange("p i n -> p (i n)") for a in (moe_h, moe_hi, moe_s))
                        own = (lambda *ev: dve.wait_ge(*until(*ev, g, e))) if r is None else (lambda *ev: dve.wait_ge(*within(r, 0, *ev, g, e)))
                        v.tensor_tensor(h, psum[g % 2][:, 2 * CAP:4 * CAP], s_, ALU.mult).then_inc(*done("moe_vec", "h_whole", g, e))
                        own("moe_vec", "h_whole")
                        v.tensor_copy(split(hi), h).then_inc(*done("moe_vec", "h_hi", g, e))
                        own("moe_vec", "h_hi")
                        v.tensor_tensor(split(h), h, whole(hi), ALU.subtract).then_inc(*done("moe_vec", "h", g, e))
                        if g == 1 and r is not None:
                            for i in range(4):
                                add_z("moe_vec", (e,), i, *now("moe_tile", "z", i))
                        dve.wait_ge(*now("moe_act", "down_hi", g))
                        w = chunk(("down", 3, e, g))
                        v.tensor_tensor(split(w), w, whole(moe_down_hi[:, g % 2]), ALU.subtract).then_inc(*done("moe_vec", "down_lo", g, e))
                        if g == 4:
                            dve.wait_ge(*now("moe_tile", "spread"))
                            picks(e, slice(1, 2) if r is None else bass.ds(r + 2, 1))

                picks("start", slice(0, 1))
                body("first", None)
                n = dve.value_load(turns[0:1, 0:1], min_val=NE - 1, max_val=TURNS - 1)
                done.begin()
                with dve.Fori(0, n) as r:
                    body("loop", r)
                done.end("moe_vec")
                for i in range(4):
                    add_z("moe_last", (), i, *until("moe_tail", "z", i, "tail"))

            def ffn(l):
                for i in range(2):
                    dve.wait_ge(*until("hT_hi", l, i))
                    h = hT[:, 4 * i:4 * i + 4, :]
                    v.tensor_tensor(split(h), h, whole(hT_hi[:, 4 * i:4 * i + 4, :]), ALU.subtract).then_inc(*done("hT_lo", l, i))
                groups = ffn_groups(l)
                for g in range(groups):
                    qs = ada_in_ffn(l, g)
                    for q in qs[0:1]:
                        mod_sum(l + 1, q)
                    if g + 1 < groups:
                        rest(("up", l, 0, g + 1, 0))
                    if g:
                        for q in ada_in_ffn(l, g - 1):
                            mod_out(l + 1, q)
                    for q in qs[1:]:
                        mod_sum(l + 1, q)
                    if g + 1 < groups:
                        rest(("up", l, 0, g + 1, 1))
                    fs = (2 * g, 2 * g + 1)
                    if l < 2:
                        for back in (1, 2):
                            for f in fs:
                                a, u = ffn_tmp[:, f % 2, :], psum[bank_of["up", l, 0, f]][:, 0:S]
                                if back == 1:
                                    dve.wait_ge(*until("tap", l, f))
                                elif f == fs[0]:
                                    after()
                                v.scalar_tensor_tensor(a[:, back:S], u[:, 0:S - back], col(l, "w_conv", 1, 22 * (2 - back) + f),
                                                       a[:, back:S], ALU.mult, ALU.add)\
                                    .then_inc(*(done("conv", l, f) if back == 2 else link()))
                    for f in fs:
                        p_ = tile("up", l, 0, f)
                        dve.wait_ge(*until("up_act", l, 0, f))
                        v.tensor_tensor(hf[:, f % 4, :], ffn_tmp[:, 2 + f % 2, :], p_[:, S:2 * S], ALU.mult).then_inc(*link())
                    after()
                    for f in fs:
                        v.tensor_copy(split(hf_hi[f % 4]), hf[:, f % 4, :]).then_inc(*link())
                    after()
                    for f in fs:
                        v.tensor_tensor(split(hf[:, f % 4, :]), hf[:, f % 4, :], whole(hf_hi[f % 4]), ALU.subtract).then_inc(*done("up_out", l, 0, f))
                for q in ada_in_ffn(l, groups - 1):
                    mod_out(l + 1, q)

            def s5_params(l):
                dt, lre, lim = s5t[:, l - 2, :], col(l, "s5_lam_re_2", 16), col(l, "s5_lam_im_2", 16)
                X, Y, TH, SH, T, U, FR, FI, M = (s5t[:, i, :] for i in (2, 3, 4, 5, 6, 7, 8, 9, 10))
                R, CO, SI, fr, fi = (s5p[:, l - 2, i, :] for i in range(5))

                def ts(o, i, a, b, f, g=None):
                    after()
                    (v.tensor_scalar(o, i, a, b, f, g) if g is not None else v.tensor_scalar(o, i, a, b, f)).then_inc(*link())

                def tt(o, a, b, f):
                    after()
                    v.tensor_tensor(o, a, b, f).then_inc(*link())

                dve.wait_ge(*until("s5_dt", l))
                if l == 3:
                    dve.wait_ge(*until("s5_sin", 2))
                v.tensor_tensor(X, lre, dt, ALU.mult).then_inc(*link())
                tt(Y, lim, dt, ALU.mult)
                ts(T, Y, 1.0 / (2 * math.pi), 12582912.0, ALU.mult, ALU.add)
                ts(T, T, 12582912.0, None, ALU.subtract)
                c1_, c2_ = 6.28125, float(np.float32(2 * math.pi - 6.28125))
                c3_ = float(2 * math.pi - 6.28125 - c2_)
                after()
                v.scalar_tensor_tensor(TH, T, -c1_, Y, ALU.mult, ALU.add).then_inc(*link())
                after()
                v.scalar_tensor_tensor(TH, T, -c2_, TH, ALU.mult, ALU.add).then_inc(*link())
                after()
                v.scalar_tensor_tensor(TH, T, -c3_, TH, ALU.mult, ALU.add).then_inc(*link())
                pi = 3.1415925
                after()
                v.tensor_scalar(TH, TH, pi, -pi, ALU.min, ALU.max).then_inc(*done("s5_angle", l))
                ts(U, X, -0.5, 0.5, ALU.max, ALU.min)
                ts(T, U, 1.0 / 9, 1.0, ALU.mult, ALU.add)
                for n in range(8, 1, -1):
                    tt(T, T, U, ALU.mult)
                    ts(T, T, 1.0 / n, 1.0, ALU.mult, ALU.add)
                tt(T, T, U, ALU.mult)
                dve.wait_ge(*until("s5_sin", l))
                tt(M, X, U, ALU.is_equal)
                ts(U, R, -1.0, None, ALU.add)
                tt(T, T, U, ALU.subtract)
                tt(T, T, M, ALU.mult)
                tt(T, T, U, ALU.add)
                tt(SH, SH, SH, ALU.mult)
                ts(SH, SH, -2.0, None, ALU.mult)
                ts(CO, SH, 1.0, None, ALU.add)
                tt(FR, T, CO, ALU.mult)
                tt(FR, FR, SH, ALU.add)
                tt(FI, R, SI, ALU.mult)
                tt(T, lre, lre, ALU.mult)
                tt(U, lim, lim, ALU.mult)
                tt(T, T, U, ALU.add)
                after()
                v.reciprocal(M, T).then_inc(*link())
                tt(fr, FR, lre, ALU.mult)
                tt(T, FI, lim, ALU.mult)
                tt(fr, fr, T, ALU.add)
                tt(fr, fr, M, ALU.mult)
                tt(fi, FI, lre, ALU.mult)
                tt(T, FR, lim, ALU.mult)
                tt(fi, fi, T, ALU.subtract)
                after()
                v.tensor_tensor(fi, fi, M, ALU.mult).then_inc(*(done("s5_params") if l == 3 else link()))

            def s5(l):
                dve.wait_ge(*until(f"s5_load{l}", 1, 1, 1))
                mask = parity.unsqueeze(1).broadcast_to([P, 4, P])
                for r in range(2):
                    b = Bnat[:, r].rearrange("p (c j) n -> p c (j n)", c=4)
                    v.tensor_tensor(b, b, mask, ALU.mult).then_inc(*(done("b_masked", l) if r else link()))
                for r in range(2):
                    p_ = tile("CT", l, r).rearrange("p (c n) -> p c n", c=4)
                    v.tensor_tensor(Cmask[:, r], p_, mask, ALU.mult).then_inc(*done("c_masked", l, r))
                fr, fi = (s5p[:, l - 2, i, :].unsqueeze(2).broadcast_to([P, 16, 32]) for i in (3, 4))
                cr, ci, o0, o1, tmp = (a.rearrange("p c (j n) -> p (c j) n", n=32) for a in
                                       (Cmask[:, 0], Cmask[:, 1], Cst[:, 0], Cst[:, 1], Cnat[:, 0]))
                after()
                v.tensor_tensor(o0, cr, fr, ALU.mult).then_inc(*link())
                v.tensor_tensor(tmp, ci, fi, ALU.mult).then_inc(*link())
                after()
                v.tensor_tensor(o0, o0, tmp, ALU.subtract).then_inc(*link())
                after()
                v.tensor_tensor(o1, cr, fi, ALU.mult).then_inc(*link())
                v.tensor_tensor(tmp, ci, fr, ALU.mult).then_inc(*link())
                after()
                v.scalar_tensor_tensor(o1, o1, -1.0, tmp, ALU.mult, ALU.subtract).then_inc(*done("cst", l))
                p_ = tile("lg", l)
                for c in range(2):
                    v.tensor_scalar(gb[:, c, :], p_[:, c * S:(c + 1) * S], col(l, "gla_b_alpha_2", 1, c), None, ALU.add)\
                        .then_inc(*(done("gla_z", l) if c else link()))
                dve.wait_ge(*until("tables", l))
                after()
                for u in range(8):
                    qq, i = u // 4, u % 4
                    c, s = eC[:, 8 * qq + i:8 * qq + i + 5:4, :], eS[:, 8 * qq + i:8 * qq + i + 5:4, :]
                    re = tile("bu", l, u, 0).rearrange("p (j s) -> p j s", j=2)
                    im = tile("bu", l, u, 1).rearrange("p (j s) -> p j s", j=2)
                    v.tensor_tensor(w5[:, 0], c, re, ALU.mult).then_inc(*link())
                    v.tensor_tensor(t5[:, 0], s, im, ALU.mult).then_inc(*link())
                    v.tensor_tensor(w5[:, 1], c, im, ALU.mult).then_inc(*link())
                    v.tensor_tensor(t5[:, 1], s, re, ALU.mult).then_inc(*done("s5_w", l, u))
                    after()
                    v.tensor_tensor(w5[:, 0], w5[:, 0], t5[:, 0], ALU.add).then_inc(*link())
                    v.tensor_tensor(w5[:, 1], w5[:, 1], t5[:, 1], ALU.subtract).then_inc(*link())
                    after()
                    if u >= 2:
                        dve.wait_ge(*until(*s5_rotated(l, u - 2)))
                    for r in range(2):
                        for jj in range(2):
                            j = 8 * qq + i + 4 * jj
                            v.tensor_tensor_scan(g5[:, u % 2, r, jj, :], s5p[:, l - 2, 0, j:j + 1].broadcast_to([P, S]),
                                                 w5[:, r, jj, :], 0.0, ALU.mult, ALU.add)\
                                .then_inc(*(done("s5_g", l, u) if r and jj else link()))
                    after()
                    if u in DVE_UNITS:
                        gg, h = g5[:, u % 2], h5[:, u % 2]
                        dve.wait_ge(*until("pe_tile", "s5o", l, u - 2))
                        v.tensor_tensor(h[:, 0], c, gg[:, 0], ALU.mult).then_inc(*link())
                        v.tensor_tensor(t5[:, 0], s, gg[:, 1], ALU.mult).then_inc(*link())
                        v.tensor_tensor(h[:, 1], s, gg[:, 0], ALU.mult).then_inc(*link())
                        v.tensor_tensor(t5[:, 1], c, gg[:, 1], ALU.mult).then_inc(*link())
                        after()
                        v.tensor_tensor(h[:, 0], h[:, 0], t5[:, 0], ALU.subtract).then_inc(*link())
                        v.tensor_tensor(h[:, 1], h[:, 1], t5[:, 1], ALU.add).then_inc(*done(*s5_rotated(l, u)))
                    after()
                for qq in range(2):
                    dve.wait_ge(*until("pe_tile", "s5o", l, 4 * qq + 3))
                    y = psum[bank_of["s5y", l, qq]]
                    for i in range(2):
                        c = 2 * qq + i
                        v.scalar_tensor_tensor(uT[:, c, :], uT[:, c, :], col(l, "s5_d_2", 1, c), y[:, i * S:(i + 1) * S],
                                               ALU.mult, ALU.add).then_inc(*(done("s5_y", l, qq) if i else link()))

            def gla(l):
                v.scalar_tensor_tensor(gz[:, 1], gb, -1.0, gb, ALU.mult, ALU.min).then_inc(*done("gla_abs", l))
                dve.wait_ge(*until("gla_ln", l))
                v.scalar_tensor_tensor(gz[:, 0], gb, 0.0, gz[:, 1], ALU.min, ALU.subtract).then_inc(*link())
                after()
                v.tensor_scalar(gz[:, 0], gz[:, 0], 1.0 / 16, None, ALU.mult).then_inc(*link())
                after()
                for c in range(2):
                    v.tensor_tensor_scan(gb[:, c, :], ones[:, 0:1].broadcast_to([P, S]), gz[:, 0, c, :], 0.0, ALU.mult, ALU.add)\
                        .then_inc(*link())
                after()
                dve.wait_ge(*until("gla_zero", l, 2))
                dve.wait_ge(*until("in_out", l, 3))
                b2, q2, k2 = (a.rearrange("p c s -> p (c s)") for a in (gb, gqT, gkT))
                halves = [P] + LEVELS[:-1]
                view = lambda a, h: a.rearrange("p (n w) -> p n w", w=2 * h)

                def factors(m):
                    h = halves[m]
                    d, b = view(gD[:, m % 2, :], h), view(b2, h)
                    mid = b[:, :, h - 1:h].broadcast_to([P, 512 // (2 * h), h])
                    after()
                    v.tensor_tensor(d[:, :, 0:h], mid, b[:, :, 0:h], ALU.subtract).then_inc(*link())
                    v.tensor_tensor(d[:, :, h:2 * h], b[:, :, h:2 * h], mid, ALU.subtract).then_inc(*done("gla_d", l, h))

                def products(m):
                    h = halves[m]
                    dve.wait_ge(*until("gla_e", l, h))
                    if m >= 2:
                        dve.wait_ge(*until("pe_tile", "off", l, 1) if m == 2 else until("pe_tile", "lv", l, m - 3, 1))
                    d = view(gD[:, m % 2, :], h)
                    v.tensor_tensor(view(gQ[:, m % 2, :], h)[:, :, h:2 * h], view(q2, h)[:, :, h:2 * h], d[:, :, h:2 * h], ALU.mult).then_inc(*link())
                    v.tensor_tensor(view(gK[:, m % 2, :], h)[:, :, 0:h], view(k2, h)[:, :, 0:h], d[:, :, 0:h], ALU.mult).then_inc(*done("gla_k", l, h))

                def collect(n):
                    for par in range(2):
                        p_ = tile("lv", l, n, par)
                        after()
                        v.copy_predicated(scT[:, par].rearrange("p j c i -> p (j c) i"),
                                          levels[:, n, :].unsqueeze(1).broadcast_to([P, 4, P]),
                                          p_.rearrange("p (a i) -> p a i", a=4)).then_inc(*done("lv_out", l, n, par))

                factors(0)
                for m in range(len(halves)):
                    if m + 1 < len(halves):
                        factors(m + 1)
                    products(m)
                    if m >= 2:
                        collect(m - 2)
                for n in range(len(halves) - 2, len(LEVELS)):
                    collect(n)
                for t in range(NT):
                    dve.wait_ge(*until("go_ssq", l, t, 3))
                    rstd(stat[:, 36:40], stat[:, 20 + 4 * t:24 + 4 * t], 1.0 / P, 1e-6, l, "gla", t)
                    if t == 0:
                        dve.wait_ge(*until("in_out", l, 7))
                    p_ = psum[bank_of["go", l, t]]
                    for h in range(4):
                        v.scalar_tensor_tensor(o_gla[:, t, h * P:(h + 1) * P], p_[:, h * P:(h + 1) * P], stat[:, 36 + h:37 + h],
                                               vg[:, t, 512 + h * P:512 + (h + 1) * P], ALU.mult, ALU.mult)\
                            .then_inc(*(done("gla_o", l, t) if h == 3 else link()))
                    after()

            def route():
                lg, m1, sh, ex, cb = moe[:, 0], moe[:, 1], moe[:, 6], moe[:, 7], moe[:, 9]
                p_ = tile("router")
                v.tensor_copy(lg, p_[:, 0:NT * NE].rearrange("p (t e) -> p t e", t=NT)).then_inc(*done("logits"))
                after()
                v.tensor_reduce(m1[:, :, 0], lg, AX.X, ALU.max).then_inc(*link())
                after()
                v.tensor_tensor(sh, lg, m1[:, :, 0:1].broadcast_to([P, NT, NE]), ALU.subtract).then_inc(*done("moe_shift"))
                for t in range(NT):
                    row = lg[:, t, :].unsqueeze(1).broadcast_to([P, NE, NE])
                    own = lg[:, t, :].unsqueeze(2).broadcast_to([P, NE, NE])
                    more, same = moe_pair[:, 0], moe_pair[:, 1]
                    v.tensor_tensor(more, row, own, ALU.is_gt).then_inc(*link())
                    v.tensor_tensor(same, row, own, ALU.is_equal).then_inc(*link())
                    after()
                    v.tensor_tensor(same, same, before, ALU.mult).then_inc(*link())
                    after()
                    v.tensor_tensor(more, more, same, ALU.add).then_inc(*link())
                    after()
                    v.tensor_reduce(moe[:, 8, t, :], more, AX.X, ALU.add).then_inc(*link())
                    after()
                after()
                v.tensor_scalar(moe[:, 8], moe[:, 8], 1.5, None, ALU.is_lt).then_inc(*done("chosen"))
                dve.wait_ge(*until("moe_exp"))
                after()
                v.tensor_tensor(cb, ex, moe[:, 8], ALU.mult).then_inc(*link())
                after()
                v.tensor_reduce(moe[:, 2, :, 0], cb, AX.X, ALU.add).then_inc(*link())
                after()
                v.reciprocal(moe[:, 3, :, 0], moe[:, 2, :, 0]).then_inc(*link())
                after()
                v.tensor_tensor(cb, cb, moe[:, 3, :, 0:1].broadcast_to([P, NT, NE]), ALU.mult).then_inc(*done("comb"))

            v.memset(prow, 0.0).then_inc(*link())
            v.memset(crow, 0.0).then_inc(*done("prow_zero"))
            dve.wait_ge(*until("c_raw"))
            for q in range(4):
                mod_sum(0, q)
            for l in (2, 3):
                dve.wait_ge(*until(f"dt_loaded{l}"))
                r = PROW2["s5_log_dt_2"]
                v.tensor_copy(prow[r:r + 16, 2 + l, :].rearrange("j (g p) -> j g p", g=2),
                              dt_row[r:r + 16, l - 2, :].unsqueeze(2).broadcast_to([16, 2, HD])).then_inc(*done("dt_rows", l))
            dve.wait_ge(*until("const", "ident"))
            v.tensor_copy(levels.rearrange("p n i -> p (n i)"), xn[:, 0, :]).then_inc(*link())
            for q in range(4, 8):
                mod_sum(0, q)
            dve.wait_ge(*until("pcol", 1))
            for q in range(8):
                mod_out(0, q)
            for l in range(LAYERS):
                scales(l, "mix")
                norm(l, "mix")
                if l == 0:
                    s5_params(2)
                    s5_params(3)
                if l < 2:
                    pending = []
                    for i, n in enumerate(PROJ_ORDER):
                        if l == 0:
                            for q in ([8 + i] if i < 14 else [22, 23]):
                                mod_sum(0, q)
                                if pending:
                                    mod_out(0, pending.pop(0))
                                pending.append(q)
                        if i == 2:
                            dve.wait_ge(*until("in_out", l, 14))
                            v.tensor_scalar(w_idx, proj[:, :, WI:WI + 8], float(np.float32(8 ** -0.5)), None, ALU.mult).then_inc(*link())
                            rope(l, QI, 9, "rope", l, 2)
                            after()
                            for h in range(2):
                                v.tensor_copy(kidup[:, :, HD * h:HD * h + HD], proj[:, :, KI:KI + HD])\
                                    .then_inc(*(done("kidup", l) if h else link()))
                        if i == 6:
                            dve.wait_ge(*until("in_out", l, 3))
                            rope(l, 0, 16, "rope", l, 0)
                            indexer_sum(l)
                        if i == 10:
                            dve.wait_ge(*until("in_out", l, 9))
                            rope(l, 1536, 16, "rope", l, 1)
                    for q in pending:
                        mod_out(0, q)
                    top_keys(l)
                    after()
                    attention(l)
                else:
                    s5(l)
                    for b in range(2):
                        dve.wait_ge(*until("s5_sig", l, b))
                        h2 = hT[:, 2 * b:2 * b + 2, :]
                        v.tensor_tensor(h2, h2, uT[:, 2 * b:2 * b + 2, :], ALU.mult)\
                            .then_inc(*(done("s5_done", l) if b else done("s5_wait", l)))
                    gla(l)
                post(l, "mix")
                scales(l, "ffn")
                norm(l, "ffn")
                if l == 3:
                    route()
                    mixture()
                else:
                    ffn(l)
                post(l, "ffn")

    return sig


_INS = ["x", "c", "w_ada", "b_ada", "g_pre_mix", "w_in", "g_moba_out", "g_dsa_out", "w_out", "g_post_mix", "g_pre_ffn",
        "w_up_act", "w_up_lin", "w_conv", "b_conv", "w_down", "g_post_ffn", "c_2", "mod_w_2", "mod_b_2", "w_in_2",
        "w_out_2", "s5_lam_re_2", "s5_lam_im_2", "s5_log_dt_2", "s5_b_re_2", "s5_b_im_2", "s5_c_re_2", "s5_c_im_2",
        "s5_d_2", "s5_w_glu_2", "s5_b_glu_2", "gla_w_alpha_up_2", "gla_b_alpha_2", "gla_head_gain_2", "ln_mix_g_2",
        "ln_mix_b_2", "ffn_w_gate_2", "ffn_w_up_2", "ffn_w_down_2", "moe_w_router_2", "moe_b_router_2", "moe_w_gate_2",
        "moe_w_up_2", "moe_w_down_2", "ln_ffn_g_2", "ln_ffn_b_2"]


class _Any(dict):

    def __missing__(self, key):
        return 1


def kernel(**inputs):
    import numpy as _np
    import concourse.bacc as _bacc
    from concourse import mybir as _mybir
    from concourse.bass_utils import run_bass_kernel_spmd as _run

    arrays = {f"in_{n}": _np.ascontiguousarray(inputs[n]) for n in _INS}
    arrays |= {f"in_const_{n}": a for n, a in constants().items()}
    names, known = [], _Any()
    for last in (False, True):
        nc = _bacc.Bacc("TRN2", target_bir_lowering=False, num_devices=1)
        A = {n[3:]: nc.dram_tensor(n, a.shape, _mybir.dt.from_np(a.dtype), kind="ExternalInput").ap() for n, a in arrays.items()}
        out = nc.dram_tensor("out_0", (1, S, D), F32, kind="ExternalOutput").ap()

        class Sems(dict):
            def __missing__(self, name):
                self[name] = nc.alloc_semaphore(name)
                return self[name]

        sig = program(nc, A, out, Sems(), known)
        known = dict(sig.at)
    r = _run(nc, [arrays], core_ids=[0])
    return r.results[0]["out_0"]
```
